# Optimizing a Trainium2 kernel written in Bass

```python
import jax, jax.numpy as jnp
from jax import lax
import numpy as np

'''Two-layer interleaved hybrid diffusion backbone over latent tokens with a context prefix.

Inputs:  x (BATCH, SEQ, D_MODEL) latent tokens, c (BATCH, D_MODEL) conditioning vector,
         ctx (BATCH, CTX_LEN, D_MODEL) context tokens, c_ctx (D_MODEL,) learned context conditioning,
         plus stacked per-layer parameters.
Output:  (BATCH, SEQ, D_MODEL) latent stream after DEPTH layers.
Layer i: token mixer (i mod 2): 0 = windowed GQA with sinks, 1 = short gated convolution;
         channel mixer: even = dense SwiGLU, odd = top-2-of-8 expert SwiGLU.
Each sub-layer: h = x*(1+scale)+shift ; x <- LayerNorm(alpha*x + gate*f(h)) (DeepNorm post-norm).
'''

D_MODEL = 1024
BATCH = 1
SEQ = 512
DEPTH = 2

GRID_W = 64
CTX_LEN = 256
N_MIXERS = 2
HEAD_DIM = 64
N_Q_HEADS = D_MODEL // HEAD_DIM
N_KV_HEADS = N_Q_HEADS // 4
GQA_GROUP = N_Q_HEADS // N_KV_HEADS
Q_DIM = N_Q_HEADS * HEAD_DIM
KV_DIM = N_KV_HEADS * HEAD_DIM
WINDOW = 128
ATTN_BLOCK = 128
ROPE_THETA = 10000.0
ROPE_AXIS_DIM = HEAD_DIM // 2
CONV_WIDTH = 3
D_FF_DENSE = 2816
N_EXPERTS = 8
TOP_K = 2
D_FF_EXPERT = 3584
MOE_BLOCK = 128
LN_EPS = 1e-5
MASK_VALUE = -1e30
DEEPNORM_ALPHA = (2 * DEPTH) ** 0.25
DEEPNORM_BETA = (8 * DEPTH) ** -0.25
N_ATTN_LAYERS = (DEPTH + N_MIXERS - 1) // N_MIXERS
N_CONV_LAYERS = DEPTH // N_MIXERS
N_DENSE_LAYERS = (DEPTH + 1) // 2
N_MOE_LAYERS = DEPTH // 2

kernel_name = 'hybrid_window_gqa_shortconv_moe_dit'

def layer_norm(x, g, b):
    xf = x.astype(jnp.float32)
    mu = xf.mean(-1, keepdims=True)
    var = jnp.square(xf - mu).mean(-1, keepdims=True)
    return ((xf - mu) * lax.rsqrt(var + LN_EPS) * g.astype(jnp.float32) + b.astype(jnp.float32)).astype(x.dtype)

def axial_rope_tables(rows_count, dtype):
    rows = jnp.repeat(jnp.arange(rows_count, dtype=jnp.float32), GRID_W)
    cols = jnp.tile(jnp.arange(GRID_W, dtype=jnp.float32), rows_count)
    inv_freq = ROPE_THETA ** (-jnp.arange(0, ROPE_AXIS_DIM, 2, dtype=jnp.float32) / ROPE_AXIS_DIM)
    ar = rows[:, None] * inv_freq
    ac = cols[:, None] * inv_freq
    ang = jnp.concatenate([ar, ar, ac, ac], axis=-1)
    return jnp.cos(ang).astype(dtype), jnp.sin(ang).astype(dtype)

def apply_rope(x, cos, sin):
    xr = x.reshape(x.shape[:-1] + (2, 2, ROPE_AXIS_DIM // 2))
    rot = jnp.stack([-xr[..., 1, :], xr[..., 0, :]], axis=-2).reshape(x.shape)
    return x * cos[:, None, :] + rot * sin[:, None, :]

def sink_softmax(logits, sink):
    m = jnp.maximum(logits.max(-1, keepdims=True), sink)
    p = jnp.exp(logits - m)
    return p / (p.sum(-1, keepdims=True) + jnp.exp(sink - m))

def windowed_latent_attention(q, k, v, k_ctx, v_ctx, sink):
    B, S = q.shape[:2]
    n_ctx = k_ctx.shape[1]
    n_blocks = S // ATTN_BLOCK
    span = ATTN_BLOCK + 2 * WINDOW
    pad = ((0, 0), (WINDOW, WINDOW), (0, 0), (0, 0))
    k_pad = jnp.pad(k, pad)
    v_pad = jnp.pad(v, pad)
    scale = HEAD_DIM ** -0.5

    def block(i):
        s0 = i * ATTN_BLOCK
        qb = lax.dynamic_slice_in_dim(q, s0, ATTN_BLOCK, axis=1)
        kb = lax.dynamic_slice_in_dim(k_pad, s0, span, axis=1)
        vb = lax.dynamic_slice_in_dim(v_pad, s0, span, axis=1)
        q_pos = s0 + jnp.arange(ATTN_BLOCK)
        k_pos = s0 - WINDOW + jnp.arange(span)
        valid = (jnp.abs(q_pos[:, None] - k_pos[None, :]) <= WINDOW) & (k_pos >= 0) & (k_pos < S)
        s_win = jnp.einsum('bqkgd,bnkd->bkgqn', qb, kb).astype(jnp.float32) * scale
        s_win = jnp.where(valid, s_win, MASK_VALUE)
        s_ctx = jnp.einsum('bqkgd,bckd->bkgqc', qb, k_ctx).astype(jnp.float32) * scale
        probs = sink_softmax(jnp.concatenate([s_ctx, s_win], axis=-1), sink)
        o = (jnp.einsum('bkgqc,bckd->bqkgd', probs[..., :n_ctx], v_ctx.astype(jnp.float32))
             + jnp.einsum('bkgqn,bnkd->bqkgd', probs[..., n_ctx:], vb.astype(jnp.float32)))
        return o.astype(q.dtype)

    out = lax.map(block, jnp.arange(n_blocks))
    return jnp.moveaxis(out, 0, 1).reshape(B, S, Q_DIM)

def context_attention(q, k, v, sink):
    B, C = q.shape[:2]
    s = jnp.einsum('bqkgd,bckd->bkgqc', q, k).astype(jnp.float32) * HEAD_DIM ** -0.5
    o = jnp.einsum('bkgqc,bckd->bqkgd', sink_softmax(s, sink), v.astype(jnp.float32))
    return o.astype(q.dtype).reshape(B, C, Q_DIM)

def attention_mixer(h, hc, w_qkv, w_o, sinks, cos, sin, update_ctx):
    B, S, _ = h.shape
    C = hc.shape[1]
    q, k, v = jnp.split(h @ w_qkv, [Q_DIM, Q_DIM + KV_DIM], axis=-1)
    q = apply_rope(q.reshape(B, S, N_Q_HEADS, HEAD_DIM), cos, sin).reshape(B, S, N_KV_HEADS, GQA_GROUP, HEAD_DIM)
    k = apply_rope(k.reshape(B, S, N_KV_HEADS, HEAD_DIM), cos, sin)
    v = v.reshape(B, S, N_KV_HEADS, HEAD_DIM)
    if update_ctx:
        q_c, k_c, v_c = jnp.split(hc @ w_qkv, [Q_DIM, Q_DIM + KV_DIM], axis=-1)
    else:
        k_c, v_c = jnp.split(hc @ w_qkv[:, Q_DIM:], [KV_DIM], axis=-1)
    k_c = k_c.reshape(B, C, N_KV_HEADS, HEAD_DIM)
    v_c = v_c.reshape(B, C, N_KV_HEADS, HEAD_DIM)
    sink = sinks.astype(jnp.float32).reshape(N_KV_HEADS, GQA_GROUP, 1, 1)
    out = windowed_latent_attention(q, k, v, k_c, v_c, sink) @ w_o
    out_c = None
    if update_ctx:
        q_c = q_c.reshape(B, C, N_KV_HEADS, GQA_GROUP, HEAD_DIM)
        out_c = context_attention(q_c, k_c, v_c, sink) @ w_o
    return out, out_c

def short_conv_mixer(h, w_in, conv_w, w_out):
    S = h.shape[1]
    b_gate, c_gate, val = jnp.split(h @ w_in, 3, axis=-1)
    u = c_gate * val
    half = CONV_WIDTH // 2
    u_pad = jnp.pad(u, ((0, 0), (half, half), (0, 0)))
    y = sum(conv_w[j] * u_pad[:, j:j + S] for j in range(CONV_WIDTH))
    return (b_gate * y) @ w_out

def swiglu(h, w1, w3, w2):
    return (jax.nn.silu(h @ w1) * (h @ w3)) @ w2

def moe_swiglu(h, w_router, w1, w3, w2):
    T, D = h.shape
    logits = (h @ w_router).astype(jnp.float32)
    top_logit, top_e = lax.top_k(logits, TOP_K)
    gates = jax.nn.softmax(top_logit, axis=-1)
    e_flat = top_e.reshape(-1).astype(jnp.int32)
    tok_flat = jnp.repeat(jnp.arange(T, dtype=jnp.int32), TOP_K)
    g_flat = gates.reshape(-1)
    order = jnp.argsort(e_flat)
    e_s, tok_s, g_s = e_flat[order], tok_flat[order], g_flat[order]
    counts = jnp.zeros((N_EXPERTS,), jnp.int32).at[e_flat].add(1)
    starts = jnp.cumsum(counts) - counts
    padded = (counts + MOE_BLOCK - 1) // MOE_BLOCK * MOE_BLOCK
    pends = jnp.cumsum(padded)
    pstarts = pends - padded
    dest = pstarts[e_s] + jnp.arange(T * TOP_K, dtype=jnp.int32) - starts[e_s]
    n_blocks = -(-(T * TOP_K) // MOE_BLOCK) + N_EXPERTS
    n_rows = n_blocks * MOE_BLOCK
    row_tok = jnp.full((n_rows,), T, jnp.int32).at[dest].set(tok_s)
    row_gate = jnp.zeros((n_rows,), jnp.float32).at[dest].set(g_s)
    block_e = jnp.minimum(jnp.searchsorted(pends, jnp.arange(n_blocks, dtype=jnp.int32) * MOE_BLOCK, side='right'), N_EXPERTS - 1)
    h_pad = jnp.concatenate([h, jnp.zeros((1, D), h.dtype)], axis=0)
    xb = h_pad[row_tok].reshape(n_blocks, MOE_BLOCK, D)

    def expert_block(args):
        xblk, e = args
        return swiglu(xblk, w1[e], w3[e], w2[e])

    yb = lax.map(expert_block, (xb, block_e)).reshape(n_rows, D)
    y = jax.ops.segment_sum(yb * row_gate[:, None], row_tok, num_segments=T + 1)
    return y[:T].astype(h.dtype)

def setup_inputs(seed: int = 0) -> dict:
    key = jax.random.key(seed)
    ks = jax.random.split(key, 22)
    D = D_MODEL

    def nrm(k, shape, scale):
        return jax.random.normal(k, shape, jnp.float32) * scale

    return {
        'x': nrm(ks[0], (BATCH, SEQ, D), 1.0),
        'c': nrm(ks[1], (BATCH, D), 1.0),
        'ctx': nrm(ks[2], (BATCH, CTX_LEN, D), 1.0),
        'c_ctx': nrm(ks[3], (D,), 1.0),
        'w_mod': nrm(ks[4], (DEPTH, D, 6 * D), 0.5 * D ** -0.5),
        'b_mod': nrm(ks[5], (DEPTH, 6 * D), 0.01),
        'ln_g': 1.0 + nrm(ks[6], (DEPTH, 2, D), 0.02),
        'ln_b': nrm(ks[7], (DEPTH, 2, D), 0.02),
        'attn_w_qkv': nrm(ks[8], (N_ATTN_LAYERS, D, Q_DIM + 2 * KV_DIM), D ** -0.5),
        'attn_w_o': nrm(ks[9], (N_ATTN_LAYERS, Q_DIM, D), Q_DIM ** -0.5 * DEEPNORM_BETA),
        'attn_sink': nrm(ks[10], (N_ATTN_LAYERS, N_Q_HEADS), 0.5),
        'conv_w_in': nrm(ks[11], (N_CONV_LAYERS, D, 3 * D), D ** -0.5),
        'conv_w': nrm(ks[12], (N_CONV_LAYERS, CONV_WIDTH, D), CONV_WIDTH ** -0.5),
        'conv_w_out': nrm(ks[13], (N_CONV_LAYERS, D, D), D ** -0.5 * DEEPNORM_BETA),
        'ffn_w1': nrm(ks[14], (N_DENSE_LAYERS, D, D_FF_DENSE), D ** -0.5),
        'ffn_w3': nrm(ks[15], (N_DENSE_LAYERS, D, D_FF_DENSE), D ** -0.5),
        'ffn_w2': nrm(ks[16], (N_DENSE_LAYERS, D_FF_DENSE, D), D_FF_DENSE ** -0.5 * DEEPNORM_BETA),
        'moe_router': nrm(ks[17], (N_MOE_LAYERS, D, N_EXPERTS), D ** -0.5),
        'moe_w1': nrm(ks[18], (N_MOE_LAYERS, N_EXPERTS, D, D_FF_EXPERT), D ** -0.5),
        'moe_w3': nrm(ks[19], (N_MOE_LAYERS, N_EXPERTS, D, D_FF_EXPERT), D ** -0.5),
        'moe_w2': nrm(ks[20], (N_MOE_LAYERS, N_EXPERTS, D_FF_EXPERT, D), D_FF_EXPERT ** -0.5 * DEEPNORM_BETA),
    }

def reference(x, c, ctx, c_ctx, w_mod, b_mod, ln_g, ln_b, attn_w_qkv, attn_w_o, attn_sink,
              conv_w_in, conv_w, conv_w_out, ffn_w1, ffn_w3, ffn_w2,
              moe_router, moe_w1, moe_w3, moe_w2):
    B, S, D = x.shape
    ROWS = S // GRID_W
    cos, sin = axial_rope_tables(ROWS, x.dtype)
    silu_c = jax.nn.silu(c)
    silu_cc = jax.nn.silu(c_ctx)
    xc = ctx
    for i in range(DEPTH):
        mi = i // N_MIXERS
        fi = i // 2
        is_attn = i % N_MIXERS == 0
        is_dense = i % 2 == 0
        update_ctx = any(j % N_MIXERS == 0 for j in range(i + 1, DEPTH))

        sh1, sc1, g1, sh2, sc2, g2 = jnp.split((silu_c @ w_mod[i] + b_mod[i])[:, None, :], 6, axis=-1)
        h = x * (1 + sc1) + sh1
        if is_attn or update_ctx:
            csh1, csc1, cg1, csh2, csc2, cg2 = jnp.split(silu_cc @ w_mod[i] + b_mod[i], 6)
            hc = xc * (1 + csc1) + csh1

        if is_attn:
            mix, mix_c = attention_mixer(h, hc, attn_w_qkv[mi], attn_w_o[mi], attn_sink[mi], cos, sin, update_ctx)
        else:
            mix = short_conv_mixer(h, conv_w_in[mi], conv_w[mi], conv_w_out[mi])
            mix_c = short_conv_mixer(hc, conv_w_in[mi], conv_w[mi], conv_w_out[mi]) if update_ctx else None
        x = layer_norm(DEEPNORM_ALPHA * x + g1 * mix, ln_g[i, 0], ln_b[i, 0])
        if update_ctx:
            xc = layer_norm(DEEPNORM_ALPHA * xc + cg1 * mix_c, ln_g[i, 0], ln_b[i, 0])

        h = x * (1 + sc2) + sh2
        if update_ctx:
            hc = xc * (1 + csc2) + csh2
        if is_dense:
            ff = swiglu(h, ffn_w1[fi], ffn_w3[fi], ffn_w2[fi])
            ff_c = swiglu(hc, ffn_w1[fi], ffn_w3[fi], ffn_w2[fi]) if update_ctx else None
        else:
            tokens = h.reshape(-1, D)
            n_c = 0
            if update_ctx:
                n_c = hc.shape[0] * hc.shape[1]
                tokens = jnp.concatenate([hc.reshape(-1, D), tokens], axis=0)
            y_all = moe_swiglu(tokens, moe_router[fi], moe_w1[fi], moe_w3[fi], moe_w2[fi])
            ff = y_all[n_c:].reshape(h.shape)
            ff_c = y_all[:n_c].reshape(hc.shape) if update_ctx else None
        x = layer_norm(DEEPNORM_ALPHA * x + g2 * ff, ln_g[i, 1], ln_b[i, 1])
        if update_ctx:
            xc = layer_norm(DEEPNORM_ALPHA * xc + cg2 * ff_c, ln_g[i, 1], ln_b[i, 1])
    return x


_drawn_inputs = setup_inputs


def setup_inputs(seed=0):
    import zlib

    import numpy as np

    out = dict(_drawn_inputs(seed))
    spreads = {}
    factors = {'ctx': 6.689, 'c_ctx': 3.238, 'b_mod': 6.411, 'attn_sink': 64.0}
    for name, (base, spread) in spreads.items():
        noise = np.random.default_rng([zlib.crc32(name.encode()), seed]).standard_normal(out[name].shape)
        drawn = base * np.exp(spread * noise) if base else spread * noise
        out[name] = __import__('jax').numpy.asarray(drawn.astype(out[name].dtype))
    for name, factor in factors.items():
        out[name] = (out[name] * factor).astype(out[name].dtype)
    return out
```

```python
from contextlib import ExitStack, contextmanager

import concourse.bass as bass
from concourse import mybir

F32 = mybir.dt.float32
F32R = mybir.dt.float32r
I32 = mybir.dt.int32
U32 = mybir.dt.uint32
ALU = mybir.AluOpType
ACT = mybir.ActivationFunctionType
AX = mybir.AxisListType

P = 128
D = 1024
KD = D // P
T = 512
CTX = 256
HD = 64
NH = 16
NKV = 4
FF = 2816
NE = 8
FE = 3584
UNIT = 2048
BLK = 128
NBLK = T // BLK
WIN = 3 * BLK
NKEY = CTX + WIN
FF_PARTS = (8, 6, 8)
GROUPS = FE // 512
CAP = 256
MAX_OVER = 2 * T // (CAP + 1)
N_ROWS = (NE + MAX_OVER) * CAP
ALPHA = 4 ** 0.25
EPS = 1e-5
SCALE = HD ** -0.5
MASKED = -1e30
WIDTHS = (128, 160, 192, 224, CAP)
DOWN6 = ([0, 1], [2, 3, 4], [5, 6, 7])
ATT_STEPS = NH + 2

SEGMENTS = [
    ("modA", 2, "mmmm"), ("kv", 1, "smmsmm"), ("q", 2, "smmsmm"), ("o", 1, "ssss"),
    ("up0", 4, "smmsmm"), ("dn0", 1, "ssss"), ("up1", 3, "smmsmm"), ("dn1", 1, "sss"),
    ("up2", 2, "ssss"), ("dn2", 1, "ssss"), ("conv", 4, "sss"), ("co", 1, "ssss"),
]
N_PRE = sum(n * len(b) for _, n, b in SEGMENTS)
RSLOT = {"smmsmm": (0, 1, 2, 3, 1, 2), "ssss": (0, 1, 2, 3), "sss": (0, 1, 2), "mmmm": (0, 1, 2, 3)}
HSLOT = {"smmsmm": (0, 1), "ssss": (0, 1, 2, 1), "sss": (0, 1, 2), "mmmm": ()}

SM = {}
_o = 0
for _n, _w in (("cc", 16), ("bmod", 192), ("lng", 32), ("lnb", 32), ("ident", 128), ("mean", 128), ("sink", 16),
               ("cw", 24), ("wr", 64)):
    SM[_n] = (_o, _o + _w)
    _o += _w
N_SM = _o
RC = {"ones": (0, 128), "upper": (128, 256), "iota": (256, 264), "base": (264, 272)}
N_RC = 272


class Turns:

    def __init__(self):
        self.at, self.levels = {}, []

    def n(self, key):
        v = self.at.get(key, 0) + 1
        self.at[key] = v
        for i, per in self.levels:
            if per.get(key):
                v = i * per[key] + v
        return v

    def skip(self, key, k):
        self.at[key] = self.at.get(key, 0) + k

    def last(self, key):
        self.skip(key, -1)
        return self.n(key)

    @contextmanager
    def loop(self, eng, count, per, start=0):
        before = dict(self.at)
        with eng.Fori(start, start + count) if isinstance(count, int) else eng.Fori(0, count) as i:
            self.levels.append((i - start if start else i, per))
            yield i
            self.levels.pop()
        for key in set(per) | set(self.at):
            did = self.at.get(key, 0) - before.get(key, 0)
            assert did == per.get(key, 0), (key, did, per.get(key, 0))
            if isinstance(count, int):
                self.at[key] = before.get(key, 0) + count * did


def positions(body):
    out, s, m = [], 0, 0
    for kind, r in zip(body, RSLOT[body]):
        if kind == "s":
            out.append((kind, r, HSLOT[body][s], s))
            s += 1
        else:
            out.append((kind, r, None, m))
            m += 1
    return out


def program(nc, small, xT_in, ctxT_in, rope, maskin, rconst, lnrow, w_pre, w_moe, out):
    with ExitStack() as ctx:
        def sem(name):
            return ctx.enter_context(nc.semaphore(name))

        base = 16512
        limit = 229344
        cur = [base]

        def put(name, shape, dt, at=None):
            size = 4
            for s in shape[1:]:
                size *= s
            off = cur[0] if at is None else at
            t = nc.alloc_sbuf_tensor_at(name, shape, dt, offset=off)
            if at is None:
                cur[0] += size
                assert cur[0] <= limit, (name, cur[0])
            else:
                assert at + size <= limit, (name, at + size)
            return t

        RAW = [put(f"raw{i}", [P, UNIT], F32) for i in range(4)]
        HI = [put(f"hi{i}", [P, UNIT], F32R) for i in range(3)]
        LO = [put(f"lo{i}", [P, UNIT], F32R) for i in range(3)]
        o_xz = cur[0]
        XZ = put("xz", [P, KD, T], F32)
        o_ah = cur[0]
        AH = put("ah", [P, KD, T], F32R)
        o_al = cur[0]
        AL = put("al", [P, KD, T], F32R)
        SMALL = put("small", [P, N_SM], F32)
        MOD = put("mod", [P, 2, 2 * 48], F32)
        COEF = put("coef", [P, 4, 4, KD], F32)
        CG = put("cg", [P, KD], F32)
        SILC = put("silc", [P, KD, 2], F32)
        IDR = put("idr", [P, P], F32R)
        NRM = put("nrm", [P, NH], F32)
        NM = put("nm", [P, NH], F32)
        LSUM = put("lsum", [P, NH], F32)
        ES = put("es", [P, NH], F32)
        RS = put("rs", [P, NH], F32)
        NSINK = put("nsink", [P, NH], F32)
        CWG = put("cwg", [P, 3, 2], F32)
        cur[0] = (cur[0] + 31) // 32 * 32
        r2 = cur[0]
        Q = put("q", [P, KD, T], F32, r2)
        CX = put("cx", [P, KD, CTX], F32, r2)
        K = put("k", [P, 2, T + 2 * BLK], F32, r2 + 16384)
        VH = put("vh", [P, NBLK + 2, 256], F32R, r2 + 22528)
        VL = put("vl", [P, NBLK + 2, 256], F32R, r2 + 28672)
        KCH = put("kch", [P, 2, CTX], F32R, r2 + 34816)
        KCL = put("kcl", [P, 2, CTX], F32R, r2 + 36864)
        VCH = put("vch", [P, 2, 256], F32R, r2 + 38912)
        VCL = put("vcl", [P, 2, 256], F32R, r2 + 40960)
        MASK = put("mask", [P, NBLK, 2 * BLK], F32R, r2 + 43008)
        o = r2 + 47104
        CXH = put("cxh", [P, KD, CTX], F32R, o)
        CXL = put("cxl", [P, KD, CTX], F32R, o + 8192)
        COS = put("cos", [P, T], F32, o + 16384)
        SIN = put("sin", [P, T], F32, o + 18432)
        ROT = put("rot", [P, T], F32, o + 20480)
        MASKF = put("maskf", [P, NBLK, 2 * BLK], F32, o)
        QSH = put("qsh", [P, KD, BLK], F32R, o)
        QSL = put("qsl", [P, KD, BLK], F32R, o + 4096)
        KSH = put("ksh", [P, 2, WIN], F32R, o + 8192)
        KSL = put("ksl", [P, 2, WIN], F32R, o + 11264)
        PTH = put("pth", [P, NKEY], F32R, o + 14336)
        PTL = put("ptl", [P, NKEY], F32R, o + 16896)
        PR = [put(f"pr{i}", [P, NKEY], F32, o + 19456 + 2560 * i) for i in range(2)]
        ON = put("on", [P, D], F32, o + 24576)
        FH = put("fh", [P, KD, T], F32R, r2)
        FL = put("fl", [P, KD, T], F32R, r2 + 16384)
        SG = [put(f"sg{i}", [P, T], F32, r2 + 32768 + 2048 * i) for i in range(2)]
        CS = put("cs", [P, 2, T], F32, r2 + 32768)
        UP = put("up", [P, 2, T + 2], F32, r2 + 36864)
        YC = put("yc", [P, 2, T], F32, r2 + 40992)
        o = limit // 32 * 32 - 18432
        ZS = put("zs", [P, T], F32, o)
        QS = put("qs", [P, T], F32, o + 2048)
        M2 = put("m2", [P, T], F32, o + 4096)
        VAR = put("var", [P, T], F32, o + 6144)
        RSTD = put("rstd", [P, T], F32, o + 8192)
        SQ = [put(f"sq{i}", [P, T], F32, o + 10240 + 2048 * i) for i in range(2)]
        TMP = [put(f"tmp{i}", [P, T], F32, o + 14336 + 2048 * i) for i in range(2)]
        TM2 = put("tm2", [P, 2, T], F32, o + 14336)
        assert r2 + 47104 + 28672 <= limit and r2 + 45152 <= o
        HF = put("hf", [P, KD, T], F32, o_ah)
        HT = put("ht", [P, 4, D], F32, o_al)
        XTH = put("xth", [P, KD, CAP], F32R, o_xz)
        XTL = put("xtl", [P, KD, CAP], F32R, o_xz + 8192)
        XR = put("xr", [P, 4, D], F32, r2)
        RAW += [put(f"raw{i}", [P, UNIT], F32, r2 + 16384 + 8192 * (i - 4)) for i in (4, 5)]
        XG = put("xg", [P, 2, D], F32, r2 + 32768)
        HH = put("hh", [P, 2, 2, CAP], F32R, r2 + 40960)
        HL = put("hl", [P, 2, 2, CAP], F32R, r2 + 45056)
        SE = put("se", [P, 2, 2 * CAP], F32, r2 + 49152)
        HE = put("he", [P, 2, 2 * CAP], F32, r2 + 53248)
        YT = put("yt", [P, KD, CAP], F32, r2 + 57344)
        RT = put("rt", [P, N_RC], F32, r2 + 45568)
        ZT = put("zt", [P, D], F32, r2 + 47104)
        o = r2 + 65536
        LG = put("lg", [P, 4, NE], F32, o + 1088)
        MX = put("mx", [P, 4, 8], F32, o + 1216)
        IX = put("ix", [P, 4, 8], U32, o + 1344)
        IXF = put("ixf", [P, 4, 2], F32, o + 1472)
        OH = put("oh", [P, 2, 4, NE], F32, o + 1504)
        MM = put("mm", [P, 4, NE], F32, o + 1760)
        DD = put("dd", [P, 4, 4], F32, o + 1888)
        PB = put("pb", [P, 4, NE], F32, o + 1952)
        PT1 = put("pt1", [P, 4, NE], F32, o + 2080)
        DF = put("df", [P, 2, 4], F32, o + 2208)
        RF = put("rf", [P, 16], F32, o + 2240)
        OV = put("ov", [P, 3, NE], F32, o + 2304)
        ADJ = put("adj", [P, NE], F32, o + 2400)
        YS = put("ys", [P, 2, D], F32, o_al)
        o = r2 + 68000 // 32 * 32
        DI = put("di", [P, 2, 4], U32, o)
        GA = put("ga", [P, 2, 4], F32, o + 32)
        RI = put("ri", [P, 16], I32, o + 64)
        assert o + 128 <= limit
        LNR = put("lnr", [P, 2, D], F32, base)
        G2R = put("g2r", [P, D], F32, base + 8192)
        DG = put("dg", [P, KD, P], F32, base + 12288)
        YG = [[put(f"yg{i}{c}", [P, D], F32, base + 16384 + 8192 * i + 4096 * c) for c in range(2)] for i in range(2)]
        ZF = [put(f"zf{i}", [P, D], F32, base + 32768 + 4096 * i) for i in range(4)]
        BST = put("bst", [P, 2, 6], F32, base + 49152)
        BAG = put("bag", [P, 4], F32, base + 49280)

        PS = ctx.enter_context(nc.psum_tensor("ps", [P, 8, 512], F32))

        xg_d = nc.dram_tensor("dispatched_x", [N_ROWS, D], F32).ap()
        yg_d = nc.dram_tensor("expert_y", [N_ROWS, D], F32).ap()

        small_in, xin, cxin, rope_in, mask_in, rc_in, lnr_in = map(sem, (
            "small_in", "x_in", "ctx_in", "rope_in", "mask_in", "routing_const_in", "lnrow_in"))
        raw_loaded = [sem(f"raw_loaded{i}") for i in range(6)]
        raw_used = [sem(f"raw_used{i}") for i in range(6)]
        hi_ready = [sem(f"hi_ready{i}") for i in range(3)]
        unit_done = [sem(f"unit_done{i}") for i in range(3)]
        pair_free = [sem(f"pair_free{i}") for i in range(3)]
        mod_full = sem("mod_full")
        mod_free = sem("mod_free")
        dve_step, act_step = sem("dve_step"), sem("act_step")
        silc_ready, idr_ready, pads_ready = map(sem, ("silc_ready", "idr_ready", "pads_ready"))
        tmp_ready, ah_ready, al_ready = map(sem, ("tmp_ready", "ah_ready", "al_ready"))
        ctx_tmp, cxh_ready, cxl_ready = map(sem, ("ctx_tmp", "cxh_ready", "cxl_ready"))
        kvh_ready, kvl_ready, rope_done = map(sem, ("kvh_ready", "kvl_ready", "rope_done"))
        st_h, st_l = sem("staged_hi"), sem("staged_lo")
        s_full = [sem(f"scores_full{i}") for i in range(2)]
        nm_ready = sem("max_ready")
        p_ready = [sem(f"probs_ready{i}") for i in range(2)]
        pt_full, pth_ready, ptl_ready, av_done = map(sem, ("pt_full", "pth_ready", "ptl_ready", "av_done"))
        es_in, es_ready, on_ready, ot_full, oh_ready, ol_ready = map(sem, (
            "es_in", "es_ready", "on_ready", "ot_full", "oh_ready", "ol_ready"))
        z_ready, sq_ready, stats_in, stats_full, m2_ready, var_ready, sd_ready = map(sem, (
            "z_ready", "sq_ready", "stats_in", "stats_full", "m2_ready", "var_ready", "sd_ready"))
        sg_ready, f_ready, fh_ready, fl_ready = map(sem, ("silu_ready", "f_ready", "fh_ready", "fl_ready"))
        cs_ready, yc_ready = sem("cs_ready"), sem("yc_ready")
        lg_full, mask_ready, pos_full, gate_in, gate_exp = map(sem, (
            "logits_full", "choice_ready", "pos_full", "gate_in", "gate_exp"))
        tr_full, tr_free = sem("rows_full"), sem("rows_free")
        dest_ready, routed = sem("dest_ready"), sem("routed")
        zero_ready, zeroed, scattered = sem("zero_ready"), sem("zeroed"), sem("scattered")
        xg_in, xt_full, xth_ready, xtl_ready = map(sem, ("xg_in", "xt_full", "xth_ready", "xtl_ready"))
        se_ready, he_ready, hh_ready, hl_ready = map(sem, ("se_ready", "he_ready", "hh_ready", "hl_ready"))
        y_zero, yt_a, yt_b, yrow_full, ys_a, ys_b, ys_free, y_out = map(sem, (
            "y_zero", "yt_a", "yt_b", "yrow_full", "ys_a", "ys_b", "ys_free", "y_out"))
        y_done, pool_turn = sem("expert_y_done"), sem("pool_turn")
        dg_ready, g2_full, g2_ready = sem("dg_ready"), sem("g2_full"), sem("g2_ready")
        yg_in = [sem(f"yg_in{i}") for i in range(2)]
        yg_free = sem("yg_free")
        v_ready, sdf_ready, out_ready, out_done = map(sem, ("v_ready", "sdf_ready", "out_ready", "out_done"))

        def sm(name):
            a, b = SM[name]
            return SMALL[:, a:b]

        ident = sm("ident")
        mean_w = sm("mean")
        bmod = sm("bmod").rearrange("p (v t) -> p v t", v=2)
        lng = sm("lng").rearrange("p (s k) -> p s k", s=4)
        lnb = sm("lnb").rearrange("p (s k) -> p s k", s=4)
        cw = sm("cw").rearrange("p (j k) -> p j k", j=3)
        wr = sm("wr").rearrange("p (k e) -> p k e", k=KD)
        ones = RT[:, 0:P]
        upper = RT[:, P:2 * P]

        def scores_view(b):
            return PS[:, 2 * b:2 * b + 2, :].rearrange("p b n -> p (b n)")[:, 512 - CTX:512 + WIN]

        def raw8(s):
            return RAW[s][:].rearrange("p (k n) -> p k n", k=KD)

        def modcol(layer, chunk):
            a = layer * 48 + chunk * 8
            return MOD[:, 0, a:a + 8]

        def ring_per(body):
            per = {}
            for kind, r, h, _ in positions(body):
                per[("raw", r)] = per.get(("raw", r), 0) + 1
                if kind == "s":
                    per[("hs", h)] = per.get(("hs", h), 0) + 1
                    per[("ud", h)] = per.get(("ud", h), 0) + 1
            return per

        MOE_BODY = [(p, p % 3) for p in range(6)]
        PER_EXP_RING = {}
        for r_, h_ in MOE_BODY:
            PER_EXP_RING[("raw", r_)] = PER_EXP_RING.get(("raw", r_), 0) + 1
            PER_EXP_RING[("hs", h_)] = PER_EXP_RING.get(("hs", h_), 0) + 1
            PER_EXP_RING[("ud", h_)] = PER_EXP_RING.get(("ud", h_), 0) + 1

        def times(per, n):
            return {k: v * n for k, v in per.items()}

        def attention_act(act, t):
            cc = {}

            with act.Fori(0, NBLK) as b:
                act.wait_ge(rope_done, 10)
                act.wait_ge(st_l, b + 1)
                act.activation(QSH[:], Q[:, :, bass.ds(b * BLK, BLK)], ACT.Copy).then_inc(st_h, 1)
                act.activation(KSH[:], K[:, :, bass.ds(b * BLK, WIN)], ACT.Copy).then_inc(st_h, 1)

                def probs(h):
                    act.wait_ge(nm_ready, b * NH + (h + 1))
                    if h >= 2:
                        act.wait_ge(pt_full, b * NH + (h - 1))
                    act.activation(PR[h % 2][:], scores_view(h % 2), ACT.Exp, bias=NM[:, h:h + 1], scale=SCALE,
                                   accum_out=LSUM[:, h:h + 1]).then_inc(p_ready[h % 2], 1)

                def pt_hi(h):
                    act.wait_ge(pt_full, b * NH + (h + 1))
                    if h >= 1:
                        act.wait_ge(av_done, b * NH + h)
                    act.activation(PTH[:], PS[:, 4:6, :].rearrange("p b n -> p (b n)")[:, 0:NKEY],
                                   ACT.Copy).then_inc(pth_ready, 1)

                for h in range(NH):
                    probs(h)
                    if h >= 1:
                        pt_hi(h - 1)
                pt_hi(NH - 1)
                act.wait_ge(es_in, b + 1)
                act.activation(ES[:], ES[:], ACT.Exp).then_inc(es_ready, 1)
                act.wait_ge(ot_full, b + 1)
                act.activation(AH[:, :, bass.ds(b * BLK, BLK)],
                               PS[:, 0:2, :].rearrange("p b (k n) -> p (b k) n", k=4), ACT.Copy).then_inc(oh_ready, 1)

        def attention_dve(dve, t):
            per = {"step": ATT_STEPS}
            dve.sem_inc(st_l, 1)
            with t.loop(dve, NBLK, per) as b:
                dve.wait_ge(rope_done, 10)
                dve.wait_ge(st_h, b * 2 + 1)
                dve.tensor_tensor(QSL[:], Q[:, :, bass.ds(b * BLK, BLK)], QSH[:].bitcast(F32), ALU.subtract)
                dve.wait_ge(st_h, b * 2 + 2)
                dve.tensor_tensor(KSL[:], K[:, :, bass.ds(b * BLK, WIN)], KSH[:].bitcast(F32),
                                  ALU.subtract).then_inc(kvl_ready, 1)

                def head_max(h):
                    dve.wait_ge(s_full[h % 2], b * 8 + (h // 2 + 1))

                    def link(ins):
                        ins.then_inc(dve_step, 1)
                        dve.wait_ge(dve_step, t.n("step"))
                    link(dve.tensor_reduce(NRM[:, h:h + 1], scores_view(h % 2), AX.X, ALU.max, negate=True))
                    dve.scalar_tensor_tensor(out=NM[:, h:h + 1], in0=NRM[:, h:h + 1], scalar=SCALE,
                                             in1=NSINK[:, h:h + 1], op0=ALU.mult, op1=ALU.min).then_inc(nm_ready, 1)

                def pt_lo(h):
                    dve.wait_ge(pth_ready, b * NH + (h + 1))
                    dve.tensor_tensor(PTL[:], PS[:, 4:6, :].rearrange("p b n -> p (b n)")[:, 0:NKEY],
                                      PTH[:].bitcast(F32), ALU.subtract).then_inc(ptl_ready, 1)

                for h in range(NH):
                    head_max(h)
                    if h >= 1:
                        pt_lo(h - 1)
                dve.wait_ge(nm_ready, b * NH + NH)
                dve.tensor_tensor(ES[:], NM[:], SMALL[:, SM["sink"][0]:SM["sink"][1]], ALU.add).then_inc(es_in, 1)
                pt_lo(NH - 1)

                def link(ins):
                    ins.then_inc(dve_step, 1)
                    dve.wait_ge(dve_step, t.n("step"))
                dve.wait_ge(es_ready, b + 1)
                link(dve.tensor_tensor(RS[:], LSUM[:], ES[:], ALU.add))
                link(dve.reciprocal(RS[:], RS[:]))
                dve.wait_ge(av_done, b * NH + NH)
                for c in range(2):
                    ins = dve.tensor_tensor(ON[:, 512 * c:512 * c + 512].rearrange("p (h d) -> p h d", d=HD),
                                            PS[:, 6 + c, :].rearrange("p (h d) -> p h d", d=HD),
                                            RS[:, 8 * c:8 * c + 8].unsqueeze(2).to_broadcast([P, 8, HD]), ALU.mult)
                ins.then_inc(on_ready, 1)
                dve.wait_ge(oh_ready, b + 1)
                dve.tensor_tensor(AL[:, :, bass.ds(b * BLK, BLK)],
                                  PS[:, 0:2, :].rearrange("p b (k n) -> p (b k) n", k=4),
                                  AH[:, :, bass.ds(b * BLK, BLK)].bitcast(F32), ALU.subtract).then_inc(ol_ready, 1)
                dve.wait_ge(ol_ready, b + 1)
                dve.sem_inc(st_l, 1)

        def attention_pe(pe, t, three):
            pe.wait_ge(idr_ready, 2)
            with pe.Fori(0, NBLK) as b:
                pe.wait_ge(kvl_ready, b + 1)

                def scores(h):
                    f, j = h % 2, h // 2
                    kp = j // 4
                    rows_ = slice(HD * f, HD * f + HD)
                    if h >= 2:
                        pe.wait_ge(p_ready[f], b * 8 + h // 2)
                    wh, wl = QSH[rows_, j, :], QSL[rows_, j, :]
                    three(PS[:, 2 * f, 512 - CTX:512], wh, wl, KCH[rows_, kp, :], KCL[rows_, kp, :], True, True)
                    three(PS[:, 2 * f + 1, 0:WIN], wh, wl, KSH[rows_, kp, :], KSL[rows_, kp, :], True, False)
                    edge = PS[:, 2 * f + 1, 0:WIN].rearrange("p (c n) -> p c n", c=3)[:, 0:3:2, :]
                    pe.matmul(edge, IDR[:], MASK[:, bass.ds(b, 1), :].rearrange("p o (c n) -> p (o c) n", c=2),
                              start=False, stop=True, skip_group_check=True).then_inc(s_full[f], 1)

                def turn(h):
                    pe.wait_ge(p_ready[h % 2], b * 8 + (h // 2 + 1))
                    if h >= 1:
                        pe.wait_ge(ptl_ready, b * NH + h)
                    for c in range(5):
                        ins = pe.transpose(PS[:, 4 + c // 4, (c % 4) * P:(c % 4 + 1) * P],
                                           PR[h % 2][:, c * P:(c + 1) * P], ident)
                    ins.then_inc(pt_full, 1)

                def values(h):
                    pe.wait_ge(ptl_ready, b * NH + (h + 1))
                    kv = 2 * (h // 8) + h % 2
                    outp = PS[:, 6 + h // 8, (h % 8) * HD:(h % 8 + 1) * HD]
                    for c in range(5):
                        cols = slice(kv * HD, kv * HD + HD)
                        if c < 2:
                            vh, vl = VCH[:, c, cols], VCL[:, c, cols]
                        else:
                            vh = VH[:, bass.ds(b + (c - 2), 1), cols].rearrange("p o n -> p (o n)")
                            vl = VL[:, bass.ds(b + (c - 2), 1), cols].rearrange("p o n -> p (o n)")
                        ins = three(outp, PTH[:, c * P:(c + 1) * P], PTL[:, c * P:(c + 1) * P], vh, vl, c == 0, c == 4)
                    ins.then_inc(av_done, 1)

                for h in range(NH):
                    scores(h)
                    if h >= 1:
                        turn(h - 1)
                    if h >= 2:
                        values(h - 2)
                turn(NH - 1)
                values(NH - 2)
                values(NH - 1)
                pe.wait_ge(on_ready, b + 1)
                for j in range(KD):
                    ins = pe.transpose(PS[:, j // 4, (j % 4) * P:(j % 4 + 1) * P], ON[:, j * P:(j + 1) * P], ident)
                ins.then_inc(ot_full, 1)

        block = ctx.enter_context(nc.Block())

        @block.sync
        def _(sp):
            t = Turns()
            sp.dma_start(SMALL[:], small).then_inc(small_in, 16)

            def load(slot, src):
                sp.wait_ge(raw_used[slot], t.n(("raw", slot)))
                sp.dma_start(RAW[slot][:], src).then_inc(raw_loaded[slot], 16)

            u0 = 0
            for name, count, body in SEGMENTS:
                pos = positions(body)

                def emit(i):
                    for j, (_, r, _, _) in enumerate(pos):
                        load(r, w_pre[bass.ds(i * len(body) + (u0 + j), 1), :, :].rearrange("o p n -> (o p) n")
                             if not isinstance(i, int) else w_pre[u0 + j])
                if count > 1:
                    per = {k: v for k, v in ring_per(body).items() if k[0] == "raw"}
                    with t.loop(sp, count, per) as i:
                        emit(i)
                else:
                    emit(0)
                if name == "modA":
                    sp.dma_start(COS[:], rope[:, 0:T]).then_inc(rope_in, 16)
                    sp.dma_start(SIN[:], rope[:, T:2 * T]).then_inc(rope_in, 16)
                u0 += count * len(body)

            per_g = {("raw", r): 1 for r, _ in MOE_BODY}

            def expert(e):
                with t.loop(sp, GROUPS, per_g) as g:
                    for j, (r, _) in enumerate(MOE_BODY):
                        load(r, w_moe[bass.ds(e * (6 * GROUPS) + g * 6 + j, 1), :, :].rearrange("o p n -> (o p) n"))

            sp.wait_ge(routed, 1)
            with t.loop(sp, NE, times(per_g, GROUPS)) as e:
                expert(e)
            n_over = sp.value_load(RI[0:1, 11:12], min_val=0, max_val=MAX_OVER)
            with sp.If(n_over > 0):
                with t.loop(sp, n_over, times(per_g, GROUPS)) as x:
                    expert(sp.value_load(RI[0:1, bass.ds(x + 8, 1)], min_val=0, max_val=NE - 1))

            sp.wait_ge(y_done, 1)
            sp.dma_start(LNR[:], lnrow.rearrange("p (a n) -> p a n", a=2)).then_inc(lnr_in, 16)
            outv = out[0].rearrange("(t p) d -> t p d", p=P)
            for i in range(4):
                sp.wait_ge(out_ready, i + 1)
                sp.dma_start(outv[i], ZF[i][:]).then_inc(out_done, 16)
            sp.wait_ge(out_done, 64)

        @block.gpsimd
        def _(pool):
            pool.dma_start(XZ[:], xT_in).then_inc(xin, 16)
            pool.dma_start(CX[:], ctxT_in).then_inc(cxin, 16)
            pool.dma_start(MASKF[:], maskin).then_inc(mask_in, 16)
            pool.wait_ge(ol_ready, NBLK)
            pool.dma_start(RT[:], rconst).then_inc(rc_in, 16)
            pool.wait_ge(zero_ready, 1)
            with pool.Fori(0, N_ROWS // P) as a:
                pool.dma_start(xg_d[bass.ds(a * P, P), :], ZT[:]).then_inc(zeroed, 16)
            with pool.Fori(NE * CAP // P, N_ROWS // P) as a:
                pool.dma_start(yg_d[bass.ds(a * P, P), :], ZT[:]).then_inc(zeroed, 16)
            pool.wait_ge(zeroed, 16 * (N_ROWS + MAX_OVER * CAP) // P)
            pool.wait_ge(dest_ready, 1)
            pool.wait_ge(tr_free, 4)
            for c in range(2):
                for i in range(4):
                    pool.indirect_dma_start(xg_d[:, :], bass.IndirectOffsetOnAxis(ap=DI[:, c, i:i + 1], axis=0),
                                            HT[:, i, :], None).then_inc(scattered, 16)
            pool.wait_ge(scattered, 16 * 8)

            def rows(buf, i):
                at = slice(i * CAP, (i + 1) * CAP) if isinstance(i, int) else bass.ds(i * CAP, CAP)
                return buf[at, :].rearrange("(s p) n -> p s n", p=P)

            def store(i, n):
                pool.wait_ge(ys_a, n)
                pool.wait_ge(ys_b, n)
                pool.sem_inc(pool_turn, 1)
                pool.dma_start(rows(yg_d, i), YS[:]).then_inc(y_out, 16)
                pool.wait_ge(y_out, n * 16)
                pool.sem_inc(ys_free, 1)

            pool.wait_ge(routed, 1)
            pool.dma_start(XG[:], rows(xg_d, 0)).then_inc(xg_in, 16)
            with pool.Fori(0, NE - 1) as e:
                pool.wait_ge(xt_full, e + 1)
                pool.sem_inc(pool_turn, 1)
                pool.dma_start(XG[:], rows(xg_d, e + 1)).then_inc(xg_in, 16)
                store(e, e + 1)
            store(NE - 1, NE)
            n_over = pool.value_load(RI[0:1, 11:12], min_val=0, max_val=MAX_OVER)
            with pool.If(n_over > 0):
                with pool.Fori(0, n_over) as x:
                    pool.dma_start(XG[:], rows(xg_d, x + NE)).then_inc(xg_in, 16)
                    store(x + NE, x + (NE + 1))
            pool.sem_inc(y_done, 1)
            for i in range(4):
                if i >= 2:
                    pool.wait_ge(yg_free, i - 1)
                for c in range(2):
                    pool.indirect_dma_start(YG[i % 2][c][:, :], None, yg_d[:, :],
                                            bass.IndirectOffsetOnAxis(ap=DI[:, c, i:i + 1], axis=0)
                                            ).then_inc(yg_in[i % 2], 16)

        @block.scalar
        def _(act):
            t = Turns()
            steps = [0]

            def full_split(r, h):
                act.wait_ge(raw_loaded[r], t.n(("raw", r)) * 16)
                act.wait_ge(unit_done[h], t.n(("hs", h)))
                act.activation(HI[h][:], RAW[r][:], ACT.Copy).then_inc(hi_ready[h], 1)

            def done(h):
                act.wait_ge(unit_done[h], t.n(("ud", h)) + 1)

            for s in raw_used:
                act.sem_inc(s, 1)
            for s in unit_done:
                act.sem_inc(s, 1)
            for s in pair_free:
                act.sem_inc(s, 1)
            act.sem_inc(mod_free, 1)
            act.sem_inc(ys_free, 1)
            act.wait_ge(small_in, 16)
            act.activation(SILC[:].rearrange("p k v -> p (k v)"), sm("cc"), ACT.Silu).then_inc(silc_ready, 1)
            act.activation(IDR[:], ident, ACT.Copy).then_inc(idr_ready, 1)
            act.wait_ge(mask_in, 16)
            act.activation(MASK[:], MASKF[:], ACT.Copy).then_inc(idr_ready, 1)

            cnt = {"tmp": 0}

            def to_hi(k):
                cnt["tmp"] += 1
                act.wait_ge(tmp_ready, cnt["tmp"])
                act.activation(AH[:, k, :], TMP[k % 2][:], ACT.Copy).then_inc(ah_ready, 1)

            act.wait_ge(idr_ready, 2)
            for k in range(KD):
                act.wait_ge(ctx_tmp, k + 1)
                act.activation(CXH[:, k, :], TMP[k % 2][:, 0:CTX], ACT.Copy).then_inc(cxh_ready, 1)
            for k in range(KD):
                to_hi(k)

            def mods(n):
                for r in n:
                    t.skip(("raw", r), 1)

            def layer_norm(stage):
                act.wait_ge(stats_full, stage)
                act.activation(M2[:], PS[:, 6, :], ACT.Square).then_inc(m2_ready, 1)
                act.wait_ge(var_ready, stage)
                act.activation(RSTD[:], VAR[:], ACT.Sqrt).then_inc(sd_ready, 1)

            zc = [0]

            def square(k):
                zc[0] += 1
                act.wait_ge(z_ready, zc[0])
                act.activation(SQ[k % 2][:], XZ[:, k, :], ACT.Square).then_inc(sq_ready, 1)

            fl = {"n": 0}
            for si, (name, count, body) in enumerate(SEGMENTS):
                pos = positions(body)
                svs = [p for p in pos if p[0] == "s"]
                if name == "modA":
                    mods([p[1] for p in pos] * count)
                    full_split(0, 0)
                    continue
                skipper = [[] for _ in svs]
                for p in pos:
                    if p[0] == "s":
                        at = p[3]
                    else:
                        skipper[at].append(p[1])

                if name[:2] == "up":
                    f0 = fl["n"]
                    per = dict(ring_per(body))
                    ns = len(svs)
                    with t.loop(act, count, per) as i:
                        for j, (_, r, h, _) in enumerate(svs):
                            mods(skipper[j])
                            nx = svs[(j + 1) % ns]
                            full_split(nx[1], nx[2])
                            done(h)
                            b = j % 2
                            act.activation(SG[b][:], PS[:, 2 * b, :], ACT.Silu).then_inc(sg_ready, 1)
                            act.wait_ge(f_ready, i * ns + (f0 + j + 1))
                            act.activation(FH[:, bass.ds(i * ns + j, 1), :].rearrange("p o n -> p (o n)"),
                                           TMP[b][:], ACT.Copy).then_inc(fh_ready, 1)
                    fl["n"] += count * ns
                    continue
                if name == "conv":
                    with t.loop(act, count, ring_per(body)) as i:
                        for j, (_, r, h, _) in enumerate(svs):
                            nx = svs[(j + 1) % 3]
                            full_split(nx[1], nx[2])
                            done(h)
                            if j == 0:
                                act.activation(CS[:], PS[:, 0:2, :], ACT.Copy).then_inc(cs_ready, 1)
                            elif j == 2:
                                act.wait_ge(yc_ready, i + 1)
                                act.activation(FH[:, bass.ds(i * 2, 2), :], TM2[:], ACT.Copy).then_inc(fh_ready, 1)
                    continue
                if name == "q":
                    with t.loop(act, count, ring_per(body)) as i:
                        for j, (_, r, h, _) in enumerate(svs):
                            mods(skipper[j])
                            nx = svs[(j + 1) % len(svs)]
                            full_split(nx[1], nx[2])
                            done(h)
                    attention_act(act, t)
                    continue
                for j, (_, r, h, _) in enumerate(svs):
                    mods(skipper[j])
                    if name != "co" or j + 1 < len(svs):
                        nx = svs[(j + 1) % len(svs)]
                        full_split(nx[1], nx[2])
                    done(h)
                    if name == "kv" and j == 0:
                        act.activation(KCH[:].rearrange("p a n -> p (a n)"), PS[:, 2, :], ACT.Copy).then_inc(kvh_ready, 1)
                    if name == "kv" and j == 1:
                        act.activation(VCH[:].rearrange("p a n -> p (a n)"), PS[:, 3, :], ACT.Copy).then_inc(kvh_ready, 1)
                        act.activation(VH[:, 1:5, :].rearrange("p (b a) n -> p b (a n)", b=2), PS[:, 4:6, :],
                                       ACT.Copy).then_inc(kvh_ready, 1)
                    if name in ("o", "dn2", "co"):
                        square(2 * j)
                        square(2 * j + 1)
                if name in ("o", "dn2"):
                    layer_norm({"o": 1, "dn2": 2}[name])
                    for k in range(KD):
                        to_hi(k)
                if name == "co":
                    layer_norm(3)

            act.wait_ge(gate_in, 1)
            act.activation(DD[:, 1, :], DD[:, 0, :], ACT.Exp).then_inc(gate_exp, 1)
            for i in range(8):
                act.wait_ge(tr_full, i + 1)
                dst = HT[:, i, :] if i < 4 else XR[:, i - 4, :]
                act.activation(dst.rearrange("p (b n) -> p b n", b=2), PS[:, 2 + 2 * (i % 2):4 + 2 * (i % 2), :],
                               ACT.Copy).then_inc(tr_free, 1)
            act.wait_ge(tr_free, 8)
            act.sem_inc(pair_free[1], 1)
            act.sem_inc(pair_free[2], 1)

            per_g = dict(times(PER_EXP_RING, 1))
            per_g.update({"he": 2})
            act.wait_ge(routed, 1)

            def expert_round(r):
                full_split(0, 0)
                act.wait_ge(xt_full, r)
                for q in range(2):
                    act.activation(XTH[:, 4 * q:4 * q + 4, :].rearrange("p (b k) n -> p b (k n)", b=2),
                                   PS[:, 2 * q:2 * q + 2, :], ACT.Copy).then_inc(xth_ready, 1)
                def group(last):
                    for j, (_, h) in enumerate(MOE_BODY):
                        if j < 5 or not last:
                            full_split(*MOE_BODY[(j + 1) % 6])
                        done(h)
                        if j in (0, 2):
                            act.activation(SE[:, j // 2, :], PS[:, j, :], ACT.Silu).then_inc(se_ready, 1)
                        if j in (1, 3):
                            act.wait_ge(he_ready, t.n("he"))
                            act.activation(HH[:, j // 2].rearrange("p a n -> p (a n)"), HE[:, j // 2, :],
                                           ACT.Copy).then_inc(hh_ready, 1)

                with t.loop(act, GROUPS - 1, per_g):
                    group(False)
                group(True)
                act.activation(YT[:, 0:4, :].rearrange("p (b k) n -> p b (k n)", b=2), PS[:, 4:6, :],
                               ACT.Copy).then_inc(yt_a, 1)
                act.wait_ge(yrow_full, r)
                act.wait_ge(ys_free, r)
                act.activation(YS[:, 0, :].rearrange("p (b n) -> p b n", b=2), PS[:, 0:2, :], ACT.Copy).then_inc(ys_a, 1)

            per_e = times(per_g, GROUPS)
            with t.loop(act, NE, per_e) as e:
                expert_round(e + 1)
            n_over = act.value_load(RI[0:1, 11:12], min_val=0, max_val=MAX_OVER)
            with act.If(n_over > 0):
                with t.loop(act, n_over, per_e) as x:
                    expert_round(x + (NE + 1))

            act.wait_ge(g2_full, 1)
            act.activation(G2R[:].rearrange("p (b n) -> p b n", b=2), PS[:, 0:2, :], ACT.Copy).then_inc(g2_ready, 1)
            for i in range(4):
                act.wait_ge(v_ready, i + 1)
                act.activation(BAG[:, 3:4], BAG[:, 2:3], ACT.Sqrt).then_inc(sdf_ready, 1)

        @block.vector
        def _(dve):
            t = Turns()

            def step(ins):
                ins.then_inc(dve_step, 1)
                dve.wait_ge(dve_step, t.n("step"))

            def split(r, h):
                dve.wait_ge(hi_ready[h], t.n(("hs", h)))
                dve.tensor_tensor(LO[h][:], RAW[r][:], HI[h][:].bitcast(F32), ALU.subtract).then_inc(raw_used[r], 1)

            def done(h):
                dve.wait_ge(unit_done[h], t.n(("ud", h)) + 1)

            mf = [1]

            def mod_evac(u, r):
                dve.wait_ge(mod_full, t.n("mod"))
                dve.sem_inc(raw_used[r], 1)
                if isinstance(u, int):
                    o_, b_ = MOD[:, :, 2 * u:2 * u + 2], bmod[:, :, 2 * u:2 * u + 2]
                else:
                    o_, b_ = MOD[:, :, bass.ds(u * 2, 2)], bmod[:, :, bass.ds(u * 2, 2)]
                dve.tensor_tensor(o_, PS[:, 7, 0:4].rearrange("p (t v) -> p v t", v=2), b_,
                                  ALU.add).then_inc(mod_free, 1)

            dve.memset(K[:, :, 0:BLK], 0.0)
            dve.memset(K[:, :, BLK + T:], 0.0)
            step(dve.memset(ROT[:], 0.0))
            dve.tensor_copy(VH[:, 0, :], ROT[:, 0:256])
            dve.tensor_copy(VH[:, 5, :], ROT[:, 0:256])
            dve.tensor_copy(VL[:, 0, :], ROT[:, 0:256])
            dve.tensor_copy(VL[:, 5, :], ROT[:, 0:256]).then_inc(pads_ready, 1)
            dve.wait_ge(small_in, 16)
            step(dve.tensor_scalar(NSINK[:], sm("sink"), -1.0, None, ALU.mult))
            with t.loop(dve, 2, {"mod": 4}) as i:
                for j in range(4):
                    mod_evac(i * 4 + j, j)
            mf[0] += 8
            dve.wait_ge(mod_free, 9)
            dve.tensor_scalar(COEF[:, 0, 0, :], modcol(0, 1), 1.0, None, ALU.add)
            step(dve.tensor_scalar(CG[:], MOD[:, 1, 8:16], 1.0, None, ALU.add))
            dve.wait_ge(cxin, 16)
            for k in range(KD):
                if k >= 2:
                    dve.wait_ge(cxl_ready, k - 1)
                dve.tensor_scalar(TMP[k % 2][:, 0:CTX], CX[:, k, :], CG[:, k:k + 1], MOD[:, 1, k:k + 1],
                                  ALU.mult, ALU.add).then_inc(ctx_tmp, 1)
                dve.wait_ge(ctx_tmp, k + 1)
                dve.wait_ge(cxh_ready, k + 1)
                dve.tensor_tensor(CXL[:, k, :], TMP[k % 2][:, 0:CTX], CXH[:, k, :].bitcast(F32),
                                  ALU.subtract).then_inc(cxl_ready, 1)

            nt = [0]

            def modulate(stage, shift, n_of):
                for k in range(KD):
                    n_of(k)
                    nt[0] += 1
                    if nl[0]:
                        dve.wait_ge(al_ready, nl[0])
                    dve.tensor_scalar(TMP[k % 2][:], XZ[:, k, :], COEF[:, stage, 0, k:k + 1], shift[:, k:k + 1],
                                      ALU.mult, ALU.add).then_inc(tmp_ready, 1)
                    if k >= 1:
                        low(k - 1)
                    dve.wait_ge(tmp_ready, nt[0])
                    if stage == 0:
                        dve.tensor_scalar(XZ[:, k, :], XZ[:, k, :], ALPHA, None, ALU.mult)
                    else:
                        dve.tensor_scalar(XZ[:, k, :], XZ[:, k, :], COEF[:, stage, 2, k:k + 1],
                                          COEF[:, stage, 3, k:k + 1], ALU.mult, ALU.add)
                low(KD - 1)

            nl = [0]

            def low(k):
                nl[0] += 1
                dve.wait_ge(tmp_ready, nl[0])
                dve.wait_ge(ah_ready, nl[0])
                dve.tensor_tensor(AL[:, k, :], TMP[k % 2][:], AH[:, k, :].bitcast(F32),
                                  ALU.subtract).then_inc(al_ready, 1)

            dve.wait_ge(xin, 16)
            dve.wait_ge(cxl_ready, KD)
            modulate(0, MOD[:, 0, 0:8], lambda k: None)
            dve.wait_ge(al_ready, KD)

            def coefs(stage, ln, layer, ch_shift, ch_scale):
                c = COEF[:, stage]
                dve.wait_ge(mod_free, mf[0])
                g, b = lng[:, ln, :], lnb[:, ln, :]
                step(dve.tensor_scalar(c[:, 2, :], modcol(layer, ch_scale), 1.0, None, ALU.add))
                dve.tensor_tensor(c[:, 0, :], c[:, 2, :], g, ALU.mult)
                step(dve.tensor_tensor(c[:, 3, :], c[:, 2, :], b, ALU.mult))
                step(dve.tensor_tensor(c[:, 1, :], c[:, 3, :], modcol(layer, ch_shift), ALU.add))
                dve.tensor_scalar(c[:, 2, :], g, ALPHA, None, ALU.mult)
                step(dve.tensor_scalar(c[:, 3, :], b, ALPHA, None, ALU.mult))

            def norm_start(stage):
                dve.wait_ge(m2_ready, stage)
                dve.scalar_tensor_tensor(out=VAR[:], in0=PS[:, 7, :], scalar=EPS, in1=M2[:], op0=ALU.add,
                                         op1=ALU.subtract).then_inc(var_ready, 1)
                for k in range(4):
                    dve.tensor_tensor(XZ[:, k, :], XZ[:, k, :], PS[:, 6, :], ALU.subtract)
                dve.wait_ge(sd_ready, stage)
                step(dve.reciprocal(RSTD[:], RSTD[:]))
                for k in range(4, KD):
                    ins = dve.tensor_tensor(XZ[:, k, :], XZ[:, k, :], PS[:, 6, :], ALU.subtract)
                step(ins)

            def norm_k(k):
                step(dve.tensor_tensor(XZ[:, k, :], XZ[:, k, :], RSTD[:], ALU.mult))

            nz = [0]
            ns_ = [0]

            def residual(k, src, gate, first, last):
                ins = dve.scalar_tensor_tensor(out=XZ[:, k, :], in0=src, scalar=gate[:, k:k + 1], in1=XZ[:, k, :],
                                               op0=ALU.mult, op1=ALU.add)
                return ins

            def sums(k):
                ns_[0] += 1
                if k == 0:
                    dve.wait_ge(z_ready, ns_[0])
                    dve.tensor_copy(ZS[:], XZ[:, 0, :])
                    dve.wait_ge(sq_ready, ns_[0])
                    step(dve.tensor_copy(QS[:], SQ[0][:]))
                else:
                    dve.tensor_tensor(ZS[:], ZS[:], XZ[:, k, :], ALU.add)
                    dve.wait_ge(sq_ready, ns_[0])
                    ins = dve.tensor_tensor(QS[:], QS[:], SQ[k % 2][:], ALU.add)
                    if k == KD - 1:
                        ins.then_inc(stats_in, 1)
                    else:
                        step(ins)

            split(0, 0)
            rot_mask = [(i + 16) % 32 for i in range(32)]

            def rope_tile(bank, dst, last_read_sem):
                n = t.n("rope")
                if not isinstance(n, int) or n > 1:
                    dve.wait_ge(rope_done, n - 1)
                dve.tensor_tensor(dst, PS[:, bank, :], COS[:], ALU.mult)
                ins = dve.stream_shuffle(ROT[:], PS[:, bank, :], rot_mask)
                if last_read_sem is not None:
                    ins.then_inc(last_read_sem, 1)
                    dve.wait_ge(last_read_sem, t.n(("rel", id(last_read_sem))) + 1)
                else:
                    step(ins)
                step(dve.tensor_tensor(ROT[:], ROT[:], SIN[:], ALU.mult))
                dve.tensor_tensor(dst, dst, ROT[:], ALU.add).then_inc(rope_done, 1)

            fl = [0]
            unit_m = 8
            for name, count, body in SEGMENTS[1:]:
                pos = positions(body)
                svs = [p for p in pos if p[0] == "s"]
                ns = len(svs)
                nm = body.count("m")
                mf_after = mf[0] + nm * count
                ringp = {k: v for k, v in ring_per(body).items() if k[0] != "raw"}

                def mod_pair(i, j):
                    if nm:
                        if isinstance(i, int):
                            mod_evac(unit_m + 2 * j, 1)
                            mod_evac(unit_m + 2 * j + 1, 2)
                        else:
                            mod_evac(i * nm + (unit_m + 2 * j), 1)
                            mod_evac(i * nm + (unit_m + 2 * j + 1), 2)

                if name == "kv":
                    dve.wait_ge(rope_in, 32)
                    split(svs[1][1], svs[1][2])
                    done(svs[0][2])
                    dve.wait_ge(kvh_ready, 1)
                    dve.tensor_tensor(KCL[:].rearrange("p a n -> p (a n)"), PS[:, 2, :],
                                      KCH[:].rearrange("p a n -> p (a n)").bitcast(F32), ALU.subtract)
                    rope_tile(0, K[:, 0, BLK:BLK + T], None)
                    rope_tile(1, K[:, 1, BLK:BLK + T], pair_free[0])
                    mod_pair(0, 0)
                    split(svs[0][1], svs[0][2])
                    done(svs[1][2])
                    dve.wait_ge(kvh_ready, 2)
                    dve.tensor_tensor(VCL[:].rearrange("p a n -> p (a n)"), PS[:, 3, :],
                                      VCH[:].rearrange("p a n -> p (a n)").bitcast(F32),
                                      ALU.subtract).then_inc(pair_free[1], 1)
                    dve.wait_ge(kvh_ready, 3)
                    dve.tensor_tensor(VL[:, 1:5, :].rearrange("p (b a) n -> p b (a n)", b=2), PS[:, 4:6, :],
                                      VH[:, 1:5, :].rearrange("p (b a) n -> p b (a n)", b=2).bitcast(F32),
                                      ALU.subtract).then_inc(pair_free[2], 1)
                    mod_pair(0, 1)
                    t.n(("rel", id(pair_free[1])))
                elif name == "q":
                    per = dict(ringp)
                    per.update({"mod": nm, "step": 6, "rope": 4, ("rel", id(pair_free[0])): 1, ("rel", id(pair_free[1])): 1})
                    with t.loop(dve, count, per) as i:
                        for j, (_, r, h, _) in enumerate(svs):
                            nx = svs[(j + 1) % ns]
                            split(nx[1], nx[2])
                            done(h)
                            pf = pair_free[j]
                            for c in range(2):
                                dst = Q[:, bass.ds(i * 4 + (2 * j + c), 1), :].rearrange("p o n -> p (o n)")
                                rope_tile(2 * j + c, dst, pf if c else None)
                            mod_pair(i, j)
                    mf[0] = mf_after
                    attention_dve(dve, t)
                    dve.memset(ZT[:], 0.0).then_inc(zero_ready, 1)
                    coefs(1, 0, 0, 3, 4)
                elif name[:2] == "up":
                    f0 = fl[0]
                    per = dict(ringp)
                    per.update({"mod": nm} if nm else {})
                    with t.loop(dve, count, per) as i:
                        for j, (_, r, h, _) in enumerate(svs):
                            nx = svs[(j + 1) % ns]
                            split(nx[1], nx[2])
                            done(h)
                            b = j % 2
                            n = i * ns + (f0 + j + 1)
                            dve.wait_ge(sg_ready, n)
                            dve.tensor_tensor(TMP[b][:], SG[b][:], PS[:, 2 * b + 1, :], ALU.mult).then_inc(f_ready, 1)
                            dve.wait_ge(f_ready, n)
                            dve.sem_inc(pair_free[b], 1)
                            dve.wait_ge(fh_ready, n)
                            fs = bass.ds(i * ns + j, 1)
                            dve.tensor_tensor(FL[:, fs, :].rearrange("p o n -> p (o n)"), TMP[b][:],
                                              FH[:, fs, :].rearrange("p o n -> p (o n)").bitcast(F32),
                                              ALU.subtract).then_inc(fl_ready, 1)
                            mod_pair(i, j)
                            dve.wait_ge(fl_ready, n)
                    fl[0] += count * ns
                elif name == "conv":
                    coefs(3, 2, 1, 3, 4)
                    dve.memset(UP[:, :, 0:1], 0.0)
                    step(dve.memset(UP[:, :, T + 1:T + 2], 0.0))
                    per = dict(ringp)
                    per.update({"step": 6})
                    with t.loop(dve, count, per) as i:
                        split(*svs[1][1:3])
                        done(svs[0][2])
                        step(dve.tensor_copy(CWG[:], cw[:, :, bass.ds(i * 2, 2)]))
                        split(*svs[2][1:3])
                        done(svs[1][2])
                        dve.wait_ge(cs_ready, i + 1)
                        step(dve.tensor_tensor(UP[:, :, 1:T + 1], PS[:, 2:4, :], CS[:], ALU.mult))
                        dve.sem_inc(pair_free[0], 1)
                        dve.sem_inc(pair_free[1], 1)
                        for c in range(2):
                            ins = dve.tensor_scalar(YC[:, c, :], UP[:, c, 0:T], CWG[:, 0, c:c + 1], None, ALU.mult)
                        step(ins)
                        for w_ in (1, 2):
                            for c in range(2):
                                ins = dve.scalar_tensor_tensor(out=YC[:, c, :], in0=UP[:, c, w_:w_ + T],
                                                               scalar=CWG[:, w_, c:c + 1], in1=YC[:, c, :],
                                                               op0=ALU.mult, op1=ALU.add)
                            step(ins)
                        split(*svs[0][1:3])
                        done(svs[2][2])
                        dve.tensor_tensor(TM2[:], PS[:, 4:6, :], YC[:], ALU.mult).then_inc(yc_ready, 1)
                        dve.wait_ge(yc_ready, i + 1)
                        dve.sem_inc(pair_free[2], 1)
                        dve.wait_ge(fh_ready, i + (fl[0] + 1))
                        step(dve.tensor_tensor(FL[:, bass.ds(i * 2, 2), :], TM2[:],
                                               FH[:, bass.ds(i * 2, 2), :].bitcast(F32), ALU.subtract))
                    dve.sem_inc(fl_ready, 1)
                else:
                    layer = 1 if name == "co" else 0
                    gate = modcol(layer, 2 if name in ("o", "co") else 5)
                    lastpart = name in ("o", "dn2", "co")
                    tiles = DOWN6 if name == "dn1" else [[2 * j, 2 * j + 1] for j in range(4)]
                    dve.wait_ge(mod_free, mf[0])
                    for j, (_, r, h, _) in enumerate(svs):
                        if name != "co" or j + 1 < ns:
                            nx = svs[(j + 1) % ns]
                            split(nx[1], nx[2])
                        done(h)
                        for k in tiles[j]:
                            bank = k % 4
                            ins = residual(k, PS[:, bank, :], gate, False, lastpart)
                            if lastpart:
                                nz[0] += 1
                                ins.then_inc(z_ready, 1)
                                dve.wait_ge(z_ready, nz[0])
                                if k % 2:
                                    dve.sem_inc(pair_free[bank // 2], 1)
                                sums(k)
                            else:
                                step(ins)
                                if k % 2:
                                    dve.sem_inc(pair_free[bank // 2], 1)
                    if lastpart:
                        stage = {"o": 1, "dn2": 2, "co": 3}[name]
                        norm_start(stage)
                        dve.sem_inc(mod_free, 1)
                        mf[0] += 1
                        if stage < 3:
                            modulate(stage, COEF[:, stage, 1, :], norm_k)
                            dve.wait_ge(al_ready, nl[0])
                        else:
                            for k in range(KD):
                                norm_k(k)
                                step(dve.tensor_scalar(HF[:, k, :], XZ[:, k, :], COEF[:, 3, 0, k:k + 1],
                                                       COEF[:, 3, 1, k:k + 1], ALU.mult, ALU.add))
                                step(dve.tensor_scalar(XZ[:, k, :], XZ[:, k, :], COEF[:, 3, 2, k:k + 1],
                                                       COEF[:, 3, 3, k:k + 1], ALU.mult, ALU.add))
                            dve.sem_inc(tmp_ready, 1)
                    if name == "dn1":
                        coefs(2, 1, 1, 0, 1)
                unit_m += nm * count
                if name != "q":
                    mf[0] += nm * count

            dve.wait_ge(lg_full, 1)
            step(dve.tensor_copy(LG[:].rearrange("p t e -> p (t e)"), PS[:, 0, 0:32]))
            dve.sem_inc(pair_free[0], 1)
            for i in range(4):
                step(dve.max(MX[:, i, :], LG[:, i, :]))
                step(dve.max_index(IX[:, i, :], MX[:, i, :], LG[:, i, :]))
            step(dve.tensor_copy(IXF[:], IX[:, :, 0:2]))
            dve.wait_ge(rc_in, 16)
            for c in range(2):
                for i in range(4):
                    ins = dve.tensor_scalar(OH[:, c, i, :], RT[:, 256:264], IXF[:, i, c:c + 1], None, ALU.is_equal)
            step(ins)
            dve.tensor_tensor(MM[:], OH[:, 0], OH[:, 1], ALU.add).then_inc(mask_ready, 1)
            dve.tensor_tensor(DD[:, 0, :], MX[:, :, 1], MX[:, :, 0], ALU.subtract).then_inc(gate_in, 1)
            dve.wait_ge(gate_exp, 1)
            step(dve.tensor_scalar(DD[:, 2, :], DD[:, 1, :], 1.0, None, ALU.add))
            step(dve.reciprocal(GA[:, 0, :], DD[:, 2, :]))
            step(dve.tensor_tensor(GA[:, 1, :], DD[:, 1, :], GA[:, 0, :], ALU.mult))
            dve.wait_ge(pos_full, 1)
            step(dve.tensor_copy(RF[:, 0:8], PS[:, 0, 32:40]))
            step(dve.tensor_scalar(OV[:, 0, :], RF[:, 0:8], float(CAP), None, ALU.is_gt))
            step(dve.tensor_tensor_scan(OV[:, 1, :], RT[:, 0:8], OV[:, 0, :], 0.0, ALU.mult, ALU.add))
            step(dve.tensor_scalar(ADJ[:], OV[:, 1, :], float(CAP), float((NE - 2) * CAP), ALU.mult, ALU.add))
            dve.tensor_scalar(PT1[:].rearrange("p t e -> p (t e)"), PS[:, 0, 0:32], float(CAP), None, ALU.is_ge)
            step(dve.tensor_tensor(ADJ[:], ADJ[:], RT[:, 264:272], ALU.subtract))
            for i in range(4):
                dve.tensor_tensor(PB[:, i, :], PS[:, 0, 8 * i:8 * i + 8], RT[:, 264:272], ALU.add)
                ins = dve.tensor_tensor(PT1[:, i, :], PT1[:, i, :], ADJ[:], ALU.mult)
            step(ins)
            dve.sem_inc(pair_free[0], 1)
            step(dve.tensor_tensor(PB[:], PB[:], PT1[:], ALU.add))
            for c in range(2):
                step(dve.tensor_tensor(PT1[:], OH[:, c], PB[:], ALU.mult))
                step(dve.tensor_reduce(DF[:, c, :], PT1[:], AX.X, ALU.add))
            dve.tensor_copy(DI[:], DF[:]).then_inc(dest_ready, 1)
            step(dve.tensor_copy(RF[:, 11:12], OV[:, 1, 7:8]))
            for x in range(MAX_OVER):
                step(dve.tensor_scalar(OV[:, 2, :], OV[:, 1, :], float(x), None, ALU.is_le))
                step(dve.tensor_reduce(RF[:, 8 + x:9 + x], OV[:, 2, :], AX.X, ALU.add))
            step(dve.tensor_copy(RI[:, 0:12], RF[:, 0:12]))
            dve.wait_ge(tr_free, 8)
            dve.sem_inc(routed, 1)

            per_g = {k: v for k, v in PER_EXP_RING.items() if k[0] != "raw"}
            per_g.update({"se": 2, "hh": 2})

            def expert_round(r):
                split(0, 0)
                for q in range(2):
                    dve.wait_ge(xth_ready, t.n("xth"))
                    dve.tensor_tensor(XTL[:, 4 * q:4 * q + 4, :].rearrange("p (b k) n -> p b (k n)", b=2),
                                      PS[:, 2 * q:2 * q + 2, :],
                                      XTH[:, 4 * q:4 * q + 4, :].rearrange("p (b k) n -> p b (k n)", b=2).bitcast(F32),
                                      ALU.subtract).then_inc(pair_free[q], 1)
                def group(last):
                    for j, (_, h) in enumerate(MOE_BODY):
                        if j < 5 or not last:
                            split(*MOE_BODY[(j + 1) % 6])
                        done(h)
                        if j in (1, 3):
                            q = j // 2
                            n = t.n("se")
                            dve.wait_ge(se_ready, n)
                            dve.tensor_tensor(HE[:, q, :], SE[:, q, :], PS[:, j, :], ALU.mult).then_inc(he_ready, 1)
                            dve.wait_ge(he_ready, n)
                            dve.sem_inc(pair_free[q], 1)
                            dve.wait_ge(hh_ready, t.n("hh"))
                            dve.tensor_tensor(HL[:, q].rearrange("p a n -> p (a n)"), HE[:, q, :],
                                              HH[:, q].rearrange("p a n -> p (a n)").bitcast(F32),
                                              ALU.subtract).then_inc(hl_ready, 1)

                with t.loop(dve, GROUPS - 1, per_g):
                    group(False)
                group(True)
                dve.tensor_copy(YT[:, 4:8, :].rearrange("p (b k) n -> p b (k n)", b=2), PS[:, 6:8, :]).then_inc(yt_b, 1)
                dve.wait_ge(yt_a, r)
                dve.wait_ge(yt_b, r)
                dve.memset(PS[:, 4:8, :], 0.0).then_inc(y_zero, 1)
                dve.wait_ge(yrow_full, r)
                dve.wait_ge(ys_free, r)
                dve.wait_ge(ys_a, r)
                dve.sem_inc(pair_free[0], 1)
                dve.tensor_copy(YS[:, 1, :].rearrange("p (b n) -> p b n", b=2), PS[:, 2:4, :]).then_inc(ys_b, 1)
                dve.wait_ge(ys_b, r)
                dve.sem_inc(pair_free[1], 1)

            per_e = times(per_g, GROUPS)
            per_e["xth"] = 2
            dve.memset(PS[:, 4:8, :], 0.0).then_inc(y_zero, 1)
            with t.loop(dve, NE, per_e) as e:
                expert_round(e + 1)
            n_over = dve.value_load(RI[0:1, 11:12], min_val=0, max_val=MAX_OVER)
            with dve.If(n_over > 0):
                with t.loop(dve, n_over, per_e) as x:
                    expert_round(x + (NE + 1))

            dve.wait_ge(y_done, 1)
            for k in range(KD):
                ins = dve.tensor_scalar(DG[:, k, :], ident, MOD[:, 0, 88 + k:89 + k], float(D), ALU.mult, ALU.mult)
            ins.then_inc(dg_ready, 1)
            dve.wait_ge(lnr_in, 16)
            s0 = t.at["step"]
            fs = sem("final_step")
            fn = [0]

            def fstep(ins):
                fn[0] += 1
                ins.then_inc(fs, 1)
                dve.wait_ge(fs, fn[0])

            for i in range(4):
                z = ZF[i]
                y0, y1 = YG[i % 2]
                dve.wait_ge(yg_in[i % 2], 32 * (i // 2 + 1))
                fstep(dve.tensor_scalar(z[:], y0[:], GA[:, 0, i:i + 1], None, ALU.mult))
                dve.scalar_tensor_tensor(out=z[:], in0=y1[:], scalar=GA[:, 1, i:i + 1], in1=z[:], op0=ALU.mult,
                                         op1=ALU.add).then_inc(yg_free, 1)
                dve.wait_ge(yg_free, i + 1)
                if i == 0:
                    dve.wait_ge(g2_ready, 1)
                fstep(dve.tensor_tensor(z[:], z[:], G2R[:], ALU.mult))
                fstep(dve.tensor_tensor(z[:], z[:], XR[:, i, :], ALU.add))
                for c in range(2):
                    ins = dve.bn_stats(BST[:, c, :], z[:, 512 * c:512 * c + 512])
                fstep(ins)
                fstep(dve.bn_aggr(BAG[:, 0:2], BST[:]))
                dve.tensor_scalar(BAG[:, 2:3], BAG[:, 1:2], EPS, None, ALU.add).then_inc(v_ready, 1)
                dve.wait_ge(sdf_ready, i + 1)
                fstep(dve.reciprocal(BAG[:, 3:4], BAG[:, 3:4]))
                fstep(dve.tensor_scalar(z[:], z[:], BAG[:, 0:1], BAG[:, 3:4], ALU.subtract, ALU.mult))
                fstep(dve.tensor_tensor(z[:], z[:], LNR[:, 0, :], ALU.mult))
                dve.tensor_tensor(z[:], z[:], LNR[:, 1, :], ALU.add).then_inc(out_ready, 1)

        @block.tensor
        def _(pe):
            t = Turns()

            def three(outp, wh, wl, ah, al, first, last):
                pe.matmul(outp, wh, ah, start=first, stop=False, skip_group_check=True)
                pe.matmul(outp, wh, al, start=False, stop=False, skip_group_check=True)
                return pe.matmul(outp, wl, ah, start=False, stop=last, skip_group_check=True)

            def ready(r, h):
                pe.wait_ge(hi_ready[h], t.n(("hs", h)))
                pe.wait_ge(raw_used[r], t.n(("raw", r)) + 1)

            def mod_unit(r):
                pe.wait_ge(raw_loaded[r], t.n(("raw", r)) * 16)
                pe.wait_ge(mod_free, t.n("mod"))
                w = raw8(r)
                for c in range(2):
                    for k in range(KD):
                        ins = pe.matmul(PS[:, 7, 2 * c:2 * c + 2], w[:, k, c * P:(c + 1) * P], SILC[:, k, :],
                                        start=(k == 0), stop=(k == KD - 1), skip_group_check=True)
                ins.then_inc(mod_full, 1)

            def pair(p):
                pe.wait_ge(pair_free[p], t.n(("pair", p)))

            def unit_k(r, h, outs, ah=AH, al=AL, k_tiles=KD, cols=P):
                hi = HI[h][:].rearrange("p (k n) -> p k n", k=KD)
                lo = LO[h][:].rearrange("p (k n) -> p k n", k=KD)
                for c, outp in enumerate(outs):
                    for k in range(KD):
                        ins = three(outp, hi[:, k, c * P:(c + 1) * P], lo[:, k, c * P:(c + 1) * P],
                                    ah[:, k, :], al[:, k, :], k == 0, k == KD - 1)
                ins.then_inc(unit_done[h], 1)

            pe.wait_ge(silc_ready, 1)
            per = {("raw", r): 1 for r in range(4)}
            per.update({"mod": 4})
            with t.loop(pe, 2, per) as i:
                for r in range(4):
                    mod_unit(r)
            pe.wait_ge(cxl_ready, KD)
            pe.wait_ge(al_ready, KD)

            def stats(stage):
                pe.wait_ge(stats_in, stage)
                pe.wait_ge(mod_free, t.n("mod"))
                pe.matmul(PS[:, 6, :], mean_w, ZS[:], start=True, stop=True)
                pe.matmul(PS[:, 7, :], mean_w, QS[:], start=True, stop=True).then_inc(stats_full, 1)

            fl_n = 0
            al_n = KD
            for name, count, body in SEGMENTS[1:]:
                pos = positions(body)
                svs = [p for p in pos if p[0] == "s"]
                ns = len(svs)
                nm = body.count("m")
                rper = dict(ring_per(body))
                rper = {k: v for k, v in rper.items() if k[0] != "ud"}
                if nm:
                    rper.update({"mod": nm})
                if name == "kv":
                    for kind, r, h, j in pos:
                        if kind == "m":
                            mod_unit(r)
                            continue
                        ready(r, h)
                        hi = HI[h][:].rearrange("p (k n) -> p k n", k=KD)
                        lo = LO[h][:].rearrange("p (k n) -> p k n", k=KD)
                        if j == 0:
                            pair(0)
                            pair(1)
                            for c in range(2):
                                for k in range(KD):
                                    three(PS[:, 2, c * CTX:(c + 1) * CTX], hi[:, k, c * P:(c + 1) * P],
                                          lo[:, k, c * P:(c + 1) * P], CXH[:, k, :], CXL[:, k, :], k == 0, k == KD - 1)
                            unit_k(r, h, [PS[:, 0, :], PS[:, 1, :]])
                        else:
                            pair(2)
                            for m in range(6):
                                bank, col = 3 + m // 2, (m % 2) * 256
                                ah, al = (CXH, CXL) if m < 2 else (AH, AL)
                                o_ = (m % 2) * P if m < 2 else (m - 2) * P
                                for k in range(KD):
                                    ins = three(PS[:, bank, col:col + 256], ah[:, k, o_:o_ + P], al[:, k, o_:o_ + P],
                                                hi[:, k, :], lo[:, k, :], k == 0, k == KD - 1)
                            ins.then_inc(unit_done[h], 1)
                elif name == "q":
                    rper.update({("pair", 0): 1, ("pair", 1): 1})
                    with t.loop(pe, count, rper) as i:
                        for kind, r, h, j in pos:
                            if kind == "m":
                                mod_unit(r)
                                continue
                            ready(r, h)
                            pair(j)
                            unit_k(r, h, [PS[:, 2 * j, :], PS[:, 2 * j + 1, :]])
                    attention_pe(pe, t, three)
                elif name[:2] == "up":
                    rper.update({("pair", 0): ns // 2, ("pair", 1): ns // 2})
                    with t.loop(pe, count, rper) as i:
                        for kind, r, h, j in pos:
                            if kind == "m":
                                mod_unit(r)
                                continue
                            ready(r, h)
                            pair(j % 2)
                            hi = HI[h][:].rearrange("p (g k n) -> p g k n", g=2, k=KD)
                            lo = LO[h][:].rearrange("p (g k n) -> p g k n", g=2, k=KD)
                            for c in range(2):
                                for k in range(KD):
                                    ins = three(PS[:, 2 * (j % 2) + c, :], hi[:, c, k, :], lo[:, c, k, :],
                                                AH[:, k, :], AL[:, k, :], k == 0, k == KD - 1)
                            ins.then_inc(unit_done[h], 1)
                    fl_n += count * ns
                elif name == "dn1":
                    pe.wait_ge(fl_ready, fl_n)
                    nk = FF_PARTS[1]
                    for _, r, h, j in svs:
                        ready(r, h)
                        hi = HI[h][:].rearrange("p (a n) -> p a n", n=P)
                        lo = LO[h][:].rearrange("p (a n) -> p a n", n=P)
                        for a in range(16):
                            d, k = divmod(16 * j + a, nk)
                            if k == 0 and d % 2 == 0:
                                pair((d // 2) % 2)
                            ins = three(PS[:, d % 4, :], hi[:, a, :], lo[:, a, :], FH[:, k, :], FL[:, k, :],
                                        k == 0, k == nk - 1)
                        ins.then_inc(unit_done[h], 1)
                elif name == "conv":
                    pe.wait_ge(al_ready, 3 * KD)
                    rper.update({("pair", 0): 1, ("pair", 1): 1, ("pair", 2): 1})
                    with t.loop(pe, count, rper) as i:
                        for kind, r, h, j in pos:
                            ready(r, h)
                            pair(j)
                            unit_k(r, h, [PS[:, 2 * j, :], PS[:, 2 * j + 1, :]])
                    fl_n += 1
                else:
                    a_, l_ = (AH, AL) if name == "o" else (FH, FL)
                    if name == "o":
                        pe.wait_ge(ol_ready, NBLK)
                    else:
                        pe.wait_ge(fl_ready, fl_n)
                    for _, r, h, j in svs:
                        ready(r, h)
                        pair(j % 2)
                        unit_k(r, h, [PS[:, 2 * (j % 2), :], PS[:, 2 * (j % 2) + 1, :]], a_, l_)
                if name in ("o", "dn2", "co"):
                    stats({"o": 1, "dn2": 2, "co": 3}[name])
                if name == "o":
                    pe.wait_ge(al_ready, 2 * KD)

            pe.wait_ge(tmp_ready, 3 * KD + 1)
            pair(0)
            for i in range(4):
                for k in range(KD):
                    ins = pe.matmul(PS[:, 0, 8 * i:8 * i + 8], HF[:, k, i * P:(i + 1) * P], wr[:, k, :],
                                    start=(k == 0), stop=(k == KD - 1), skip_group_check=True)
            ins.then_inc(lg_full, 1)

            def rows(i):
                if i >= 2:
                    pe.wait_ge(tr_free, i - 1)
                else:
                    pair(1 + i)
                src = HF if i < 4 else XZ
                for k in range(KD):
                    ins = pe.transpose(PS[:, 2 + 2 * (i % 2) + k // 4, (k % 4) * P:(k % 4 + 1) * P],
                                       src[:, k, (i % 4) * P:(i % 4 + 1) * P], ident)
                ins.then_inc(tr_full, 1)

            for i in range(4):
                rows(i)
            pe.wait_ge(rc_in, 16)
            pe.wait_ge(mask_ready, 1)
            pair(0)
            for i in range(4):
                for j in range(i + 1):
                    pe.matmul(PS[:, 0, 8 * i:8 * i + 8], ones if j < i else upper, MM[:, j, :], start=(j == 0),
                              stop=(j == i), skip_group_check=True)
            for j in range(4):
                ins = pe.matmul(PS[:, 0, 32:40], ones, MM[:, j, :], start=(j == 0), stop=(j == 3),
                                skip_group_check=True)
            ins.then_inc(pos_full, 1)
            for i in range(4, 8):
                rows(i)
            pe.wait_ge(routed, 1)

            per_g = {k: v for k, v in PER_EXP_RING.items() if k[0] != "ud"}
            per_g.update({("pair", 0): 1, ("pair", 1): 1, "hl": 2})

            def expert_groups(n, r):
                with t.loop(pe, GROUPS, per_g) as g:
                    for j, (rs_, h) in enumerate(MOE_BODY):
                        ready(rs_, h)
                        if j < 4:
                            if j == 0:
                                pair(0)
                                pair(1)
                            hi = HI[h][:].rearrange("p (k n) -> p k n", k=KD)
                            lo = LO[h][:].rearrange("p (k n) -> p k n", k=KD)
                            for c in range(2):
                                for k in range(KD):
                                    ins = three(PS[:, j, c * CAP:c * CAP + n], hi[:, k, c * P:(c + 1) * P],
                                                lo[:, k, c * P:(c + 1) * P], XTH[:, k, 0:n], XTL[:, k, 0:n],
                                                k == 0, k == KD - 1)
                        else:
                            q = j - 4
                            pe.wait_ge(hl_ready, t.n("hl"))
                            if j == 4:
                                pe.wait_ge(y_zero, r)
                            hi = HI[h][:].rearrange("p (k d n) -> p k d n", k=2, n=P)
                            lo = LO[h][:].rearrange("p (k d n) -> p k d n", k=2, n=P)
                            for k in range(2):
                                for d in range(KD):
                                    ins = three(PS[:, 4 + d // 2, (d % 2) * CAP:(d % 2) * CAP + n], hi[:, k, d, :],
                                                lo[:, k, d, :], HH[:, q, k, 0:n], HL[:, q, k, 0:n], False, True)
                        ins.then_inc(unit_done[h], 1)

            def expert_round(r, count):
                pe.wait_ge(xg_in, r * 16)
                pair(0)
                pair(1)
                for k in range(KD):
                    for s in range(2):
                        ins = pe.transpose(PS[:, k // 2, (k % 2) * CAP + s * P:(k % 2) * CAP + (s + 1) * P],
                                           XG[:, s, k * P:(k + 1) * P], ident)
                ins.then_inc(xt_full, 1)
                if count is None:
                    expert_groups(CAP, r)
                else:
                    saved = dict(t.at)
                    for below, n in zip((None,) + WIDTHS[:-1], WIDTHS):
                        t.at = dict(saved)
                        if below is None:
                            with pe.If(count < n + 1):
                                expert_groups(n, r)
                        elif n == CAP:
                            with pe.If(count > below):
                                expert_groups(n, r)
                        else:
                            with pe.If(count > below):
                                with pe.If(count < n + 1):
                                    expert_groups(n, r)
                pair(0)
                pair(1)
                pe.wait_ge(yt_a, r)
                pe.wait_ge(yt_b, r)
                for s in range(2):
                    for d in range(KD):
                        ins = pe.transpose(PS[:, 2 * s + d // 4, (d % 4) * P:(d % 4 + 1) * P],
                                           YT[:, d, s * P:(s + 1) * P], ident)
                ins.then_inc(yrow_full, 1)

            per_e = times(per_g, GROUPS)
            per_e[("pair", 0)] += 2
            per_e[("pair", 1)] += 2
            with t.loop(pe, NE, per_e) as e:
                cnt = pe.value_load(RI[0:1, bass.ds(e, 1)], min_val=0, max_val=T)
                expert_round(e + 1, cnt)
            n_over = pe.value_load(RI[0:1, 11:12], min_val=0, max_val=MAX_OVER)
            with pe.If(n_over > 0):
                with t.loop(pe, n_over, per_e) as x:
                    expert_round(x + (NE + 1), None)

            pe.wait_ge(dg_ready, 1)
            for k in range(KD):
                ins = pe.matmul(PS[:, k // 4, (k % 4) * P:(k % 4 + 1) * P], mean_w, DG[:, k, :], start=True, stop=True,
                                skip_group_check=True)
            ins.then_inc(g2_full, 1)



def kernel(**inputs):
    import numpy as np
    import concourse.bacc as _bacc
    from concourse.bass_utils import run_bass_kernel_spmd as _run

    f = np.float32
    a = {k: np.asarray(v) for k, v in inputs.items()}

    def cols(w):
        return w.reshape(KD, P, -1, 256).transpose(2, 1, 0, 3).reshape(-1, P, UNIT)

    order = [8 * kp + 4 * h + g for kp in range(2) for g in range(4) for h in range(2)]
    feat = np.concatenate([np.arange(h * HD, (h + 1) * HD) for h in order])
    mods = np.concatenate([cols(a["w_mod"][0]), cols(a["w_mod"][1])])
    wqkv = a["attn_w_qkv"][0]
    split = {
        "kv": cols(wqkv[:, D:]), "q": cols(wqkv[:, :D][:, feat]), "o": cols(a["attn_w_o"][0][feat]),
        "co": cols(a["conv_w_out"][0]),
        "conv": cols(a["conv_w_in"][0]).reshape(3, 4, P, UNIT)[[1, 2, 0]].transpose(1, 0, 2, 3).reshape(12, P, UNIT),
    }
    w1 = a["ffn_w1"][0].reshape(KD, P, FF // P, P).transpose(2, 1, 0, 3)
    w3 = a["ffn_w3"][0].reshape(KD, P, FF // P, P).transpose(2, 1, 0, 3)
    up = np.stack([w1, w3], axis=2).reshape(FF // P, P, UNIT)
    t0 = 0
    for i, n in enumerate(FF_PARTS):
        split[f"up{i}"] = up[t0:t0 + n]
        w2 = a["ffn_w2"][0][t0 * P:(t0 + n) * P]
        if n == KD:
            split[f"dn{i}"] = cols(w2)
        else:
            split[f"dn{i}"] = w2.reshape(n, P, KD, P).transpose(1, 2, 0, 3).reshape(P, -1, UNIT).transpose(1, 0, 2)
        t0 += n
    w_pre = np.empty((N_PRE, P, UNIT), f)
    u = m = 0
    for name, count, body in SEGMENTS:
        k = 0
        for _ in range(count):
            for kind in body:
                if kind == "s":
                    w_pre[u] = split[name][k]
                    k += 1
                else:
                    w_pre[u] = mods[m]
                    m += 1
                u += 1
    w_moe = np.empty((NE, GROUPS, 6, P, UNIT), f)
    e1 = a["moe_w1"][0].reshape(NE, KD, P, GROUPS, 2, 256)
    e3 = a["moe_w3"][0].reshape(NE, KD, P, GROUPS, 2, 256)
    e2 = a["moe_w2"][0].reshape(NE, GROUPS, 2, 2, P, D)
    for q in range(2):
        w_moe[:, :, 2 * q] = e1[:, :, :, :, q].transpose(0, 3, 2, 1, 4).reshape(NE, GROUPS, P, UNIT)
        w_moe[:, :, 2 * q + 1] = e3[:, :, :, :, q].transpose(0, 3, 2, 1, 4).reshape(NE, GROUPS, P, UNIT)
        w_moe[:, :, 4 + q] = e2[:, :, q].transpose(0, 1, 3, 2, 4).reshape(NE, GROUPS, P, UNIT)
    w_moe = w_moe.reshape(NE * GROUPS * 6, P, UNIT)

    small = np.zeros((P, N_SM), f)

    def put(name, v):
        lo, hi = SM[name]
        small[:, lo:hi] = v.reshape(P, hi - lo)

    put("cc", np.stack([a["c"][0].reshape(KD, P).T, a["c_ctx"].reshape(KD, P).T], axis=2))
    bm = a["b_mod"].reshape(96, P).T
    put("bmod", np.stack([bm, bm], axis=1))
    put("lng", a["ln_g"].reshape(4 * KD, P).T)
    put("lnb", a["ln_b"].reshape(4 * KD, P).T)
    put("ident", np.eye(P, dtype=f))
    put("mean", np.full((P, P), 1.0 / D, f))
    put("sink", np.broadcast_to(a["attn_sink"][0][order], (P, NH)))
    put("cw", a["conv_w"][0].reshape(3 * KD, P).T)
    put("wr", a["moe_router"][0].reshape(KD, P, NE).transpose(1, 0, 2))

    inv = (10000.0 ** (-np.arange(0, HD // 2, 2, dtype=f) / f(HD // 2))).astype(f)
    pos = np.arange(T)
    ar, ac = (pos // 64).astype(f)[:, None] * inv, (pos % 64).astype(f)[:, None] * inv
    ang = np.concatenate([ar, ar, ac, ac], axis=-1).T
    sign = np.where(np.arange(HD) % 32 < 16, -1.0, 1.0).astype(f)[:, None]
    rope = np.concatenate([np.tile(np.cos(ang), (2, 1)), np.tile(np.sin(ang) * sign, (2, 1))], axis=1).astype(f)
    qi, kj = np.arange(P)[:, None], np.arange(P)[None, :]
    mask = np.zeros((P, NBLK, 2, P), f)
    mask[:, :, 0][np.broadcast_to((kj < qi)[:, None], (P, NBLK, P))] = MASKED
    mask[:, :, 1][np.broadcast_to((kj > qi)[:, None], (P, NBLK, P))] = MASKED
    mask[:, 0, 0] = MASKED
    mask[:, NBLK - 1, 1] = MASKED
    rconst = np.zeros((P, N_RC), f)
    rconst[:, 0:P] = 1.0
    rconst[:, P:2 * P] = (qi < kj)
    rconst[:, 256:264] = np.arange(NE)
    rconst[:, 264:272] = np.arange(NE) * CAP
    lnrow = np.broadcast_to(np.concatenate([a["ln_g"][1, 1], a["ln_b"][1, 1]]), (P, 2 * D))

    arrays = {
        "small": small, "x_t": a["x"][0].T.reshape(KD, P, T).transpose(1, 0, 2),
        "ctx_t": a["ctx"][0].T.reshape(KD, P, CTX).transpose(1, 0, 2), "rope": rope,
        "mask": mask.reshape(P, NBLK, 2 * P), "rconst": rconst, "lnrow": lnrow, "w_pre": w_pre, "w_moe": w_moe,
    }
    arrays = {k: np.ascontiguousarray(v) for k, v in arrays.items()}
    nc = _bacc.Bacc("TRN2", target_bir_lowering=False, num_devices=1)
    args = [nc.dram_tensor(k, v.shape, F32, kind="ExternalInput").ap() for k, v in arrays.items()]
    args.append(nc.dram_tensor("out", (1, T, D), F32, kind="ExternalOutput").ap())
    program(nc, *args)
    r = _run(nc, [arrays], core_ids=[0])
    return r.results[0]["out"]
```

```python
from contextlib import ExitStack, contextmanager

import concourse.bass as bass
from concourse import mybir

F32 = mybir.dt.float32
F32R = mybir.dt.float32r
I32 = mybir.dt.int32
U32 = mybir.dt.uint32
ALU = mybir.AluOpType
ACT = mybir.ActivationFunctionType
AX = mybir.AxisListType

P = 128
D = 1024
KD = D // P
T = 512
CTX = 256
HD = 64
NH = 16
NKV = 4
FF = 2816
NE = 8
FE = 3584
UNIT = 2048
BLK = 128
NBLK = T // BLK
WIN = 3 * BLK
NKEY = CTX + WIN
FF_PARTS = (8, 6, 8)
GROUPS = FE // 512
CAP = 256
MAX_OVER = 2 * T // (CAP + 1)
N_ROWS = (NE + MAX_OVER) * CAP
ALPHA = 4 ** 0.25
EPS = 1e-5
SCALE = HD ** -0.5
MASKED = -1e30
DOWN6 = ([0, 1], [2, 3, 4], [5, 6, 7])
ATT_STEPS = 3 * NH

SEGMENTS = [
    ("modA", 2, "mmmm"), ("kv", 1, "smmsmm"), ("q", 2, "smmsmm"), ("o", 1, "ssss"),
    ("up0", 4, "smmsmm"), ("dn0", 1, "ssss"), ("up1", 3, "smmsmm"), ("dn1", 1, "sss"),
    ("up2", 2, "ssss"), ("dn2", 1, "ssss"), ("conv", 4, "sss"), ("co", 1, "ssss"),
]
N_PRE = sum(n * len(b) for _, n, b in SEGMENTS)
RSLOT = {"smmsmm": (0, 1, 2, 3, 1, 2), "ssss": (0, 1, 2, 3), "sss": (0, 1, 2), "mmmm": (0, 1, 2, 3)}
HSLOT = {"smmsmm": (0, 1), "ssss": (0, 1, 2, 1), "sss": (0, 1, 2), "mmmm": ()}

SM = {}
_o = 0
for _n, _w in (("cc", 16), ("bmod", 192), ("lng", 32), ("lnb", 32), ("ident", 128), ("mean", 128), ("sink", 16),
               ("cw", 24), ("wr", 64)):
    SM[_n] = (_o, _o + _w)
    _o += _w
N_SM = _o
RC = {"ones": (0, 128), "upper": (128, 256), "iota": (256, 264), "base": (264, 272)}
N_RC = 272


class Turns:

    def __init__(self):
        self.at, self.levels = {}, []

    def n(self, key):
        v = self.at.get(key, 0) + 1
        self.at[key] = v
        for i, per in self.levels:
            if per.get(key):
                v = i * per[key] + v
        return v

    def skip(self, key, k):
        self.at[key] = self.at.get(key, 0) + k

    def last(self, key):
        self.skip(key, -1)
        return self.n(key)

    @contextmanager
    def loop(self, eng, count, per, start=0):
        before = dict(self.at)
        with eng.Fori(start, start + count) if isinstance(count, int) else eng.Fori(0, count) as i:
            self.levels.append((i - start if start else i, per))
            yield i
            self.levels.pop()
        for key in set(per) | set(self.at):
            did = self.at.get(key, 0) - before.get(key, 0)
            assert did == per.get(key, 0), (key, did, per.get(key, 0))
            if isinstance(count, int):
                self.at[key] = before.get(key, 0) + count * did


def positions(body):
    out, s, m = [], 0, 0
    for kind, r in zip(body, RSLOT[body]):
        if kind == "s":
            out.append((kind, r, HSLOT[body][s], s))
            s += 1
        else:
            out.append((kind, r, None, m))
            m += 1
    return out


def program(nc, small, xT_in, ctxT_in, rope, maskin, rconst, lnrow, w_pre, w_moe, out):
    with ExitStack() as ctx:
        def sem(name):
            return ctx.enter_context(nc.semaphore(name))

        base = 16512
        limit = 229344
        cur = [base]

        def put(name, shape, dt, at=None):
            size = 4
            for s in shape[1:]:
                size *= s
            off = cur[0] if at is None else at
            t = nc.alloc_sbuf_tensor_at(name, shape, dt, offset=off)
            if at is None:
                cur[0] += size
                assert cur[0] <= limit, (name, cur[0])
            else:
                assert at + size <= limit, (name, at + size)
            return t

        RAW = [put(f"raw{i}", [P, UNIT], F32) for i in range(4)]
        o_hi = cur[0]
        HI = [put(f"hi{i}", [P, UNIT], F32R) for i in range(3)]
        o_lo = cur[0]
        LO = [put(f"lo{i}", [P, UNIT], F32R) for i in range(3)]
        o_xz = cur[0]
        XZ = put("xz", [P, KD, T], F32)
        o_ah = cur[0]
        AH = put("ah", [P, KD, T], F32R)
        o_al = cur[0]
        AL = put("al", [P, KD, T], F32R)
        SMALL = put("small", [P, N_SM], F32)
        MOD = put("mod", [P, 2, 2 * 48], F32)
        COEF = put("coef", [P, 4, 4, KD], F32)
        CG = put("cg", [P, KD], F32)
        SILC = put("silc", [P, KD, 2], F32)
        IDR = put("idr", [P, P], F32R)
        NRM = put("nrm", [P, NH], F32)
        NM = put("nm", [P, NH], F32)
        LSUM = put("lsum", [P, NH], F32)
        ES = put("es", [P, NH], F32)
        RS = put("rs", [P, NH], F32)
        NSINK = put("nsink", [P, NH], F32)
        CWG = put("cwg", [P, 3, 2], F32)
        cur[0] = (cur[0] + 31) // 32 * 32
        r2 = cur[0]
        Q = put("q", [P, KD, T], F32, r2)
        CX = put("cx", [P, KD, CTX], F32, r2)
        K = put("k", [P, 2, T + 2 * BLK], F32, r2 + 16384)
        VH = put("vh", [P, NBLK + 2, 256], F32R, r2 + 22528)
        VL = put("vl", [P, NBLK + 2, 256], F32R, r2 + 28672)
        KCH = put("kch", [P, 2, CTX], F32R, r2 + 34816)
        KCL = put("kcl", [P, 2, CTX], F32R, r2 + 36864)
        VCH = put("vch", [P, 2, 256], F32R, r2 + 38912)
        VCL = put("vcl", [P, 2, 256], F32R, r2 + 40960)
        MASK = put("mask", [P, NBLK, 2 * BLK], F32R, r2 + 43008)
        o = r2 + 47104
        CXH = put("cxh", [P, KD, CTX], F32R, o)
        CXL = put("cxl", [P, KD, CTX], F32R, o + 8192)
        COS = put("cos", [P, T], F32, o + 16384)
        SIN = put("sin", [P, T], F32, o + 18432)
        ROT = put("rot", [P, T], F32, o + 20480)
        MASKF = put("maskf", [P, NBLK, 2 * BLK], F32, o)
        QSH = put("qsh", [P, KD, BLK], F32R, o)
        QSL = put("qsl", [P, KD, BLK], F32R, o + 4096)
        KSH = put("ksh", [P, 2, WIN], F32R, o + 8192)
        KSL = put("ksl", [P, 2, WIN], F32R, o + 11264)
        VSH = put("vsh", [P, 3, 256], F32R, o + 14336)
        VSL = put("vsl", [P, 3, 256], F32R, o + 17408)
        PR = [put(f"pr{i}", [P, NKEY], F32, o + 20480 + 2560 * i) for i in range(3)]
        PTH = [put(f"pth{i}", [P, 5, 2, BLK], F32R, o_hi + 8192 * (i + 1)) for i in range(2)]
        PTL = [put(f"ptl{i}", [P, 5, 2, BLK], F32R, o_lo + 8192 * (i + 1)) for i in range(2)]
        FH = put("fh", [P, KD, T], F32R, r2)
        FL = put("fl", [P, KD, T], F32R, r2 + 16384)
        SG = [put(f"sg{i}", [P, T], F32, r2 + 32768 + 2048 * i) for i in range(2)]
        CS = put("cs", [P, 2, T], F32, r2 + 32768)
        UP = put("up", [P, 2, T + 2], F32, r2 + 36864)
        YC = put("yc", [P, 2, T], F32, r2 + 40992)
        o = limit // 32 * 32 - 18432
        ZS = put("zs", [P, T], F32, o)
        QS = put("qs", [P, T], F32, o + 2048)
        M2 = put("m2", [P, T], F32, o + 4096)
        VAR = put("var", [P, T], F32, o + 6144)
        RSTD = put("rstd", [P, T], F32, o + 8192)
        SQ = [put(f"sq{i}", [P, T], F32, o + 10240 + 2048 * i) for i in range(2)]
        TMP = [put(f"tmp{i}", [P, T], F32, o + 14336 + 2048 * i) for i in range(2)]
        TM2 = put("tm2", [P, 2, T], F32, o + 14336)
        assert r2 + 47104 + 28672 <= limit and r2 + 45152 <= o
        HF = put("hf", [P, KD, T], F32, o_ah)
        HT = put("ht", [P, 4, D], F32, o_al)
        XTH = put("xth", [P, KD, CAP], F32R, o_xz)
        XTL = put("xtl", [P, KD, CAP], F32R, o_xz + 8192)
        XR = put("xr", [P, 4, D], F32, r2)
        RAW += [put(f"raw{i}", [P, UNIT], F32, r2 + 16384 + 8192 * (i - 4)) for i in (4, 5)]
        XG = put("xg", [P, 2, D], F32, r2 + 32768)
        HH = put("hh", [P, 2, 2, CAP], F32R, r2 + 40960)
        HL = put("hl", [P, 2, 2, CAP], F32R, r2 + 45056)
        SE = put("se", [P, 2, 2 * CAP], F32, r2 + 49152)
        HE = put("he", [P, 2, 2 * CAP], F32, r2 + 53248)
        RT = put("rt", [P, N_RC], F32, r2 + 45568)
        ZT = put("zt", [P, D], F32, r2 + 47104)
        o = r2 + 65536
        LG = put("lg", [P, 4, NE], F32, o + 1088)
        MX = put("mx", [P, 4, 8], F32, o + 1216)
        IX = put("ix", [P, 4, 8], U32, o + 1344)
        IXF = put("ixf", [P, 4, 2], F32, o + 1472)
        OH = put("oh", [P, 2, 4, NE], F32, o + 1504)
        MM = put("mm", [P, 4, NE], F32, o + 1760)
        DD = put("dd", [P, 4, 4], F32, o + 1888)
        PB = put("pb", [P, 4, NE], F32, o + 1952)
        PT1 = put("pt1", [P, 4, NE], F32, o + 2080)
        DF = put("df", [P, 2, 4], F32, o + 2208)
        RF = put("rf", [P, 16], F32, o + 2240)
        OV = put("ov", [P, 3, NE], F32, o + 2304)
        ADJ = put("adj", [P, NE], F32, o + 2400)
        YS = put("ys", [P, 2, D], F32, o_al)
        o = r2 + 68000 // 32 * 32
        DI = put("di", [P, 2, 4], U32, o)
        GA = put("ga", [P, 2, 4], F32, o + 32)
        RI = put("ri", [P, 16], I32, o + 64)
        assert o + 128 <= limit
        LNR = put("lnr", [P, 2, D], F32, base)
        G2R = put("g2r", [P, D], F32, base + 8192)
        DG = put("dg", [P, KD, P], F32, base + 12288)
        YG = [[put(f"yg{i}{c}", [P, D], F32, base + 16384 + 8192 * i + 4096 * c) for c in range(2)] for i in range(2)]
        ZF = [put(f"zf{i}", [P, D], F32, base + 32768 + 4096 * i) for i in range(4)]
        BST = put("bst", [P, 2, 6], F32, base + 49152)
        BAG = put("bag", [P, 4], F32, base + 49280)

        PS = ctx.enter_context(nc.psum_tensor("ps", [P, 8, 512], F32))

        xg_d = nc.dram_tensor("dispatched_x", [N_ROWS, D], F32).ap()
        yg_d = nc.dram_tensor("expert_y", [N_ROWS, D], F32).ap()

        small_in, xin, cxin, rope_in, mask_in, rc_in, lnr_in = map(sem, (
            "small_in", "x_in", "ctx_in", "rope_in", "mask_in", "routing_const_in", "lnrow_in"))
        raw_loaded = [sem(f"raw_loaded{i}") for i in range(6)]
        raw_used = [sem(f"raw_used{i}") for i in range(6)]
        hi_ready = [sem(f"hi_ready{i}") for i in range(3)]
        unit_done = [sem(f"unit_done{i}") for i in range(3)]
        pair_free = [sem(f"pair_free{i}") for i in range(3)]
        mod_full = sem("mod_full")
        mod_free = sem("mod_free")
        dve_step, act_step = sem("dve_step"), sem("act_step")
        silc_ready, idr_ready, pads_ready = map(sem, ("silc_ready", "idr_ready", "pads_ready"))
        tmp_ready, ah_ready, al_ready = map(sem, ("tmp_ready", "ah_ready", "al_ready"))
        ctx_tmp, cxh_ready, cxl_ready = map(sem, ("ctx_tmp", "cxh_ready", "cxl_ready"))
        kvh_ready, kvl_ready, rope_done = map(sem, ("kvh_ready", "kvl_ready", "rope_done"))
        st_h, st_l = sem("staged_hi"), sem("staged_lo")
        s_full = [sem(f"scores_full{i}") for i in range(2)]
        nm_ready = sem("max_ready")
        p_ready = [sem(f"probs_ready{i}") for i in range(2)]
        pt_full, pth_ready, ptl_ready, av_done = map(sem, ("pt_full", "pth_ready", "ptl_ready", "av_done"))
        es_ready, pr_ready, oh_ready, ol_ready = map(sem, ("es_ready", "pr_ready", "oh_ready", "ol_ready"))
        z_ready, sq_ready, stats_in, stats_full, m2_ready, var_ready, sd_ready = map(sem, (
            "z_ready", "sq_ready", "stats_in", "stats_full", "m2_ready", "var_ready", "sd_ready"))
        sg_ready, f_ready, fh_ready, fl_ready = map(sem, ("silu_ready", "f_ready", "fh_ready", "fl_ready"))
        cs_ready, yc_ready = sem("cs_ready"), sem("yc_ready")
        lg_full, mask_ready, pos_full, gate_in, gate_exp = map(sem, (
            "logits_full", "choice_ready", "pos_full", "gate_in", "gate_exp"))
        tr_full, tr_free = sem("rows_full"), sem("rows_free")
        dest_ready, routed = sem("dest_ready"), sem("routed")
        zero_ready, zeroed, scattered = sem("zero_ready"), sem("zeroed"), sem("scattered")
        ht_full, pe_turn = sem("ht_full"), sem("pe_turn")
        xg_in, xt_full, xth_ready, xtl_ready = map(sem, ("xg_in", "xt_full", "xth_ready", "xtl_ready"))
        se_ready, he_ready, hh_ready, hl_ready = map(sem, ("se_ready", "he_ready", "hh_ready", "hl_ready"))
        y_zero, ys_a, ys_b, ys_free, y_out = map(sem, ("y_zero", "ys_a", "ys_b", "ys_free", "y_out"))
        y_done, pool_turn = sem("expert_y_done"), sem("pool_turn")
        dg_ready, g2_full, g2_ready = sem("dg_ready"), sem("g2_full"), sem("g2_ready")
        yg_in = [sem(f"yg_in{i}") for i in range(2)]
        yg_free = sem("yg_free")
        v_ready, sdf_ready, out_ready, out_done = map(sem, ("v_ready", "sdf_ready", "out_ready", "out_done"))

        def sm(name):
            a, b = SM[name]
            return SMALL[:, a:b]

        ident = sm("ident")
        mean_w = sm("mean")
        bmod = sm("bmod").rearrange("p (v t) -> p v t", v=2)
        lng = sm("lng").rearrange("p (s k) -> p s k", s=4)
        lnb = sm("lnb").rearrange("p (s k) -> p s k", s=4)
        cw = sm("cw").rearrange("p (j k) -> p j k", j=3)
        wr = sm("wr").rearrange("p (k e) -> p k e", k=KD)
        ones = RT[:, 0:P]
        upper = RT[:, P:2 * P]

        def scores_view(b):
            return PS[:, 2 * b:2 * b + 2, :].rearrange("p b n -> p (b n)")[:, 512 - CTX:512 + WIN]

        def raw8(s):
            return RAW[s][:].rearrange("p (k n) -> p k n", k=KD)

        def modcol(layer, chunk):
            a = layer * 48 + chunk * 8
            return MOD[:, 0, a:a + 8]

        def ring_per(body):
            per = {}
            for kind, r, h, _ in positions(body):
                per[("raw", r)] = per.get(("raw", r), 0) + 1
                if kind == "s":
                    per[("hs", h)] = per.get(("hs", h), 0) + 1
                    per[("ud", h)] = per.get(("ud", h), 0) + 1
            return per

        MOE_BODY = [(p, p % 3) for p in range(6)]
        PER_EXP_RING = {}
        for r_, h_ in MOE_BODY:
            PER_EXP_RING[("raw", r_)] = PER_EXP_RING.get(("raw", r_), 0) + 1
            PER_EXP_RING[("hs", h_)] = PER_EXP_RING.get(("hs", h_), 0) + 1
            PER_EXP_RING[("ud", h_)] = PER_EXP_RING.get(("ud", h_), 0) + 1

        def times(per, n):
            return {k: v * n for k, v in per.items()}

        def plus_ahead(per):
            per = dict(per)
            for r, h in MOE_BODY[:2]:
                for key in (("raw", r), ("hs", h), ("ud", h)):
                    if key in per:
                        per[key] += 1
            return per

        def pt_view():
            return PS[:, 4:6, :].rearrange("p b n -> p (b n)")[:, 0:NKEY].rearrange("p (c n) -> p c n", n=BLK)

        def out_view(g, f):
            return PS[HD * f:HD * f + HD, 6 + g % 2, :].rearrange("p (j f n) -> p j f n", j=2, f=2)[:, :, f, :]

        def attention_act(act):
            act.preload_act_table(ACT.Exp)
            with act.Fori(0, NBLK) as b:
                act.wait_ge(rope_done, 10)
                act.wait_ge(st_l, b + 1)
                act.activation(QSH[:], Q[:, :, bass.ds(b * BLK, BLK)], ACT.Copy).then_inc(st_h, 1)
                act.activation(KSH[:], K[:, :, bass.ds(b * BLK, WIN)], ACT.Copy).then_inc(st_h, 1)
                act.activation(VSH[:], VH[:, bass.ds(b, 3), :].bitcast(F32), ACT.Copy).then_inc(st_h, 1)
                for h in range(NH + 4):
                    if h < NH:
                        act.wait_ge(nm_ready, b * NH + (h + 1))
                        if h >= 3:
                            act.wait_ge(pt_full, b * NH + (h - 2))
                        act.activation(PR[h % 3][:], scores_view(h % 2), ACT.Exp, bias=NM[:, h:h + 1], scale=SCALE,
                                       accum_out=LSUM[:, h:h + 1]).then_inc(p_ready[h % 2], 1)
                        act.activation(ES[:, h:h + 1], NM[:, h:h + 1], ACT.Exp,
                                       bias=SMALL[:, SM["sink"][0] + h:SM["sink"][0] + h + 1]).then_inc(es_ready, 1)
                    if 2 <= h < NH + 2:
                        o = h - 2
                        act.wait_ge(pt_full, b * NH + (o + 1))
                        if o >= 4:
                            act.wait_ge(av_done, b * (NH // 2) + (o // 2 - 1))
                        act.activation(PTH[o // 2 % 2][:, :, o % 2, :], pt_view(), ACT.Copy).then_inc(pth_ready, 1)
                    if h % 4 == 3 and h >= 7:
                        g = h // 4 - 1
                        act.wait_ge(av_done, b * (NH // 2) + (2 * g + 2))
                        for f in range(2):
                            ins = act.activation(AH[HD * f:HD * f + HD, 2 * g:2 * g + 2, bass.ds(b * BLK, BLK)],
                                                 out_view(g, f), ACT.Copy)
                        ins.then_inc(oh_ready, 1)

        def attention_dve(dve, t):
            dve.sem_inc(st_l, 1)
            with t.loop(dve, NBLK, {"step": ATT_STEPS}) as b:
                dve.wait_ge(rope_done, 10)
                dve.wait_ge(st_h, b * 3 + 1)
                dve.tensor_tensor(QSL[:], Q[:, :, bass.ds(b * BLK, BLK)], QSH[:].bitcast(F32), ALU.subtract)
                dve.wait_ge(st_h, b * 3 + 2)
                dve.tensor_tensor(KSL[:], K[:, :, bass.ds(b * BLK, WIN)], KSH[:].bitcast(F32), ALU.subtract)
                dve.wait_ge(st_h, b * 3 + 3)
                dve.tensor_copy(VSL[:], VL[:, bass.ds(b, 3), :].bitcast(F32)).then_inc(kvl_ready, 1)

                def link(ins):
                    ins.then_inc(dve_step, 1)
                    dve.wait_ge(dve_step, t.n("step"))

                for h in range(NH + 5):
                    if h < NH:
                        dve.wait_ge(s_full[h % 2], b * (NH // 2) + (h // 2 + 1))
                        link(dve.tensor_reduce(NRM[:, h:h + 1], scores_view(h % 2), AX.X, ALU.max, negate=True))
                        dve.scalar_tensor_tensor(out=NM[:, h:h + 1], in0=NRM[:, h:h + 1], scalar=SCALE,
                                                 in1=NSINK[:, h:h + 1], op0=ALU.mult, op1=ALU.min).then_inc(nm_ready, 1)
                    if 1 <= h < NH + 1:
                        o = h - 1
                        dve.wait_ge(es_ready, b * NH + (o + 1))
                        link(dve.tensor_tensor(RS[:, o:o + 1], LSUM[:, o:o + 1], ES[:, o:o + 1], ALU.add))
                        link(dve.reciprocal(RS[:, o:o + 1], RS[:, o:o + 1]))
                        dve.tensor_scalar(PR[o % 3][:], PR[o % 3][:], RS[:, o:o + 1], None,
                                          ALU.mult).then_inc(pr_ready, 1)
                    if 2 <= h < NH + 2:
                        o = h - 2
                        dve.wait_ge(pth_ready, b * NH + (o + 1))
                        dve.tensor_tensor(PTL[o // 2 % 2][:, :, o % 2, :], pt_view(),
                                          PTH[o // 2 % 2][:, :, o % 2, :].bitcast(F32), ALU.subtract).then_inc(ptl_ready, 1)
                    if h % 4 == 0 and h >= 8:
                        g = h // 4 - 2
                        dve.wait_ge(oh_ready, b * 4 + (g + 1))
                        for f in range(2):
                            rows_ = slice(HD * f, HD * f + HD)
                            at = (rows_, slice(2 * g, 2 * g + 2), bass.ds(b * BLK, BLK))
                            ins = dve.tensor_tensor(AL[at], out_view(g, f), AH[at].bitcast(F32), ALU.subtract)
                        ins.then_inc(ol_ready, 1)
                dve.wait_ge(ol_ready, b * 4 + 4)
                dve.sem_inc(st_l, 1)

        def attention_pe(pe, three):
            pe.wait_ge(idr_ready, 2)
            with pe.Fori(0, NBLK) as b:
                pe.wait_ge(kvl_ready, b + 1)
                for h in range(NH + 4):
                    if h < NH:
                        f, j = h % 2, h // 2
                        kp = j // 4
                        rows_ = slice(HD * f, HD * f + HD)
                        if h >= 2:
                            pe.wait_ge(p_ready[f], b * (NH // 2) + h // 2)
                        wh, wl = QSH[rows_, j, :], QSL[rows_, j, :]
                        three(PS[:, 2 * f, 512 - CTX:512], wh, wl, KCH[rows_, kp, :], KCL[rows_, kp, :], True, True)
                        three(PS[:, 2 * f + 1, 0:WIN], wh, wl, KSH[rows_, kp, :], KSL[rows_, kp, :], True, False)
                        edge = PS[:, 2 * f + 1, 0:WIN].rearrange("p (c n) -> p c n", c=3)[:, 0:3:2, :]
                        pe.matmul(edge, IDR[:], MASK[:, bass.ds(b, 1), :].rearrange("p o (c n) -> p (o c) n", c=2),
                                  start=False, stop=True, skip_group_check=True).then_inc(s_full[f], 1)
                    if 2 <= h < NH + 2:
                        o = h - 2
                        pe.wait_ge(pr_ready, b * NH + (o + 1))
                        if o >= 1:
                            pe.wait_ge(ptl_ready, b * NH + o)
                        for c in range(5):
                            ins = pe.transpose(PS[:, 4 + c // 4, (c % 4) * P:(c % 4 + 1) * P],
                                               PR[o % 3][:, c * P:(c + 1) * P], ident)
                        ins.then_inc(pt_full, 1)
                    if h % 2 == 0 and h >= 4:
                        p = h // 2 - 2
                        pe.wait_ge(ptl_ready, b * NH + (2 * p + 2))
                        if p % 2 == 0 and p >= 4:
                            pe.wait_ge(ol_ready, b * 4 + (p // 2 - 1))
                        cols_ = slice((p // 4) * P, (p // 4) * P + P)
                        outp = PS[:, 6 + p // 2 % 2, (p % 2) * 256:(p % 2) * 256 + 256]
                        for c in range(5):
                            vh = VCH[:, c, cols_] if c < 2 else VSH[:, c - 2, cols_]
                            vl = VCL[:, c, cols_] if c < 2 else VSL[:, c - 2, cols_]
                            ins = three(outp, vh, vl, PTH[p % 2][:, c].rearrange("p f n -> p (f n)"),
                                        PTL[p % 2][:, c].rearrange("p f n -> p (f n)"), c == 0, c == 4)
                        ins.then_inc(av_done, 1)

        block = ctx.enter_context(nc.Block())

        @block.sync
        def _(sp):
            t = Turns()
            sp.dma_start(SMALL[:], small).then_inc(small_in, 16)

            def load(slot, src):
                sp.wait_ge(raw_used[slot], t.n(("raw", slot)))
                sp.dma_start(RAW[slot][:], src).then_inc(raw_loaded[slot], 16)

            u0 = 0
            for name, count, body in SEGMENTS:
                pos = positions(body)

                def emit(i):
                    for j, (_, r, _, _) in enumerate(pos):
                        load(r, w_pre[bass.ds(i * len(body) + (u0 + j), 1), :, :].rearrange("o p n -> (o p) n")
                             if not isinstance(i, int) else w_pre[u0 + j])
                if count > 1:
                    per = {k: v for k, v in ring_per(body).items() if k[0] == "raw"}
                    with t.loop(sp, count, per) as i:
                        emit(i)
                else:
                    emit(0)
                if name == "modA":
                    sp.dma_start(COS[:], rope[:, 0:T]).then_inc(rope_in, 16)
                    sp.dma_start(SIN[:], rope[:, T:2 * T]).then_inc(rope_in, 16)
                u0 += count * len(body)

            per_g = {("raw", r): 1 for r, _ in MOE_BODY}

            def unit(i):
                return w_moe[bass.ds(i, 1), :, :].rearrange("o p n -> (o p) n") if not isinstance(i, int) else w_moe[i]

            def group(first):
                for j in range(2, 8):
                    load(j % 6, unit(first + j))

            for j in range(4):
                load(j, unit(j))
            sp.wait_ge(routed, 1)
            for j in range(4, 8):
                load(j % 6, unit(j))
            with t.loop(sp, GROUPS - 1, per_g, 1) as g:
                group(g * 6)
            with t.loop(sp, NE - 1, times(per_g, GROUPS), 1) as e:
                with t.loop(sp, GROUPS, per_g) as g:
                    group(e * (6 * GROUPS) + g * 6)
            n_over = sp.value_load(RI[0:1, 11:12], min_val=0, max_val=MAX_OVER)
            with sp.If(n_over > 0):
                per_x = times(per_g, GROUPS)
                per_x[("raw", 0)] += 1
                per_x[("raw", 1)] += 1
                with t.loop(sp, n_over, per_x) as x:
                    e = sp.value_load(RI[0:1, bass.ds(x + 8, 1)], min_val=0, max_val=NE - 1)
                    for j in range(2):
                        load(j, unit(e * (6 * GROUPS) + j))
                    with t.loop(sp, GROUPS, per_g) as g:
                        group(e * (6 * GROUPS) + g * 6)

            sp.wait_ge(y_done, 1)
            sp.dma_start(LNR[:], lnrow.rearrange("p (a n) -> p a n", a=2)).then_inc(lnr_in, 16)
            outv = out[0].rearrange("(t p) d -> t p d", p=P)
            for i in range(4):
                sp.wait_ge(out_ready, i + 1)
                sp.dma_start(outv[i], ZF[i][:]).then_inc(out_done, 16)
            sp.wait_ge(out_done, 64)

        @block.gpsimd
        def _(pool):
            pool.dma_start(XZ[:], xT_in).then_inc(xin, 16)
            pool.dma_start(CX[:], ctxT_in).then_inc(cxin, 16)
            pool.dma_start(MASKF[:], maskin).then_inc(mask_in, 16)
            pool.wait_ge(ol_ready, 4 * NBLK)
            pool.dma_start(RT[:], rconst).then_inc(rc_in, 16)
            pool.wait_ge(zero_ready, 1)
            with pool.Fori(0, N_ROWS // P) as a:
                pool.dma_start(xg_d[bass.ds(a * P, P), :], ZT[:]).then_inc(zeroed, 16)
            with pool.Fori(NE * CAP // P, N_ROWS // P) as a:
                pool.dma_start(yg_d[bass.ds(a * P, P), :], ZT[:]).then_inc(zeroed, 16)
            pool.wait_ge(zeroed, 16 * (N_ROWS + MAX_OVER * CAP) // P)
            pool.wait_ge(dest_ready, 1)
            pool.wait_ge(tr_free, 4)
            for c in range(2):
                for i in range(4):
                    pool.indirect_dma_start(xg_d[:, :], bass.IndirectOffsetOnAxis(ap=DI[:, c, i:i + 1], axis=0),
                                            HT[:, i, :], None).then_inc(scattered, 16)
            pool.wait_ge(scattered, 16 * 8)

            def rows(buf, i):
                at = slice(i * CAP, (i + 1) * CAP) if isinstance(i, int) else bass.ds(i * CAP, CAP)
                return buf[at, :].rearrange("(s p) n -> p s n", p=P)

            def store(i, n):
                pool.wait_ge(ys_a, n)
                pool.wait_ge(ys_b, n)
                pool.sem_inc(pool_turn, 1)
                pool.dma_start(rows(yg_d, i), YS[:]).then_inc(y_out, 16)
                pool.wait_ge(y_out, n * 16)
                pool.sem_inc(ys_free, 1)

            pool.wait_ge(routed, 1)
            pool.dma_start(XG[:], rows(xg_d, 0)).then_inc(xg_in, 16)
            with pool.Fori(0, NE - 1) as e:
                pool.wait_ge(xt_full, e + 1)
                pool.sem_inc(pool_turn, 1)
                pool.dma_start(XG[:], rows(xg_d, e + 1)).then_inc(xg_in, 16)
                store(e, e + 1)
            store(NE - 1, NE)
            n_over = pool.value_load(RI[0:1, 11:12], min_val=0, max_val=MAX_OVER)
            with pool.If(n_over > 0):
                with pool.Fori(0, n_over) as x:
                    pool.dma_start(XG[:], rows(xg_d, x + NE)).then_inc(xg_in, 16)
                    store(x + NE, x + (NE + 1))
            pool.sem_inc(y_done, 1)
            for i in range(4):
                if i >= 2:
                    pool.wait_ge(yg_free, i - 1)
                for c in range(2):
                    pool.indirect_dma_start(YG[i % 2][c][:, :], None, yg_d[:, :],
                                            bass.IndirectOffsetOnAxis(ap=DI[:, c, i:i + 1], axis=0)
                                            ).then_inc(yg_in[i % 2], 16)

        @block.scalar
        def _(act):
            t = Turns()
            steps = [0]

            def full_split(r, h):
                act.wait_ge(raw_loaded[r], t.n(("raw", r)) * 16)
                act.wait_ge(unit_done[h], t.n(("hs", h)))
                act.activation(HI[h][:], RAW[r][:], ACT.Copy).then_inc(hi_ready[h], 1)

            def done(h):
                act.wait_ge(unit_done[h], t.n(("ud", h)) + 1)

            for s in raw_used:
                act.sem_inc(s, 1)
            for s in unit_done:
                act.sem_inc(s, 1)
            for s in pair_free:
                act.sem_inc(s, 1)
            act.sem_inc(mod_free, 1)
            act.sem_inc(ys_free, 1)
            act.wait_ge(small_in, 16)
            act.activation(SILC[:].rearrange("p k v -> p (k v)"), sm("cc"), ACT.Silu).then_inc(silc_ready, 1)
            act.activation(IDR[:], ident, ACT.Copy).then_inc(idr_ready, 1)
            act.wait_ge(mask_in, 16)
            act.activation(MASK[:], MASKF[:], ACT.Copy).then_inc(idr_ready, 1)

            cnt = {"tmp": 0}

            def to_hi(k):
                cnt["tmp"] += 1
                act.wait_ge(tmp_ready, cnt["tmp"])
                act.activation(AH[:, k, :], TMP[k % 2][:], ACT.Copy).then_inc(ah_ready, 1)

            act.wait_ge(idr_ready, 2)
            for k in range(KD):
                act.wait_ge(ctx_tmp, k + 1)
                act.activation(CXH[:, k, :], TMP[k % 2][:, 0:CTX], ACT.Copy).then_inc(cxh_ready, 1)
            for k in range(KD):
                to_hi(k)

            def mods(n):
                for r in n:
                    t.skip(("raw", r), 1)

            def layer_norm(stage):
                act.wait_ge(stats_full, stage)
                act.activation(M2[:], PS[:, 6, :], ACT.Square).then_inc(m2_ready, 1)
                act.wait_ge(var_ready, stage)
                act.activation(RSTD[:], VAR[:], ACT.Sqrt).then_inc(sd_ready, 1)

            zc = [0]

            def square(k):
                zc[0] += 1
                act.wait_ge(z_ready, zc[0])
                act.activation(SQ[k % 2][:], XZ[:, k, :], ACT.Square).then_inc(sq_ready, 1)

            fl = {"n": 0}
            for si, (name, count, body) in enumerate(SEGMENTS):
                pos = positions(body)
                svs = [p for p in pos if p[0] == "s"]
                if name == "modA":
                    mods([p[1] for p in pos] * count)
                    full_split(0, 0)
                    continue
                skipper = [[] for _ in svs]
                for p in pos:
                    if p[0] == "s":
                        at = p[3]
                    else:
                        skipper[at].append(p[1])

                if name[:2] == "up":
                    f0 = fl["n"]
                    per = dict(ring_per(body))
                    ns = len(svs)
                    act.preload_act_table(ACT.Silu)
                    with t.loop(act, count, per) as i:
                        for j, (_, r, h, _) in enumerate(svs):
                            mods(skipper[j])
                            nx = svs[(j + 1) % ns]
                            full_split(nx[1], nx[2])
                            done(h)
                            b = j % 2
                            act.activation(SG[b][:], PS[:, 2 * b, :], ACT.Silu).then_inc(sg_ready, 1)
                            act.wait_ge(f_ready, i * ns + (f0 + j + 1))
                            act.activation(FH[:, bass.ds(i * ns + j, 1), :].rearrange("p o n -> p (o n)"),
                                           TMP[b][:], ACT.Copy).then_inc(fh_ready, 1)
                    fl["n"] += count * ns
                    continue
                if name == "conv":
                    with t.loop(act, count, ring_per(body)) as i:
                        for j, (_, r, h, _) in enumerate(svs):
                            nx = svs[(j + 1) % 3]
                            full_split(nx[1], nx[2])
                            done(h)
                            if j == 0:
                                act.activation(CS[:], PS[:, 0:2, :], ACT.Copy).then_inc(cs_ready, 1)
                            elif j == 2:
                                act.wait_ge(yc_ready, i + 1)
                                act.activation(FH[:, bass.ds(i * 2, 2), :], TM2[:], ACT.Copy).then_inc(fh_ready, 1)
                    continue
                if name == "q":
                    with t.loop(act, count, ring_per(body)) as i:
                        for j, (_, r, h, _) in enumerate(svs):
                            mods(skipper[j])
                            nx = svs[(j + 1) % len(svs)]
                            full_split(nx[1], nx[2])
                            done(h)
                    attention_act(act)
                    continue
                for j, (_, r, h, _) in enumerate(svs):
                    mods(skipper[j])
                    if name != "co" or j + 1 < len(svs):
                        nx = svs[(j + 1) % len(svs)]
                        full_split(nx[1], nx[2])
                    done(h)
                    if name == "kv" and j == 0:
                        act.activation(KCH[:].rearrange("p a n -> p (a n)"), PS[:, 2, :], ACT.Copy).then_inc(kvh_ready, 1)
                    if name == "kv" and j == 1:
                        act.activation(VCH[:].rearrange("p a n -> p (a n)"), PS[:, 3, :], ACT.Copy).then_inc(kvh_ready, 1)
                        act.activation(VH[:, 1:5, :].rearrange("p (b a) n -> p b (a n)", b=2), PS[:, 4:6, :],
                                       ACT.Copy).then_inc(kvh_ready, 1)
                    if name in ("o", "dn2", "co"):
                        square(2 * j)
                        square(2 * j + 1)
                if name in ("o", "dn2"):
                    layer_norm({"o": 1, "dn2": 2}[name])
                    for k in range(KD):
                        to_hi(k)
                if name == "co":
                    layer_norm(3)

            for r, h in MOE_BODY[:2]:
                full_split(r, h)
            act.wait_ge(gate_in, 1)
            act.activation(DD[:, 1, :], DD[:, 0, :], ACT.Exp).then_inc(gate_exp, 1)
            for i in range(8):
                act.wait_ge(tr_full, i + 1)
                dst = HT[:, i, :] if i < 4 else XR[:, i - 4, :]
                act.activation(dst.rearrange("p (b n) -> p b n", b=2), PS[:, 2 + 2 * (i % 2):4 + 2 * (i % 2), :],
                               ACT.Copy).then_inc(tr_free, 1)
            act.wait_ge(tr_free, 8)
            act.sem_inc(pair_free[1], 1)
            act.sem_inc(pair_free[2], 1)

            per_g = dict(times(PER_EXP_RING, 1))
            per_g.update({"ht": 2})
            act.wait_ge(routed, 1)

            def expert_round(r):
                act.preload_act_table(ACT.Silu)
                act.wait_ge(xt_full, r)
                for q in range(2):
                    act.activation(XTH[:, 4 * q:4 * q + 4, :].rearrange("p (b k) n -> p b (k n)", b=2),
                                   PS[:, 2 * q:2 * q + 2, :], ACT.Copy).then_inc(xth_ready, 1)
                with t.loop(act, GROUPS, per_g):
                    for j, (_, h) in enumerate(MOE_BODY):
                        full_split(*MOE_BODY[(j + 2) % 6])
                        if j != 4:
                            done(h)
                        if j in (0, 2):
                            act.activation(SE[:, j // 2, :], PS[:, j, :], ACT.Silu).then_inc(se_ready, 1)
                        if j in (2, 4):
                            q = j // 2 - 1
                            act.wait_ge(ht_full, t.n("ht"))
                            act.activation(HH[:, q].rearrange("p a n -> p (a n)"), PS[:, 2 * q, :],
                                           ACT.Copy).then_inc(hh_ready, 1)
                        if j == 4:
                            done(h)
                act.wait_ge(ys_free, r)
                act.activation(YS[:, 0, :].rearrange("p (b n) -> p b n", b=2), PS[:, 4:6, :], ACT.Copy).then_inc(ys_a, 1)

            def ahead():
                for r, h in MOE_BODY[:2]:
                    full_split(r, h)

            def unused():
                for _, h in MOE_BODY[:2]:
                    t.skip(("ud", h), 1)

            per_e = times(per_g, GROUPS)
            with t.loop(act, NE, per_e) as e:
                expert_round(e + 1)
            unused()
            n_over = act.value_load(RI[0:1, 11:12], min_val=0, max_val=MAX_OVER)
            with act.If(n_over > 0):
                per_x = plus_ahead(per_e)
                with t.loop(act, n_over, per_x) as x:
                    ahead()
                    expert_round(x + (NE + 1))
                    unused()

            act.wait_ge(g2_full, 1)
            act.activation(G2R[:].rearrange("p (b n) -> p b n", b=2), PS[:, 0:2, :], ACT.Copy).then_inc(g2_ready, 1)
            for i in range(4):
                act.wait_ge(v_ready, i + 1)
                act.activation(BAG[:, 3:4], BAG[:, 2:3], ACT.Sqrt).then_inc(sdf_ready, 1)

        @block.vector
        def _(dve):
            t = Turns()

            def step(ins):
                ins.then_inc(dve_step, 1)
                dve.wait_ge(dve_step, t.n("step"))

            def split(r, h):
                dve.wait_ge(hi_ready[h], t.n(("hs", h)))
                dve.tensor_tensor(LO[h][:], RAW[r][:], HI[h][:].bitcast(F32), ALU.subtract).then_inc(raw_used[r], 1)

            def done(h):
                dve.wait_ge(unit_done[h], t.n(("ud", h)) + 1)

            mf = [1]

            def mod_evac(u, r):
                dve.wait_ge(mod_full, t.n("mod"))
                dve.sem_inc(raw_used[r], 1)
                if isinstance(u, int):
                    o_, b_ = MOD[:, :, 2 * u:2 * u + 2], bmod[:, :, 2 * u:2 * u + 2]
                else:
                    o_, b_ = MOD[:, :, bass.ds(u * 2, 2)], bmod[:, :, bass.ds(u * 2, 2)]
                dve.tensor_tensor(o_, PS[:, 7, 0:4].rearrange("p (t v) -> p v t", v=2), b_,
                                  ALU.add).then_inc(mod_free, 1)

            dve.memset(K[:, :, 0:BLK], 0.0)
            dve.memset(K[:, :, BLK + T:], 0.0)
            step(dve.memset(ROT[:], 0.0))
            dve.tensor_copy(VH[:, 0, :], ROT[:, 0:256])
            dve.tensor_copy(VH[:, 5, :], ROT[:, 0:256])
            dve.tensor_copy(VL[:, 0, :], ROT[:, 0:256])
            dve.tensor_copy(VL[:, 5, :], ROT[:, 0:256]).then_inc(pads_ready, 1)
            dve.wait_ge(small_in, 16)
            step(dve.tensor_scalar(NSINK[:], sm("sink"), -1.0, None, ALU.mult))
            with t.loop(dve, 2, {"mod": 4}) as i:
                for j in range(4):
                    mod_evac(i * 4 + j, j)
            mf[0] += 8
            dve.wait_ge(mod_free, 9)
            dve.tensor_scalar(COEF[:, 0, 0, :], modcol(0, 1), 1.0, None, ALU.add)
            step(dve.tensor_scalar(CG[:], MOD[:, 1, 8:16], 1.0, None, ALU.add))
            dve.wait_ge(cxin, 16)
            for k in range(KD):
                if k >= 2:
                    dve.wait_ge(cxl_ready, k - 1)
                dve.tensor_scalar(TMP[k % 2][:, 0:CTX], CX[:, k, :], CG[:, k:k + 1], MOD[:, 1, k:k + 1],
                                  ALU.mult, ALU.add).then_inc(ctx_tmp, 1)
                dve.wait_ge(ctx_tmp, k + 1)
                dve.wait_ge(cxh_ready, k + 1)
                dve.tensor_tensor(CXL[:, k, :], TMP[k % 2][:, 0:CTX], CXH[:, k, :].bitcast(F32),
                                  ALU.subtract).then_inc(cxl_ready, 1)

            nt = [0]

            def modulate(stage, shift, n_of):
                for k in range(KD):
                    n_of(k)
                    nt[0] += 1
                    if nl[0]:
                        dve.wait_ge(al_ready, nl[0])
                    dve.tensor_scalar(TMP[k % 2][:], XZ[:, k, :], COEF[:, stage, 0, k:k + 1], shift[:, k:k + 1],
                                      ALU.mult, ALU.add).then_inc(tmp_ready, 1)
                    if k >= 1:
                        low(k - 1)
                    dve.wait_ge(tmp_ready, nt[0])
                    if stage == 0:
                        dve.tensor_scalar(XZ[:, k, :], XZ[:, k, :], ALPHA, None, ALU.mult)
                    else:
                        dve.tensor_scalar(XZ[:, k, :], XZ[:, k, :], COEF[:, stage, 2, k:k + 1],
                                          COEF[:, stage, 3, k:k + 1], ALU.mult, ALU.add)
                low(KD - 1)

            nl = [0]

            def low(k):
                nl[0] += 1
                dve.wait_ge(tmp_ready, nl[0])
                dve.wait_ge(ah_ready, nl[0])
                dve.tensor_tensor(AL[:, k, :], TMP[k % 2][:], AH[:, k, :].bitcast(F32),
                                  ALU.subtract).then_inc(al_ready, 1)

            dve.wait_ge(xin, 16)
            dve.wait_ge(cxl_ready, KD)
            modulate(0, MOD[:, 0, 0:8], lambda k: None)
            dve.wait_ge(al_ready, KD)

            def coefs(stage, ln, layer, ch_shift, ch_scale):
                c = COEF[:, stage]
                dve.wait_ge(mod_free, mf[0])
                g, b = lng[:, ln, :], lnb[:, ln, :]
                step(dve.tensor_scalar(c[:, 2, :], modcol(layer, ch_scale), 1.0, None, ALU.add))
                dve.tensor_tensor(c[:, 0, :], c[:, 2, :], g, ALU.mult)
                step(dve.tensor_tensor(c[:, 3, :], c[:, 2, :], b, ALU.mult))
                step(dve.tensor_tensor(c[:, 1, :], c[:, 3, :], modcol(layer, ch_shift), ALU.add))
                dve.tensor_scalar(c[:, 2, :], g, ALPHA, None, ALU.mult)
                step(dve.tensor_scalar(c[:, 3, :], b, ALPHA, None, ALU.mult))

            def norm_start(stage):
                dve.wait_ge(m2_ready, stage)
                dve.scalar_tensor_tensor(out=VAR[:], in0=PS[:, 7, :], scalar=EPS, in1=M2[:], op0=ALU.add,
                                         op1=ALU.subtract).then_inc(var_ready, 1)
                for k in range(4):
                    dve.tensor_tensor(XZ[:, k, :], XZ[:, k, :], PS[:, 6, :], ALU.subtract)
                dve.wait_ge(sd_ready, stage)
                step(dve.reciprocal(RSTD[:], RSTD[:]))
                for k in range(4, KD):
                    ins = dve.tensor_tensor(XZ[:, k, :], XZ[:, k, :], PS[:, 6, :], ALU.subtract)
                step(ins)

            def norm_k(k):
                step(dve.tensor_tensor(XZ[:, k, :], XZ[:, k, :], RSTD[:], ALU.mult))

            nz = [0]
            ns_ = [0]

            def residual(k, src, gate, first, last):
                ins = dve.scalar_tensor_tensor(out=XZ[:, k, :], in0=src, scalar=gate[:, k:k + 1], in1=XZ[:, k, :],
                                               op0=ALU.mult, op1=ALU.add)
                return ins

            def sums(k):
                ns_[0] += 1
                if k == 0:
                    dve.wait_ge(z_ready, ns_[0])
                    dve.tensor_copy(ZS[:], XZ[:, 0, :])
                    dve.wait_ge(sq_ready, ns_[0])
                    step(dve.tensor_copy(QS[:], SQ[0][:]))
                else:
                    dve.tensor_tensor(ZS[:], ZS[:], XZ[:, k, :], ALU.add)
                    dve.wait_ge(sq_ready, ns_[0])
                    ins = dve.tensor_tensor(QS[:], QS[:], SQ[k % 2][:], ALU.add)
                    if k == KD - 1:
                        ins.then_inc(stats_in, 1)
                    else:
                        step(ins)

            split(0, 0)
            rot_mask = [(i + 16) % 32 for i in range(32)]

            def rope_tile(bank, dst, last_read_sem):
                n = t.n("rope")
                if not isinstance(n, int) or n > 1:
                    dve.wait_ge(rope_done, n - 1)
                dve.tensor_tensor(dst, PS[:, bank, :], COS[:], ALU.mult)
                ins = dve.stream_shuffle(ROT[:], PS[:, bank, :], rot_mask)
                if last_read_sem is not None:
                    ins.then_inc(last_read_sem, 1)
                    dve.wait_ge(last_read_sem, t.n(("rel", id(last_read_sem))) + 1)
                else:
                    step(ins)
                step(dve.tensor_tensor(ROT[:], ROT[:], SIN[:], ALU.mult))
                dve.tensor_tensor(dst, dst, ROT[:], ALU.add).then_inc(rope_done, 1)

            fl = [0]
            unit_m = 8
            for name, count, body in SEGMENTS[1:]:
                pos = positions(body)
                svs = [p for p in pos if p[0] == "s"]
                ns = len(svs)
                nm = body.count("m")
                mf_after = mf[0] + nm * count
                ringp = {k: v for k, v in ring_per(body).items() if k[0] != "raw"}

                def mod_pair(i, j):
                    if nm:
                        if isinstance(i, int):
                            mod_evac(unit_m + 2 * j, 1)
                            mod_evac(unit_m + 2 * j + 1, 2)
                        else:
                            mod_evac(i * nm + (unit_m + 2 * j), 1)
                            mod_evac(i * nm + (unit_m + 2 * j + 1), 2)

                if name == "kv":
                    dve.wait_ge(rope_in, 32)
                    split(svs[1][1], svs[1][2])
                    done(svs[0][2])
                    dve.wait_ge(kvh_ready, 1)
                    dve.tensor_tensor(KCL[:].rearrange("p a n -> p (a n)"), PS[:, 2, :],
                                      KCH[:].rearrange("p a n -> p (a n)").bitcast(F32), ALU.subtract)
                    rope_tile(0, K[:, 0, BLK:BLK + T], None)
                    rope_tile(1, K[:, 1, BLK:BLK + T], pair_free[0])
                    mod_pair(0, 0)
                    split(svs[0][1], svs[0][2])
                    done(svs[1][2])
                    dve.wait_ge(kvh_ready, 2)
                    dve.tensor_tensor(VCL[:].rearrange("p a n -> p (a n)"), PS[:, 3, :],
                                      VCH[:].rearrange("p a n -> p (a n)").bitcast(F32),
                                      ALU.subtract).then_inc(pair_free[1], 1)
                    dve.wait_ge(kvh_ready, 3)
                    dve.tensor_tensor(VL[:, 1:5, :].rearrange("p (b a) n -> p b (a n)", b=2), PS[:, 4:6, :],
                                      VH[:, 1:5, :].rearrange("p (b a) n -> p b (a n)", b=2).bitcast(F32),
                                      ALU.subtract).then_inc(pair_free[2], 1)
                    mod_pair(0, 1)
                    t.n(("rel", id(pair_free[1])))
                elif name == "q":
                    per = dict(ringp)
                    per.update({"mod": nm, "step": 6, "rope": 4, ("rel", id(pair_free[0])): 1, ("rel", id(pair_free[1])): 1})
                    with t.loop(dve, count, per) as i:
                        for j, (_, r, h, _) in enumerate(svs):
                            nx = svs[(j + 1) % ns]
                            split(nx[1], nx[2])
                            done(h)
                            pf = pair_free[j]
                            for c in range(2):
                                dst = Q[:, bass.ds(i * 4 + (2 * j + c), 1), :].rearrange("p o n -> p (o n)")
                                rope_tile(2 * j + c, dst, pf if c else None)
                            mod_pair(i, j)
                    mf[0] = mf_after
                    attention_dve(dve, t)
                    dve.memset(ZT[:], 0.0).then_inc(zero_ready, 1)
                    coefs(1, 0, 0, 3, 4)
                elif name[:2] == "up":
                    f0 = fl[0]
                    per = dict(ringp)
                    per.update({"mod": nm} if nm else {})
                    with t.loop(dve, count, per) as i:
                        for j, (_, r, h, _) in enumerate(svs):
                            nx = svs[(j + 1) % ns]
                            split(nx[1], nx[2])
                            done(h)
                            b = j % 2
                            n = i * ns + (f0 + j + 1)
                            dve.wait_ge(sg_ready, n)
                            dve.tensor_tensor(TMP[b][:], SG[b][:], PS[:, 2 * b + 1, :], ALU.mult).then_inc(f_ready, 1)
                            dve.wait_ge(f_ready, n)
                            dve.sem_inc(pair_free[b], 1)
                            dve.wait_ge(fh_ready, n)
                            fs = bass.ds(i * ns + j, 1)
                            dve.tensor_tensor(FL[:, fs, :].rearrange("p o n -> p (o n)"), TMP[b][:],
                                              FH[:, fs, :].rearrange("p o n -> p (o n)").bitcast(F32),
                                              ALU.subtract).then_inc(fl_ready, 1)
                            mod_pair(i, j)
                            dve.wait_ge(fl_ready, n)
                    fl[0] += count * ns
                elif name == "conv":
                    coefs(3, 2, 1, 3, 4)
                    dve.memset(UP[:, :, 0:1], 0.0)
                    step(dve.memset(UP[:, :, T + 1:T + 2], 0.0))
                    per = dict(ringp)
                    per.update({"step": 6})
                    with t.loop(dve, count, per) as i:
                        split(*svs[1][1:3])
                        done(svs[0][2])
                        step(dve.tensor_copy(CWG[:], cw[:, :, bass.ds(i * 2, 2)]))
                        split(*svs[2][1:3])
                        done(svs[1][2])
                        dve.wait_ge(cs_ready, i + 1)
                        step(dve.tensor_tensor(UP[:, :, 1:T + 1], PS[:, 2:4, :], CS[:], ALU.mult))
                        dve.sem_inc(pair_free[0], 1)
                        dve.sem_inc(pair_free[1], 1)
                        for c in range(2):
                            ins = dve.tensor_scalar(YC[:, c, :], UP[:, c, 0:T], CWG[:, 0, c:c + 1], None, ALU.mult)
                        step(ins)
                        for w_ in (1, 2):
                            for c in range(2):
                                ins = dve.scalar_tensor_tensor(out=YC[:, c, :], in0=UP[:, c, w_:w_ + T],
                                                               scalar=CWG[:, w_, c:c + 1], in1=YC[:, c, :],
                                                               op0=ALU.mult, op1=ALU.add)
                            step(ins)
                        split(*svs[0][1:3])
                        done(svs[2][2])
                        dve.tensor_tensor(TM2[:], PS[:, 4:6, :], YC[:], ALU.mult).then_inc(yc_ready, 1)
                        dve.wait_ge(yc_ready, i + 1)
                        dve.sem_inc(pair_free[2], 1)
                        dve.wait_ge(fh_ready, i + (fl[0] + 1))
                        step(dve.tensor_tensor(FL[:, bass.ds(i * 2, 2), :], TM2[:],
                                               FH[:, bass.ds(i * 2, 2), :].bitcast(F32), ALU.subtract))
                    dve.sem_inc(fl_ready, 1)
                else:
                    layer = 1 if name == "co" else 0
                    gate = modcol(layer, 2 if name in ("o", "co") else 5)
                    lastpart = name in ("o", "dn2", "co")
                    tiles = DOWN6 if name == "dn1" else [[2 * j, 2 * j + 1] for j in range(4)]
                    dve.wait_ge(mod_free, mf[0])
                    for j, (_, r, h, _) in enumerate(svs):
                        if name != "co" or j + 1 < ns:
                            nx = svs[(j + 1) % ns]
                            split(nx[1], nx[2])
                        done(h)
                        for k in tiles[j]:
                            bank = k % 4
                            ins = residual(k, PS[:, bank, :], gate, False, lastpart)
                            if lastpart:
                                nz[0] += 1
                                ins.then_inc(z_ready, 1)
                                dve.wait_ge(z_ready, nz[0])
                                if k % 2:
                                    dve.sem_inc(pair_free[bank // 2], 1)
                                sums(k)
                            else:
                                step(ins)
                                if k % 2:
                                    dve.sem_inc(pair_free[bank // 2], 1)
                    if lastpart:
                        stage = {"o": 1, "dn2": 2, "co": 3}[name]
                        norm_start(stage)
                        dve.sem_inc(mod_free, 1)
                        mf[0] += 1
                        if stage < 3:
                            modulate(stage, COEF[:, stage, 1, :], norm_k)
                            dve.wait_ge(al_ready, nl[0])
                        else:
                            for k in range(KD):
                                norm_k(k)
                                step(dve.tensor_scalar(HF[:, k, :], XZ[:, k, :], COEF[:, 3, 0, k:k + 1],
                                                       COEF[:, 3, 1, k:k + 1], ALU.mult, ALU.add))
                                step(dve.tensor_scalar(XZ[:, k, :], XZ[:, k, :], COEF[:, 3, 2, k:k + 1],
                                                       COEF[:, 3, 3, k:k + 1], ALU.mult, ALU.add))
                            dve.sem_inc(tmp_ready, 1)
                    if name == "dn1":
                        coefs(2, 1, 1, 0, 1)
                unit_m += nm * count
                if name != "q":
                    mf[0] += nm * count

            for r, h in MOE_BODY[:2]:
                split(r, h)
            dve.wait_ge(lg_full, 1)
            step(dve.tensor_copy(LG[:].rearrange("p t e -> p (t e)"), PS[:, 0, 0:32]))
            dve.sem_inc(pair_free[0], 1)
            for i in range(4):
                step(dve.max(MX[:, i, :], LG[:, i, :]))
                step(dve.max_index(IX[:, i, :], MX[:, i, :], LG[:, i, :]))
            step(dve.tensor_copy(IXF[:], IX[:, :, 0:2]))
            dve.wait_ge(rc_in, 16)
            for c in range(2):
                for i in range(4):
                    ins = dve.tensor_scalar(OH[:, c, i, :], RT[:, 256:264], IXF[:, i, c:c + 1], None, ALU.is_equal)
            step(ins)
            dve.tensor_tensor(MM[:], OH[:, 0], OH[:, 1], ALU.add).then_inc(mask_ready, 1)
            dve.tensor_tensor(DD[:, 0, :], MX[:, :, 1], MX[:, :, 0], ALU.subtract).then_inc(gate_in, 1)
            dve.wait_ge(gate_exp, 1)
            step(dve.tensor_scalar(DD[:, 2, :], DD[:, 1, :], 1.0, None, ALU.add))
            step(dve.reciprocal(GA[:, 0, :], DD[:, 2, :]))
            step(dve.tensor_tensor(GA[:, 1, :], DD[:, 1, :], GA[:, 0, :], ALU.mult))
            dve.wait_ge(pos_full, 1)
            step(dve.tensor_copy(RF[:, 0:8], PS[:, 0, 32:40]))
            step(dve.tensor_scalar(OV[:, 0, :], RF[:, 0:8], float(CAP), None, ALU.is_gt))
            step(dve.tensor_tensor_scan(OV[:, 1, :], RT[:, 0:8], OV[:, 0, :], 0.0, ALU.mult, ALU.add))
            step(dve.tensor_scalar(ADJ[:], OV[:, 1, :], float(CAP), float((NE - 2) * CAP), ALU.mult, ALU.add))
            dve.tensor_scalar(PT1[:].rearrange("p t e -> p (t e)"), PS[:, 0, 0:32], float(CAP), None, ALU.is_ge)
            step(dve.tensor_tensor(ADJ[:], ADJ[:], RT[:, 264:272], ALU.subtract))
            for i in range(4):
                dve.tensor_tensor(PB[:, i, :], PS[:, 0, 8 * i:8 * i + 8], RT[:, 264:272], ALU.add)
                ins = dve.tensor_tensor(PT1[:, i, :], PT1[:, i, :], ADJ[:], ALU.mult)
            step(ins)
            dve.sem_inc(pair_free[0], 1)
            step(dve.tensor_tensor(PB[:], PB[:], PT1[:], ALU.add))
            for c in range(2):
                step(dve.tensor_tensor(PT1[:], OH[:, c], PB[:], ALU.mult))
                step(dve.tensor_reduce(DF[:, c, :], PT1[:], AX.X, ALU.add))
            dve.tensor_copy(DI[:], DF[:]).then_inc(dest_ready, 1)
            step(dve.tensor_copy(RF[:, 11:12], OV[:, 1, 7:8]))
            for x in range(MAX_OVER):
                step(dve.tensor_scalar(OV[:, 2, :], OV[:, 1, :], float(x), None, ALU.is_le))
                step(dve.tensor_reduce(RF[:, 8 + x:9 + x], OV[:, 2, :], AX.X, ALU.add))
            step(dve.tensor_copy(RI[:, 0:12], RF[:, 0:12]))
            dve.wait_ge(tr_free, 8)
            dve.sem_inc(routed, 1)

            per_g = {k: v for k, v in PER_EXP_RING.items() if k[0] != "raw"}
            per_g.update({"se": 2, "hh": 2})

            def expert_round(r):
                for q in range(2):
                    dve.wait_ge(xth_ready, t.n("xth"))
                    dve.tensor_tensor(XTL[:, 4 * q:4 * q + 4, :].rearrange("p (b k) n -> p b (k n)", b=2),
                                      PS[:, 2 * q:2 * q + 2, :],
                                      XTH[:, 4 * q:4 * q + 4, :].rearrange("p (b k) n -> p b (k n)", b=2).bitcast(F32),
                                      ALU.subtract).then_inc(xtl_ready, 1)
                with t.loop(dve, GROUPS, per_g):
                    for j, (_, h) in enumerate(MOE_BODY):
                        split(*MOE_BODY[(j + 2) % 6])
                        if j != 4:
                            done(h)
                        if j in (1, 3):
                            q = j // 2
                            dve.wait_ge(se_ready, t.n("se"))
                            dve.tensor_tensor(HE[:, q, :], SE[:, q, :], PS[:, j, :], ALU.mult).then_inc(he_ready, 1)
                        if j in (2, 4):
                            q = j // 2 - 1
                            dve.wait_ge(hh_ready, t.n("hh"))
                            dve.tensor_tensor(HL[:, q].rearrange("p a n -> p (a n)"), PS[:, 2 * q, :],
                                              HH[:, q].rearrange("p a n -> p (a n)").bitcast(F32),
                                              ALU.subtract).then_inc(hl_ready, 1)
                        if j == 4:
                            done(h)
                dve.wait_ge(ys_free, r)
                dve.tensor_copy(YS[:, 1, :].rearrange("p (b n) -> p b n", b=2), PS[:, 6:8, :]).then_inc(ys_b, 1)
                dve.wait_ge(ys_b, r)
                dve.wait_ge(ys_a, r)
                dve.memset(PS[:, 4:8, :], 0.0).then_inc(y_zero, 1)

            def unused():
                for _, h in MOE_BODY[:2]:
                    t.skip(("ud", h), 1)

            per_e = times(per_g, GROUPS)
            per_e["xth"] = 2
            dve.memset(PS[:, 4:8, :], 0.0).then_inc(y_zero, 1)
            with t.loop(dve, NE, per_e) as e:
                expert_round(e + 1)
            unused()
            n_over = dve.value_load(RI[0:1, 11:12], min_val=0, max_val=MAX_OVER)
            with dve.If(n_over > 0):
                with t.loop(dve, n_over, plus_ahead(per_e)) as x:
                    for r, h in MOE_BODY[:2]:
                        split(r, h)
                    expert_round(x + (NE + 1))
                    unused()

            dve.wait_ge(y_done, 1)
            for k in range(KD):
                ins = dve.tensor_scalar(DG[:, k, :], ident, MOD[:, 0, 88 + k:89 + k], float(D), ALU.mult, ALU.mult)
            ins.then_inc(dg_ready, 1)
            dve.wait_ge(lnr_in, 16)
            s0 = t.at["step"]
            fs = sem("final_step")
            fn = [0]

            def fstep(ins):
                fn[0] += 1
                ins.then_inc(fs, 1)
                dve.wait_ge(fs, fn[0])

            for i in range(4):
                z = ZF[i]
                y0, y1 = YG[i % 2]
                dve.wait_ge(yg_in[i % 2], 32 * (i // 2 + 1))
                fstep(dve.tensor_scalar(z[:], y0[:], GA[:, 0, i:i + 1], None, ALU.mult))
                dve.scalar_tensor_tensor(out=z[:], in0=y1[:], scalar=GA[:, 1, i:i + 1], in1=z[:], op0=ALU.mult,
                                         op1=ALU.add).then_inc(yg_free, 1)
                dve.wait_ge(yg_free, i + 1)
                if i == 0:
                    dve.wait_ge(g2_ready, 1)
                fstep(dve.tensor_tensor(z[:], z[:], G2R[:], ALU.mult))
                fstep(dve.tensor_tensor(z[:], z[:], XR[:, i, :], ALU.add))
                for c in range(2):
                    ins = dve.bn_stats(BST[:, c, :], z[:, 512 * c:512 * c + 512])
                fstep(ins)
                fstep(dve.bn_aggr(BAG[:, 0:2], BST[:]))
                dve.tensor_scalar(BAG[:, 2:3], BAG[:, 1:2], EPS, None, ALU.add).then_inc(v_ready, 1)
                dve.wait_ge(sdf_ready, i + 1)
                fstep(dve.reciprocal(BAG[:, 3:4], BAG[:, 3:4]))
                fstep(dve.tensor_scalar(z[:], z[:], BAG[:, 0:1], BAG[:, 3:4], ALU.subtract, ALU.mult))
                fstep(dve.tensor_tensor(z[:], z[:], LNR[:, 0, :], ALU.mult))
                dve.tensor_tensor(z[:], z[:], LNR[:, 1, :], ALU.add).then_inc(out_ready, 1)

        @block.tensor
        def _(pe):
            t = Turns()

            def three(outp, wh, wl, ah, al, first, last):
                pe.matmul(outp, wh, ah, start=first, stop=False, skip_group_check=True)
                pe.matmul(outp, wh, al, start=False, stop=False, skip_group_check=True)
                return pe.matmul(outp, wl, ah, start=False, stop=last, skip_group_check=True)

            def ready(r, h):
                pe.wait_ge(hi_ready[h], t.n(("hs", h)))
                pe.wait_ge(raw_used[r], t.n(("raw", r)) + 1)

            def mod_unit(r):
                pe.wait_ge(raw_loaded[r], t.n(("raw", r)) * 16)
                pe.wait_ge(mod_free, t.n("mod"))
                w = raw8(r)
                for c in range(2):
                    for k in range(KD):
                        ins = pe.matmul(PS[:, 7, 2 * c:2 * c + 2], w[:, k, c * P:(c + 1) * P], SILC[:, k, :],
                                        start=(k == 0), stop=(k == KD - 1), skip_group_check=True)
                ins.then_inc(mod_full, 1)

            def pair(p):
                pe.wait_ge(pair_free[p], t.n(("pair", p)))

            def unit_k(r, h, outs, ah=AH, al=AL, k_tiles=KD, cols=P):
                hi = HI[h][:].rearrange("p (k n) -> p k n", k=KD)
                lo = LO[h][:].rearrange("p (k n) -> p k n", k=KD)
                for c, outp in enumerate(outs):
                    for k in range(KD):
                        ins = three(outp, hi[:, k, c * P:(c + 1) * P], lo[:, k, c * P:(c + 1) * P],
                                    ah[:, k, :], al[:, k, :], k == 0, k == KD - 1)
                ins.then_inc(unit_done[h], 1)

            pe.wait_ge(silc_ready, 1)
            per = {("raw", r): 1 for r in range(4)}
            per.update({"mod": 4})
            with t.loop(pe, 2, per) as i:
                for r in range(4):
                    mod_unit(r)
            pe.wait_ge(cxl_ready, KD)
            pe.wait_ge(al_ready, KD)

            def stats(stage):
                pe.wait_ge(stats_in, stage)
                pe.wait_ge(mod_free, t.n("mod"))
                pe.matmul(PS[:, 6, :], mean_w, ZS[:], start=True, stop=True)
                pe.matmul(PS[:, 7, :], mean_w, QS[:], start=True, stop=True).then_inc(stats_full, 1)

            fl_n = 0
            al_n = KD
            for name, count, body in SEGMENTS[1:]:
                pos = positions(body)
                svs = [p for p in pos if p[0] == "s"]
                ns = len(svs)
                nm = body.count("m")
                rper = dict(ring_per(body))
                rper = {k: v for k, v in rper.items() if k[0] != "ud"}
                if nm:
                    rper.update({"mod": nm})
                if name == "kv":
                    for kind, r, h, j in pos:
                        if kind == "m":
                            mod_unit(r)
                            continue
                        ready(r, h)
                        hi = HI[h][:].rearrange("p (k n) -> p k n", k=KD)
                        lo = LO[h][:].rearrange("p (k n) -> p k n", k=KD)
                        if j == 0:
                            pair(0)
                            pair(1)
                            for c in range(2):
                                for k in range(KD):
                                    three(PS[:, 2, c * CTX:(c + 1) * CTX], hi[:, k, c * P:(c + 1) * P],
                                          lo[:, k, c * P:(c + 1) * P], CXH[:, k, :], CXL[:, k, :], k == 0, k == KD - 1)
                            unit_k(r, h, [PS[:, 0, :], PS[:, 1, :]])
                        else:
                            pair(2)
                            for m in range(6):
                                bank, col = 3 + m // 2, (m % 2) * 256
                                ah, al = (CXH, CXL) if m < 2 else (AH, AL)
                                o_ = (m % 2) * P if m < 2 else (m - 2) * P
                                for k in range(KD):
                                    ins = three(PS[:, bank, col:col + 256], ah[:, k, o_:o_ + P], al[:, k, o_:o_ + P],
                                                hi[:, k, :], lo[:, k, :], k == 0, k == KD - 1)
                            ins.then_inc(unit_done[h], 1)
                elif name == "q":
                    rper.update({("pair", 0): 1, ("pair", 1): 1})
                    with t.loop(pe, count, rper) as i:
                        for kind, r, h, j in pos:
                            if kind == "m":
                                mod_unit(r)
                                continue
                            ready(r, h)
                            pair(j)
                            unit_k(r, h, [PS[:, 2 * j, :], PS[:, 2 * j + 1, :]])
                    attention_pe(pe, three)
                elif name[:2] == "up":
                    rper.update({("pair", 0): ns // 2, ("pair", 1): ns // 2})
                    with t.loop(pe, count, rper) as i:
                        for kind, r, h, j in pos:
                            if kind == "m":
                                mod_unit(r)
                                continue
                            ready(r, h)
                            pair(j % 2)
                            hi = HI[h][:].rearrange("p (g k n) -> p g k n", g=2, k=KD)
                            lo = LO[h][:].rearrange("p (g k n) -> p g k n", g=2, k=KD)
                            for c in range(2):
                                for k in range(KD):
                                    ins = three(PS[:, 2 * (j % 2) + c, :], hi[:, c, k, :], lo[:, c, k, :],
                                                AH[:, k, :], AL[:, k, :], k == 0, k == KD - 1)
                            ins.then_inc(unit_done[h], 1)
                    fl_n += count * ns
                elif name == "dn1":
                    pe.wait_ge(fl_ready, fl_n)
                    nk = FF_PARTS[1]
                    for _, r, h, j in svs:
                        ready(r, h)
                        hi = HI[h][:].rearrange("p (a n) -> p a n", n=P)
                        lo = LO[h][:].rearrange("p (a n) -> p a n", n=P)
                        for a in range(16):
                            d, k = divmod(16 * j + a, nk)
                            if k == 0 and d % 2 == 0:
                                pair((d // 2) % 2)
                            ins = three(PS[:, d % 4, :], hi[:, a, :], lo[:, a, :], FH[:, k, :], FL[:, k, :],
                                        k == 0, k == nk - 1)
                        ins.then_inc(unit_done[h], 1)
                elif name == "conv":
                    pe.wait_ge(al_ready, 3 * KD)
                    rper.update({("pair", 0): 1, ("pair", 1): 1, ("pair", 2): 1})
                    with t.loop(pe, count, rper) as i:
                        for kind, r, h, j in pos:
                            ready(r, h)
                            pair(j)
                            unit_k(r, h, [PS[:, 2 * j, :], PS[:, 2 * j + 1, :]])
                    fl_n += 1
                else:
                    a_, l_ = (AH, AL) if name == "o" else (FH, FL)
                    if name == "o":
                        pe.wait_ge(ol_ready, 4 * NBLK)
                    else:
                        pe.wait_ge(fl_ready, fl_n)
                    for _, r, h, j in svs:
                        ready(r, h)
                        pair(j % 2)
                        unit_k(r, h, [PS[:, 2 * (j % 2), :], PS[:, 2 * (j % 2) + 1, :]], a_, l_)
                if name in ("o", "dn2", "co"):
                    stats({"o": 1, "dn2": 2, "co": 3}[name])
                if name == "o":
                    pe.wait_ge(al_ready, 2 * KD)

            pe.wait_ge(tmp_ready, 3 * KD + 1)
            pair(0)
            for i in range(4):
                for k in range(KD):
                    ins = pe.matmul(PS[:, 0, 8 * i:8 * i + 8], HF[:, k, i * P:(i + 1) * P], wr[:, k, :],
                                    start=(k == 0), stop=(k == KD - 1), skip_group_check=True)
            ins.then_inc(lg_full, 1)

            def rows(i):
                if i >= 2:
                    pe.wait_ge(tr_free, i - 1)
                else:
                    pair(1 + i)
                src = HF if i < 4 else XZ
                for k in range(KD):
                    ins = pe.transpose(PS[:, 2 + 2 * (i % 2) + k // 4, (k % 4) * P:(k % 4 + 1) * P],
                                       src[:, k, (i % 4) * P:(i % 4 + 1) * P], ident)
                ins.then_inc(tr_full, 1)

            for i in range(4):
                rows(i)
            pe.wait_ge(rc_in, 16)
            pe.wait_ge(mask_ready, 1)
            pair(0)
            for i in range(4):
                for j in range(i + 1):
                    pe.matmul(PS[:, 0, 8 * i:8 * i + 8], ones if j < i else upper, MM[:, j, :], start=(j == 0),
                              stop=(j == i), skip_group_check=True)
            for j in range(4):
                ins = pe.matmul(PS[:, 0, 32:40], ones, MM[:, j, :], start=(j == 0), stop=(j == 3),
                                skip_group_check=True)
            ins.then_inc(pos_full, 1)
            for i in range(4, 8):
                rows(i)
            pe.wait_ge(routed, 1)

            per_g = {k: v for k, v in PER_EXP_RING.items() if k[0] != "ud"}
            per_g.update({"he": 2, "hl": 2})

            def turn_hidden(q, tiles):
                pe.wait_ge(he_ready, t.n("he"))
                for k in range(2):
                    for s in range(tiles):
                        ins = pe.transpose(PS[:, 2 * q, k * CAP + s * P:k * CAP + (s + 1) * P],
                                           HE[:, q, s * 256 + k * P:s * 256 + (k + 1) * P], ident)
                ins.then_inc(ht_full, 1)

            def expert_groups(tiles, r):
                with t.loop(pe, GROUPS, per_g):
                    for j, (rs_, h) in enumerate(MOE_BODY):
                        ready(rs_, h)
                        if j < 4:
                            hi = HI[h][:].rearrange("p (k n) -> p k n", k=KD)
                            lo = LO[h][:].rearrange("p (k n) -> p k n", k=KD)
                            for s in range(tiles):
                                cols_ = slice(s * P, (s + 1) * P)
                                for k in range(KD):
                                    ins = three(PS[:, j, s * 256:(s + 1) * 256], XTH[:, k, cols_], XTL[:, k, cols_],
                                                hi[:, k, :], lo[:, k, :], k == 0, k == KD - 1)
                        else:
                            q = j - 4
                            pe.wait_ge(hl_ready, t.n("hl"))
                            if j == 4:
                                pe.wait_ge(y_zero, r)
                            hi = HI[h][:].rearrange("p (k n) -> p k n", k=2)
                            lo = LO[h][:].rearrange("p (k n) -> p k n", k=2)
                            for k in range(2):
                                if (j, k) == (4, 1):
                                    turn_hidden(1, tiles)
                                for s in range(tiles):
                                    cols_ = slice(s * P, (s + 1) * P)
                                    for b in range(2):
                                        ins = three(PS[:, 4 + 2 * s + b, :], HH[:, q, k, cols_], HL[:, q, k, cols_],
                                                    hi[:, k, b * 512:(b + 1) * 512], lo[:, k, b * 512:(b + 1) * 512],
                                                    False, True)
                        ins.then_inc(unit_done[h], 1)
                        if j == 2:
                            turn_hidden(0, tiles)

            def expert_round(r, count):
                pe.wait_ge(xg_in, r * 16)
                for k in range(KD):
                    for s in range(2):
                        ins = pe.transpose(PS[:, k // 2, (k % 2) * CAP + s * P:(k % 2) * CAP + (s + 1) * P],
                                           XG[:, s, k * P:(k + 1) * P], ident)
                ins.then_inc(xt_full, 1)
                if count is None:
                    pe.wait_ge(xtl_ready, r * 2)
                    pe.sem_inc(pe_turn, 1)
                    expert_groups(2, r)
                else:
                    pe.wait_ge(xtl_ready, r * 2)
                    pe.sem_inc(pe_turn, 1)
                    saved = dict(t.at)
                    with pe.If(count < P + 1):
                        expert_groups(1, r)
                    t.at = saved
                    with pe.If(count > P):
                        expert_groups(2, r)

            def unused():
                for r, h in MOE_BODY[:2]:
                    ready(r, h)
                    pe.sem_inc(unit_done[h], 1)

            per_e = times(per_g, GROUPS)
            with t.loop(pe, NE, per_e) as e:
                cnt = pe.value_load(RI[0:1, bass.ds(e, 1)], min_val=0, max_val=T)
                expert_round(e + 1, cnt)
            unused()
            n_over = pe.value_load(RI[0:1, 11:12], min_val=0, max_val=MAX_OVER)
            with pe.If(n_over > 0):
                with t.loop(pe, n_over, plus_ahead(per_e)) as x:
                    expert_round(x + (NE + 1), None)
                    unused()

            pe.wait_ge(dg_ready, 1)
            for k in range(KD):
                ins = pe.matmul(PS[:, k // 4, (k % 4) * P:(k % 4 + 1) * P], mean_w, DG[:, k, :], start=True, stop=True,
                                skip_group_check=True)
            ins.then_inc(g2_full, 1)



def kernel(**inputs):
    import numpy as np
    import concourse.bacc as _bacc
    from concourse.bass_utils import run_bass_kernel_spmd as _run

    f = np.float32
    a = {k: np.asarray(v) for k, v in inputs.items()}

    def cols(w):
        return w.reshape(KD, P, -1, 256).transpose(2, 1, 0, 3).reshape(-1, P, UNIT)

    order = [8 * kp + 4 * h + g for kp in range(2) for g in range(4) for h in range(2)]
    feat = np.concatenate([np.arange(h * HD, (h + 1) * HD) for h in order])
    mods = np.concatenate([cols(a["w_mod"][0]), cols(a["w_mod"][1])])
    wqkv = a["attn_w_qkv"][0]
    split = {
        "kv": cols(wqkv[:, D:]), "q": cols(wqkv[:, :D][:, feat]), "o": cols(a["attn_w_o"][0][feat]),
        "co": cols(a["conv_w_out"][0]),
        "conv": cols(a["conv_w_in"][0]).reshape(3, 4, P, UNIT)[[1, 2, 0]].transpose(1, 0, 2, 3).reshape(12, P, UNIT),
    }
    w1 = a["ffn_w1"][0].reshape(KD, P, FF // P, P).transpose(2, 1, 0, 3)
    w3 = a["ffn_w3"][0].reshape(KD, P, FF // P, P).transpose(2, 1, 0, 3)
    up = np.stack([w1, w3], axis=2).reshape(FF // P, P, UNIT)
    t0 = 0
    for i, n in enumerate(FF_PARTS):
        split[f"up{i}"] = up[t0:t0 + n]
        w2 = a["ffn_w2"][0][t0 * P:(t0 + n) * P]
        if n == KD:
            split[f"dn{i}"] = cols(w2)
        else:
            split[f"dn{i}"] = w2.reshape(n, P, KD, P).transpose(1, 2, 0, 3).reshape(P, -1, UNIT).transpose(1, 0, 2)
        t0 += n
    w_pre = np.empty((N_PRE, P, UNIT), f)
    u = m = 0
    for name, count, body in SEGMENTS:
        k = 0
        for _ in range(count):
            for kind in body:
                if kind == "s":
                    w_pre[u] = split[name][k]
                    k += 1
                else:
                    w_pre[u] = mods[m]
                    m += 1
                u += 1
    w_all = np.zeros((NE * GROUPS * 6 + 2, P, UNIT), f)
    w_moe = w_all[:-2].reshape(NE, GROUPS, 6, P, UNIT)
    e1 = a["moe_w1"][0].reshape(NE, KD, P, GROUPS, 2, 256)
    e3 = a["moe_w3"][0].reshape(NE, KD, P, GROUPS, 2, 256)
    e2 = a["moe_w2"][0].reshape(NE, GROUPS, 2, 2, P, D)
    for q in range(2):
        w_moe[:, :, 2 * q] = e1[:, :, :, :, q].transpose(0, 3, 2, 1, 4).reshape(NE, GROUPS, P, UNIT)
        w_moe[:, :, 2 * q + 1] = e3[:, :, :, :, q].transpose(0, 3, 2, 1, 4).reshape(NE, GROUPS, P, UNIT)
        w_moe[:, :, 4 + q] = e2[:, :, q].transpose(0, 1, 3, 2, 4).reshape(NE, GROUPS, P, UNIT)

    small = np.zeros((P, N_SM), f)

    def put(name, v):
        lo, hi = SM[name]
        small[:, lo:hi] = v.reshape(P, hi - lo)

    put("cc", np.stack([a["c"][0].reshape(KD, P).T, a["c_ctx"].reshape(KD, P).T], axis=2))
    bm = a["b_mod"].reshape(96, P).T
    put("bmod", np.stack([bm, bm], axis=1))
    put("lng", a["ln_g"].reshape(4 * KD, P).T)
    put("lnb", a["ln_b"].reshape(4 * KD, P).T)
    put("ident", np.eye(P, dtype=f))
    put("mean", np.full((P, P), 1.0 / D, f))
    put("sink", np.broadcast_to(a["attn_sink"][0][order], (P, NH)))
    put("cw", a["conv_w"][0].reshape(3 * KD, P).T)
    put("wr", a["moe_router"][0].reshape(KD, P, NE).transpose(1, 0, 2))

    inv = (10000.0 ** (-np.arange(0, HD // 2, 2, dtype=f) / f(HD // 2))).astype(f)
    pos = np.arange(T)
    ar, ac = (pos // 64).astype(f)[:, None] * inv, (pos % 64).astype(f)[:, None] * inv
    ang = np.concatenate([ar, ar, ac, ac], axis=-1).T
    sign = np.where(np.arange(HD) % 32 < 16, -1.0, 1.0).astype(f)[:, None]
    rope = np.concatenate([np.tile(np.cos(ang), (2, 1)), np.tile(np.sin(ang) * sign, (2, 1))], axis=1).astype(f)
    qi, kj = np.arange(P)[:, None], np.arange(P)[None, :]
    mask = np.zeros((P, NBLK, 2, P), f)
    mask[:, :, 0][np.broadcast_to((kj < qi)[:, None], (P, NBLK, P))] = MASKED
    mask[:, :, 1][np.broadcast_to((kj > qi)[:, None], (P, NBLK, P))] = MASKED
    mask[:, 0, 0] = MASKED
    mask[:, NBLK - 1, 1] = MASKED
    rconst = np.zeros((P, N_RC), f)
    rconst[:, 0:P] = 1.0
    rconst[:, P:2 * P] = (qi < kj)
    rconst[:, 256:264] = np.arange(NE)
    rconst[:, 264:272] = np.arange(NE) * CAP
    lnrow = np.broadcast_to(np.concatenate([a["ln_g"][1, 1], a["ln_b"][1, 1]]), (P, 2 * D))

    arrays = {
        "small": small, "x_t": a["x"][0].T.reshape(KD, P, T).transpose(1, 0, 2),
        "ctx_t": a["ctx"][0].T.reshape(KD, P, CTX).transpose(1, 0, 2), "rope": rope,
        "mask": mask.reshape(P, NBLK, 2 * P), "rconst": rconst, "lnrow": lnrow, "w_pre": w_pre, "w_moe": w_all,
    }
    arrays = {k: np.ascontiguousarray(v) for k, v in arrays.items()}
    nc = _bacc.Bacc("TRN2", target_bir_lowering=False, num_devices=1)
    args = [nc.dram_tensor(k, v.shape, F32, kind="ExternalInput").ap() for k, v in arrays.items()]
    args.append(nc.dram_tensor("out", (1, T, D), F32, kind="ExternalOutput").ap())
    program(nc, *args)
    r = _run(nc, [arrays], core_ids=[0])
    return r.results[0]["out"]
```

```python
from contextlib import ExitStack, contextmanager

import concourse.bass as bass
from concourse import mybir

F32 = mybir.dt.float32
F32R = mybir.dt.float32r
I32 = mybir.dt.int32
U32 = mybir.dt.uint32
ALU = mybir.AluOpType
ACT = mybir.ActivationFunctionType
AX = mybir.AxisListType

P = 128
D = 1024
KD = D // P
T = 512
CTX = 256
HD = 64
NH = 16
NKV = 4
FF = 2816
NE = 8
FE = 3584
UNIT = 2048
BLK = 128
NBLK = T // BLK
WIN = 3 * BLK
NKEY = CTX + WIN
FF_PARTS = (8, 6, 8)
GROUPS = FE // 512
CAP = 256
MAX_OVER = 2 * T // (CAP + 1)
N_ROWS = (NE + MAX_OVER) * CAP
ALPHA = 4 ** 0.25
EPS = 1e-5
SCALE = HD ** -0.5
MASKED = -1e30
DOWN6 = ([0, 1], [2, 3, 4], [5, 6, 7])
ATT_STEPS = 3 * NH

SEGMENTS = [
    ("kv", 1, 2), ("q", 2, 2), ("o", 1, 4), ("up0", 4, 2), ("dn0", 1, 4), ("up1", 3, 2), ("dn1", 1, 3),
    ("up2", 4, 2), ("dn2", 1, 4), ("conv", 4, 3), ("co", 1, 4),
]
N_PRE = sum(n * b for _, n, b in SEGMENTS)
SLOT = {2: (0, 1), 3: (0, 1, 2), 4: (0, 1, 2, 1)}
MOD_A = 8
MOD_B = 8
N_MODB = 5
SM = {}
_o = 0
for _n, _w in (("cc", 16), ("bmod", 192), ("lng", 32), ("lnb", 32), ("ident", 128), ("mean", 128), ("sink", 16),
               ("cw", 24), ("wr", 64)):
    SM[_n] = (_o, _o + _w)
    _o += _w
N_SM = _o
RC = {"ones": (0, 128), "upper": (128, 256), "iota": (256, 264), "base": (264, 272)}
N_RC = 272


class Turns:

    def __init__(self):
        self.at, self.levels = {}, []

    def n(self, key):
        v = self.at.get(key, 0) + 1
        self.at[key] = v
        for i, per in self.levels:
            if per.get(key):
                v = i * per[key] + v
        return v

    def skip(self, key, k):
        self.at[key] = self.at.get(key, 0) + k

    def last(self, key):
        self.skip(key, -1)
        return self.n(key)

    @contextmanager
    def loop(self, eng, count, per, start=0):
        before = dict(self.at)
        with eng.Fori(start, start + count) if isinstance(count, int) else eng.Fori(0, count) as i:
            self.levels.append((i - start if start else i, per))
            yield i
            self.levels.pop()
        for key in set(per) | set(self.at):
            did = self.at.get(key, 0) - before.get(key, 0)
            assert did == per.get(key, 0), (key, did, per.get(key, 0))
            if isinstance(count, int):
                self.at[key] = before.get(key, 0) + count * did


def program(nc, small, xT_in, ctxT_in, rope, maskin, rconst, lnrow, w_mod, w_pre, w_moe, out):
    with ExitStack() as ctx:
        def sem(name):
            return ctx.enter_context(nc.semaphore(name))

        base = 16512
        limit = 229344
        cur = [base]

        def put(name, shape, dt, at=None):
            size = 4
            for s in shape[1:]:
                size *= s
            off = cur[0] if at is None else at
            t = nc.alloc_sbuf_tensor_at(name, shape, dt, offset=off)
            if at is None:
                cur[0] += size
                assert cur[0] <= limit, (name, cur[0])
            else:
                assert at + size <= limit, (name, at + size)
            return t

        RAW = [put(f"raw{i}", [P, UNIT], F32) for i in range(4)]
        o_hi = cur[0]
        HI = [put(f"hi{i}", [P, UNIT], F32R) for i in range(3)]
        o_lo = cur[0]
        LO = [put(f"lo{i}", [P, UNIT], F32R) for i in range(3)]
        o_xz = cur[0]
        XZ = put("xz", [P, KD, T], F32)
        o_ah = cur[0]
        AH = put("ah", [P, KD, T], F32R)
        o_al = cur[0]
        AL = put("al", [P, KD, T], F32R)
        SMALL = put("small", [P, N_SM], F32)
        MOD = put("mod", [P, 2, 2 * 48], F32)
        COEF = put("coef", [P, 4, 4, KD], F32)
        CG = put("cg", [P, KD], F32)
        SILC = put("silc", [P, KD, 2], F32)
        IDR = put("idr", [P, P], F32R)
        NRM = put("nrm", [P, NH], F32)
        NM = put("nm", [P, NH], F32)
        LSUM = put("lsum", [P, NH], F32)
        ES = put("es", [P, NH], F32)
        RS = put("rs", [P, NH], F32)
        NSINK = put("nsink", [P, NH], F32)
        CWG = put("cwg", [P, 3, 2], F32)
        cur[0] = (cur[0] + 31) // 32 * 32
        r2 = cur[0]
        Q = put("q", [P, KD, T], F32, r2)
        CX = put("cx", [P, KD, CTX], F32, r2)
        K = put("k", [P, 2, T + 2 * BLK], F32, r2 + 16384)
        VH = put("vh", [P, NBLK + 2, 256], F32R, r2 + 22528)
        VL = put("vl", [P, NBLK + 2, 256], F32R, r2 + 28672)
        KCH = put("kch", [P, 2, CTX], F32R, r2 + 34816)
        KCL = put("kcl", [P, 2, CTX], F32R, r2 + 36864)
        VCH = put("vch", [P, 2, 256], F32R, r2 + 38912)
        VCL = put("vcl", [P, 2, 256], F32R, r2 + 40960)
        MASK = put("mask", [P, NBLK, 2 * BLK], F32R, r2 + 43008)
        o = r2 + 47104
        CXH = put("cxh", [P, KD, CTX], F32R, o)
        CXL = put("cxl", [P, KD, CTX], F32R, o + 8192)
        COS = put("cos", [P, T], F32, o + 16384)
        SIN = put("sin", [P, T], F32, o + 18432)
        ROT = put("rot", [P, T], F32, o + 20480)
        MASKF = put("maskf", [P, NBLK, 2 * BLK], F32, o)
        QSH = put("qsh", [P, KD, BLK], F32R, o)
        QSL = put("qsl", [P, KD, BLK], F32R, o + 4096)
        KSH = put("ksh", [P, 2, WIN], F32R, o + 8192)
        KSL = put("ksl", [P, 2, WIN], F32R, o + 11264)
        VSH = put("vsh", [P, 3, 256], F32R, o + 14336)
        VSL = put("vsl", [P, 3, 256], F32R, o + 17408)
        PR = [put(f"pr{i}", [P, NKEY], F32, o + 20480 + 2560 * i) for i in range(3)]
        PTH = [put(f"pth{i}", [P, 5, 2, BLK], F32R, o_hi + 8192 + 5120 * i) for i in range(2)]
        PTL = [put(f"ptl{i}", [P, 5, 2, BLK], F32R, at) for i, at in enumerate((o_hi + 8192 + 10240, o_lo + 8192))]
        FH = put("fh", [P, KD, T], F32R, r2)
        FL = put("fl", [P, KD, T], F32R, r2 + 16384)
        SG = [put(f"sg{i}", [P, T], F32, r2 + 32768 + 2048 * i) for i in range(2)]
        CS = put("cs", [P, 2, T], F32, r2 + 32768)
        UP = put("up", [P, 2, T + 2], F32, r2 + 36864)
        YC = put("yc", [P, 2, T], F32, r2 + 40992)
        o = limit // 32 * 32 - 18432
        ZS = put("zs", [P, T], F32, o)
        QS = put("qs", [P, T], F32, o + 2048)
        M2 = put("m2", [P, T], F32, o + 4096)
        VAR = put("var", [P, T], F32, o + 6144)
        RSTD = put("rstd", [P, T], F32, o + 8192)
        SQ = [put(f"sq{i}", [P, T], F32, o + 10240 + 2048 * i) for i in range(2)]
        TMP = [put(f"tmp{i}", [P, T], F32, o + 14336 + 2048 * i) for i in range(2)]
        TM2 = put("tm2", [P, 2, T], F32, o + 14336)
        assert r2 + 47104 + 28672 <= limit and r2 + 45152 <= o
        HF = put("hf", [P, KD, T], F32, o_ah)
        HT = put("ht", [P, 4, D], F32, o_al)
        XTH = put("xth", [P, KD, CAP], F32R, o_xz)
        XTL = put("xtl", [P, KD, CAP], F32R, o_xz + 8192)
        XR = put("xr", [P, 4, D], F32, r2)
        RAW += [put(f"raw{i}", [P, UNIT], F32, r2 + 16384 + 8192 * (i - 4)) for i in (4, 5)]
        XG = put("xg", [P, 2, D], F32, r2 + 32768)
        HH = put("hh", [P, 2, 2, CAP], F32R, r2 + 40960)
        HL = put("hl", [P, 2, 2, CAP], F32R, r2 + 45056)
        SE = put("se", [P, 2, 2 * CAP], F32, r2 + 49152)
        HE = put("he", [P, 2, 2 * CAP], F32, r2 + 53248)
        RT = put("rt", [P, N_RC], F32, r2 + 45088)
        ZT = put("zt", [P, D], F32, r2 + 46176)
        MSA = put("msa", [P, MOD_B, 256], F32, o_lo + 16384)
        MROW = put("mrow", [2, MOD_A * 256], F32, o_hi + 8192)
        MW = put("mw", [P, UNIT], F32, o_hi + 16384)
        MSB = put("msb", [P, MOD_B, 256], F32, r2 + 50272)
        o = r2 + 65536
        LG = put("lg", [P, 4, NE], F32, o + 1088)
        MX = put("mx", [P, 4, 8], F32, o + 1216)
        IX = put("ix", [P, 4, 8], U32, o + 1344)
        IXF = put("ixf", [P, 4, 2], F32, o + 1472)
        OH = put("oh", [P, 2, 4, NE], F32, o + 1504)
        MM = put("mm", [P, 4, NE], F32, o + 1760)
        DD = put("dd", [P, 4, 4], F32, o + 1888)
        PB = put("pb", [P, 4, NE], F32, o + 1952)
        PT1 = put("pt1", [P, 4, NE], F32, o + 2080)
        DF = put("df", [P, 2, 4], F32, o + 2208)
        RF = put("rf", [P, 16], F32, o + 2240)
        OV = put("ov", [P, 3, NE], F32, o + 2304)
        ADJ = put("adj", [P, NE], F32, o + 2400)
        YS = put("ys", [P, 2, D], F32, o_al)
        o = r2 + 68000 // 32 * 32
        DI = put("di", [P, 2, 4], U32, o)
        GA = put("ga", [P, 2, 4], F32, o + 32)
        RI = put("ri", [P, 16], I32, o + 64)
        assert o + 128 <= limit
        LNR = put("lnr", [P, 2, D], F32, base)
        G2R = put("g2r", [P, D], F32, base + 8192)
        DG = put("dg", [P, KD, P], F32, base + 12288)
        YG = [[put(f"yg{i}{c}", [P, D], F32, base + 16384 + 8192 * i + 4096 * c) for c in range(2)] for i in range(2)]
        ZF = [put(f"zf{i}", [P, D], F32, base + 32768 + 4096 * i) for i in range(4)]
        BST = put("bst", [P, 2, 6], F32, base + 49152)
        BAG = put("bag", [P, 4], F32, base + 49280)

        PS = ctx.enter_context(nc.psum_tensor("ps", [P, 8, 512], F32))

        xg_d = nc.dram_tensor("dispatched_x", [N_ROWS, D], F32).ap()
        yg_d = nc.dram_tensor("expert_y", [N_ROWS, D], F32).ap()

        small_in, xin, cxin, rope_in, mask_in, rc_in, lnr_in = map(sem, (
            "small_in", "x_in", "ctx_in", "rope_in", "mask_in", "routing_const_in", "lnrow_in"))
        raw_loaded = [sem(f"raw_loaded{i}") for i in range(6)]
        raw_used = [sem(f"raw_used{i}") for i in range(6)]
        hi_ready = [sem(f"hi_ready{i}") for i in range(3)]
        unit_done = [sem(f"unit_done{i}") for i in range(3)]
        pair_free = [sem(f"pair_free{i}") for i in range(3)]
        modw_in, pool_step, mod_sums = sem("w_mod_in"), sem("pool_step"), sem("mod_sums")
        mod_full, mrow_ready = sem("mod_full"), sem("mrow_ready")
        mod_free = sem("mod_free")
        dve_step = sem("dve_step")
        silc_ready, idr_ready, pads_ready = map(sem, ("silc_ready", "idr_ready", "pads_ready"))
        xz_ready, hf_ready = sem("xz_ready"), sem("hf_ready")
        tmp_ready, ah_ready, al_ready = map(sem, ("tmp_ready", "ah_ready", "al_ready"))
        ctx_tmp, cxh_ready, cxl_ready = map(sem, ("ctx_tmp", "cxh_ready", "cxl_ready"))
        kvh_ready, kvl_ready, rope_done = map(sem, ("kvh_ready", "kvl_ready", "rope_done"))
        st_h, st_l = sem("staged_hi"), sem("staged_lo")
        s_full = [sem(f"scores_full{i}") for i in range(2)]
        nm_ready = sem("max_ready")
        p_ready = [sem(f"probs_ready{i}") for i in range(2)]
        pt_full, pth_ready, ptl_ready, av_done = map(sem, ("pt_full", "pth_ready", "ptl_ready", "av_done"))
        es_ready, pr_ready, oh_ready, ol_ready = map(sem, ("es_ready", "pr_ready", "oh_ready", "ol_ready"))
        z_ready, sq_ready, stats_in, stats_full, m2_ready, var_ready, sd_ready = map(sem, (
            "z_ready", "sq_ready", "stats_in", "stats_full", "m2_ready", "var_ready", "sd_ready"))
        sg_ready, f_ready, fh_ready, fl_ready = map(sem, ("silu_ready", "f_ready", "fh_ready", "fl_ready"))
        cs_ready, yc_ready = sem("cs_ready"), sem("yc_ready")
        lg_full, mask_ready, pos_full, gate_in, gate_exp = map(sem, (
            "logits_full", "choice_ready", "pos_full", "gate_in", "gate_exp"))
        tr_full, tr_free = sem("rows_full"), sem("rows_free")
        dest_ready, routed = sem("dest_ready"), sem("routed")
        zero_ready, zeroed, scattered = sem("zero_ready"), sem("zeroed"), sem("scattered")
        ht_full = sem("ht_full")
        xg_in, xt_full, xth_ready, xtl_ready = map(sem, ("xg_in", "xt_full", "xth_ready", "xtl_ready"))
        se_ready, he_ready, hh_ready, hl_ready = map(sem, ("se_ready", "he_ready", "hh_ready", "hl_ready"))
        y_zero, ys_a, ys_b, ys_free, y_out = map(sem, ("y_zero", "ys_a", "ys_b", "ys_free", "y_out"))
        y_done, pool_turn = sem("expert_y_done"), sem("pool_turn")
        dg_ready, g2_full, g2_ready = sem("dg_ready"), sem("g2_full"), sem("g2_ready")
        yg_in = [sem(f"yg_in{i}") for i in range(2)]
        yg_free = sem("yg_free")
        z_part, n_ready, zg_ready, out_last = map(sem, ("z_part", "n_ready", "zg_ready", "out_last"))
        v_ready, sdf_ready, out_ready, out_done = map(sem, ("v_ready", "sdf_ready", "out_ready", "out_done"))

        def sm(name):
            a, b = SM[name]
            return SMALL[:, a:b]

        ident = sm("ident")
        mean_w = sm("mean")
        bmod = sm("bmod").rearrange("p (v t) -> p v t", v=2)
        lng = sm("lng").rearrange("p (s k) -> p s k", s=4)
        lnb = sm("lnb").rearrange("p (s k) -> p s k", s=4)
        cw = sm("cw").rearrange("p (j k) -> p j k", j=3)
        wr = sm("wr").rearrange("p (k e) -> p k e", k=KD)
        ones = RT[:, 0:P]
        upper = RT[:, P:2 * P]

        def scores_view(b):
            return PS[:, 2 * b:2 * b + 2, :].rearrange("p b n -> p (b n)")[:, 512 - CTX:512 + WIN]

        def raw8(s):
            return RAW[s][:].rearrange("p (k n) -> p k n", k=KD)

        def modcol(layer, chunk):
            a = layer * 48 + chunk * 8
            return MOD[:, 0, a:a + 8]

        def ring_per(units):
            per = {}
            for r in SLOT[units]:
                for key in ("raw", "hs", "ud"):
                    per[(key, r)] = per.get((key, r), 0) + 1
            return per

        MOE_BODY = [(p, p % 3) for p in range(6)]
        PER_EXP_RING = {}
        for r_, h_ in MOE_BODY:
            PER_EXP_RING[("raw", r_)] = PER_EXP_RING.get(("raw", r_), 0) + 1
            PER_EXP_RING[("hs", h_)] = PER_EXP_RING.get(("hs", h_), 0) + 1
            PER_EXP_RING[("ud", h_)] = PER_EXP_RING.get(("ud", h_), 0) + 1

        def times(per, n):
            return {k: v * n for k, v in per.items()}

        def plus_ahead(per):
            per = dict(per)
            for r, h in MOE_BODY[:2]:
                for key in (("raw", r), ("hs", h), ("ud", h)):
                    if key in per:
                        per[key] += 1
            return per

        def pt_view():
            return PS[:, 4:6, :].rearrange("p b n -> p (b n)")[:, 0:NKEY].rearrange("p (c n) -> p c n", n=BLK)

        def out_view(g, f):
            return PS[HD * f:HD * f + HD, 6 + g % 2, :].rearrange("p (j f n) -> p j f n", j=2, f=2)[:, :, f, :]

        def attention_act(act):
            act.preload_act_table(ACT.Exp)
            with act.Fori(0, NBLK) as b:
                act.wait_ge(rope_done, 10)
                act.wait_ge(st_l, b + 1)
                act.activation(QSH[:], Q[:, :, bass.ds(b * BLK, BLK)], ACT.Copy).then_inc(st_h, 1)
                act.activation(KSH[:], K[:, :, bass.ds(b * BLK, WIN)], ACT.Copy).then_inc(st_h, 1)
                act.activation(VSH[:], VH[:, bass.ds(b, 3), :].bitcast(F32), ACT.Copy).then_inc(st_h, 1)
                for h in range(NH + 5):
                    if 2 <= h < NH + 2:
                        o = h - 2
                        act.wait_ge(pt_full, b * NH + (o + 1))
                        if o >= 4:
                            act.wait_ge(av_done, b * (NH // 2) + (o // 2 - 1))
                        act.activation(PTH[o // 2 % 2][:, :, o % 2, :], pt_view(), ACT.Copy).then_inc(pth_ready, 1)
                    if h < NH:
                        act.wait_ge(nm_ready, b * NH + (h + 1))
                        if h >= 3:
                            act.wait_ge(pt_full, b * NH + (h - 2))
                        act.activation(PR[h % 3][:], scores_view(h % 2), ACT.Exp, bias=NM[:, h:h + 1], scale=SCALE,
                                       accum_out=LSUM[:, h:h + 1]).then_inc(p_ready[h % 2], 1)
                        act.activation(ES[:, h:h + 1], NM[:, h:h + 1], ACT.Exp,
                                       bias=SMALL[:, SM["sink"][0] + h:SM["sink"][0] + h + 1]).then_inc(es_ready, 1)
                    if h % 4 == 0 and h >= 8:
                        g = h // 4 - 2
                        act.wait_ge(av_done, b * (NH // 2) + (2 * g + 2))
                        for f in range(2):
                            ins = act.activation(AH[HD * f:HD * f + HD, 2 * g:2 * g + 2, bass.ds(b * BLK, BLK)],
                                                 out_view(g, f), ACT.Copy)
                        ins.then_inc(oh_ready, 1)

        def attention_dve(dve, t):
            dve.sem_inc(st_l, 1)
            with t.loop(dve, NBLK, {"step": ATT_STEPS}) as b:
                dve.wait_ge(rope_done, 10)
                dve.wait_ge(st_h, b * 3 + 1)
                dve.tensor_tensor(QSL[:], Q[:, :, bass.ds(b * BLK, BLK)], QSH[:].bitcast(F32), ALU.subtract)
                dve.wait_ge(st_h, b * 3 + 2)
                dve.tensor_tensor(KSL[:], K[:, :, bass.ds(b * BLK, WIN)], KSH[:].bitcast(F32), ALU.subtract)
                dve.wait_ge(st_h, b * 3 + 3)
                dve.tensor_copy(VSL[:], VL[:, bass.ds(b, 3), :].bitcast(F32)).then_inc(kvl_ready, 1)

                def link(ins):
                    ins.then_inc(dve_step, 1)
                    dve.wait_ge(dve_step, t.n("step"))

                for h in range(NH + 6):
                    if h < NH:
                        dve.wait_ge(s_full[h % 2], b * (NH // 2) + (h // 2 + 1))
                        link(dve.tensor_reduce(NRM[:, h:h + 1], scores_view(h % 2), AX.X, ALU.max, negate=True))
                        dve.scalar_tensor_tensor(out=NM[:, h:h + 1], in0=NRM[:, h:h + 1], scalar=SCALE,
                                                 in1=NSINK[:, h:h + 1], op0=ALU.mult, op1=ALU.min).then_inc(nm_ready, 1)
                    if 1 <= h < NH + 1:
                        o = h - 1
                        dve.wait_ge(es_ready, b * NH + (o + 1))
                        link(dve.tensor_tensor(RS[:, o:o + 1], LSUM[:, o:o + 1], ES[:, o:o + 1], ALU.add))
                        link(dve.reciprocal(RS[:, o:o + 1], RS[:, o:o + 1]))
                        dve.tensor_scalar(PR[o % 3][:], PR[o % 3][:], RS[:, o:o + 1], None,
                                          ALU.mult).then_inc(pr_ready, 1)
                    if 2 <= h < NH + 2:
                        o = h - 2
                        dve.wait_ge(pth_ready, b * NH + (o + 1))
                        dve.tensor_tensor(PTL[o // 2 % 2][:, :, o % 2, :], pt_view(),
                                          PTH[o // 2 % 2][:, :, o % 2, :].bitcast(F32), ALU.subtract).then_inc(ptl_ready, 1)
                    if h % 4 == 1 and h >= 9:
                        g = h // 4 - 2
                        dve.wait_ge(oh_ready, b * 4 + (g + 1))
                        for f in range(2):
                            rows_ = slice(HD * f, HD * f + HD)
                            at = (rows_, slice(2 * g, 2 * g + 2), bass.ds(b * BLK, BLK))
                            ins = dve.tensor_tensor(AL[at], out_view(g, f), AH[at].bitcast(F32), ALU.subtract)
                        ins.then_inc(ol_ready, 1)
                dve.wait_ge(ol_ready, b * 4 + 4)
                dve.sem_inc(st_l, 1)

        def attention_pe(pe, three):
            pe.wait_ge(idr_ready, 2)
            with pe.Fori(0, NBLK) as b:
                pe.wait_ge(kvl_ready, b + 1)
                for h in range(NH + 4):
                    if h < NH:
                        f, j = h % 2, h // 2
                        kp = j // 4
                        rows_ = slice(HD * f, HD * f + HD)
                        if h >= 2:
                            pe.wait_ge(p_ready[f], b * (NH // 2) + h // 2)
                        wh, wl = QSH[rows_, j, :], QSL[rows_, j, :]
                        three(PS[:, 2 * f, 512 - CTX:512], wh, wl, KCH[rows_, kp, :], KCL[rows_, kp, :], True, True)
                        three(PS[:, 2 * f + 1, 0:WIN], wh, wl, KSH[rows_, kp, :], KSL[rows_, kp, :], True, False)
                        edge = PS[:, 2 * f + 1, 0:WIN].rearrange("p (c n) -> p c n", c=3)[:, 0:3:2, :]
                        pe.matmul(edge, IDR[:], MASK[:, bass.ds(b, 1), :].rearrange("p o (c n) -> p (o c) n", c=2),
                                  start=False, stop=True, skip_group_check=True).then_inc(s_full[f], 1)
                    if 2 <= h < NH + 2:
                        o = h - 2
                        pe.wait_ge(pr_ready, b * NH + (o + 1))
                        if o >= 1:
                            pe.wait_ge(ptl_ready, b * NH + o)
                        for c in range(5):
                            ins = pe.transpose(PS[:, 4 + c // 4, (c % 4) * P:(c % 4 + 1) * P],
                                               PR[o % 3][:, c * P:(c + 1) * P], ident)
                        ins.then_inc(pt_full, 1)
                    if h >= 4:
                        p = h // 2 - 2
                        if h % 2 == 0:
                            pe.wait_ge(ptl_ready, b * NH + (2 * p + 2))
                        if h % 4 == 0 and p >= 4:
                            pe.wait_ge(ol_ready, b * 4 + (p // 2 - 1))
                        cols_ = slice((p // 4) * P, (p // 4) * P + P)
                        outp = PS[:, 6 + p // 2 % 2, (p % 2) * 256:(p % 2) * 256 + 256]
                        for c in (range(3) if h % 2 == 0 else range(3, 5)):
                            vh = VCH[:, c, cols_] if c < 2 else VSH[:, c - 2, cols_]
                            vl = VCL[:, c, cols_] if c < 2 else VSL[:, c - 2, cols_]
                            ins = three(outp, vh, vl, PTH[p % 2][:, c].rearrange("p f n -> p (f n)"),
                                        PTL[p % 2][:, c].rearrange("p f n -> p (f n)"), c == 0, c == 4)
                        if h % 2:
                            ins.then_inc(av_done, 1)

        block = ctx.enter_context(nc.Block())

        @block.sync
        def _(sp):
            t = Turns()
            sp.dma_start(SMALL[:], small).then_inc(small_in, 16)

            def load(slot, src):
                sp.wait_ge(raw_used[slot], t.n(("raw", slot)))
                sp.dma_start(RAW[slot][:], src).then_inc(raw_loaded[slot], 16)

            with t.loop(sp, 2, {("raw", r): 1 for r in range(4)}) as i:
                for r in range(4):
                    load(r, w_mod[bass.ds(i * 4 + r, 1), :, :].rearrange("o p n -> (o p) n"))
            sp.dma_start(COS[:], rope[:, 0:T]).then_inc(rope_in, 16)
            sp.dma_start(SIN[:], rope[:, T:2 * T]).then_inc(rope_in, 16)
            u0 = 0
            for name, count, units in SEGMENTS:
                per = {k: v for k, v in ring_per(units).items() if k[0] == "raw"}
                if count > 1:
                    with t.loop(sp, count, per) as i:
                        for j, r in enumerate(SLOT[units]):
                            load(r, w_pre[bass.ds(i * units + (u0 + j), 1), :, :].rearrange("o p n -> (o p) n"))
                else:
                    for j, r in enumerate(SLOT[units]):
                        load(r, w_pre[u0 + j])
                u0 += count * units
            t.skip(("raw", 3), 1)

            per_g = {("raw", r): 1 for r, _ in MOE_BODY}

            def unit(i):
                return w_moe[bass.ds(i, 1), :, :].rearrange("o p n -> (o p) n") if not isinstance(i, int) else w_moe[i]

            def group(first):
                for j in range(2, 8):
                    load(j % 6, unit(first + j))

            for j in range(4):
                load(j, unit(j))
            sp.wait_ge(routed, 1)
            sp.wait_ge(scattered, 16 * 8)
            for j in range(4, 8):
                load(j % 6, unit(j))
            with t.loop(sp, GROUPS - 1, per_g, 1) as g:
                group(g * 6)
            with t.loop(sp, NE - 1, times(per_g, GROUPS), 1) as e:
                with t.loop(sp, GROUPS, per_g) as g:
                    group(e * (6 * GROUPS) + g * 6)
            n_over = sp.value_load(RI[0:1, 11:12], min_val=0, max_val=MAX_OVER)
            with sp.If(n_over > 0):
                per_x = times(per_g, GROUPS)
                per_x[("raw", 0)] += 1
                per_x[("raw", 1)] += 1
                with t.loop(sp, n_over, per_x) as x:
                    e = sp.value_load(RI[0:1, bass.ds(x + 8, 1)], min_val=0, max_val=NE - 1)
                    for j in range(2):
                        load(j, unit(e * (6 * GROUPS) + j))
                    with t.loop(sp, GROUPS, per_g) as g:
                        group(e * (6 * GROUPS) + g * 6)

            sp.wait_ge(y_done, 1)
            sp.dma_start(LNR[:], lnrow.rearrange("p (a n) -> p a n", a=2)).then_inc(lnr_in, 16)
            outv = out[0].rearrange("(t p) d -> t p d", p=P)
            for i in range(4):
                sp.wait_ge(out_ready, i + 1) if i < 3 else sp.wait_ge(out_last, 1)
                sp.dma_start(outv[i], ZF[i][:]).then_inc(out_done, 16)
            sp.wait_ge(out_done, 64)

        @block.gpsimd
        def _(pool):
            pool.dma_start(XZ[:], xT_in).then_inc(xin, 16)
            pool.dma_start(CX[:], ctxT_in).then_inc(cxin, 16)
            pool.dma_start(MASKF[:], maskin).then_inc(mask_in, 16)
            pool.wait_ge(silc_ready, 1)
            silc = SILC[:, :, 0:1].to_broadcast([P, KD, 256])

            def batch(n, sums, buf):
                if n == 1:
                    pool.wait_ge(raw_used[3], 3)
                if n:
                    pool.wait_ge(mod_full, 2 + n)
                with pool.Fori(0, MOD_B) as i:
                    done = i + n * MOD_B
                    src = w_mod[bass.ds(i + (MOD_A + n * MOD_B), 1), :, :].rearrange("o p n -> (o p) n")
                    pool.dma_start(buf[:], src).then_inc(modw_in, 16)
                    pool.wait_ge(modw_in, done * 16 + 16)
                    w = buf[:].rearrange("p (k n) -> p k n", k=KD)
                    pool.tensor_tensor(w, w, silc, ALU.mult).then_inc(pool_step, 1)
                    pool.wait_ge(pool_step, done * 4 + 1)
                    pool.tensor_tensor(w[:, 0:4], w[:, 0:4], w[:, 4:8], ALU.add).then_inc(pool_step, 1)
                    pool.wait_ge(pool_step, done * 4 + 2)
                    pool.tensor_tensor(w[:, 0:2], w[:, 0:2], w[:, 2:4], ALU.add).then_inc(pool_step, 1)
                    pool.wait_ge(pool_step, done * 4 + 3)
                    pool.tensor_tensor(sums[:, bass.ds(i, 1), :], w[:, 0:1, :], w[:, 1:2, :],
                                       ALU.add).then_inc(pool_step, 1)
                    pool.wait_ge(pool_step, done * 4 + 4)
                    pool.sem_inc(mod_sums, 1)

            batch(0, MSA, MW)
            batch(1, MSA, RAW[3])
            pool.wait_ge(ol_ready, 4 * NBLK)
            pool.dma_start(RT[:], rconst).then_inc(rc_in, 16)
            pool.wait_ge(zero_ready, 1)
            with pool.Fori(0, N_ROWS // P) as a:
                pool.dma_start(xg_d[bass.ds(a * P, P), :], ZT[:]).then_inc(zeroed, 16)
            with pool.Fori(NE * CAP // P, N_ROWS // P) as a:
                pool.dma_start(yg_d[bass.ds(a * P, P), :], ZT[:]).then_inc(zeroed, 16)
            for n in range(2, N_MODB):
                batch(n, MSB, RAW[3])
            pool.sem_inc(raw_used[3], 1)
            pool.wait_ge(zeroed, 16 * (N_ROWS + MAX_OVER * CAP) // P)
            pool.wait_ge(dest_ready, 1)
            pool.wait_ge(tr_free, 4)
            for c in range(2):
                for i in range(4):
                    pool.indirect_dma_start(xg_d[:, :], bass.IndirectOffsetOnAxis(ap=DI[:, c, i:i + 1], axis=0),
                                            HT[:, i, :], None).then_inc(scattered, 16)
            pool.wait_ge(scattered, 16 * 8)

            def rows(buf, i):
                at = slice(i * CAP, (i + 1) * CAP) if isinstance(i, int) else bass.ds(i * CAP, CAP)
                return buf[at, :].rearrange("(s p) n -> p s n", p=P)

            def store(i, n):
                pool.wait_ge(ys_a, n + 1)
                pool.wait_ge(ys_b, n + 1)
                pool.sem_inc(pool_turn, 1)
                pool.dma_start(rows(yg_d, i), YS[:]).then_inc(y_out, 16)
                pool.wait_ge(y_out, n * 16)
                pool.sem_inc(ys_free, 1)

            pool.wait_ge(routed, 1)
            pool.dma_start(XG[:], rows(xg_d, 0)).then_inc(xg_in, 16)
            with pool.Fori(0, NE - 1) as e:
                pool.wait_ge(xt_full, e * 4 + 4)
                pool.sem_inc(pool_turn, 1)
                pool.dma_start(XG[:], rows(xg_d, e + 1)).then_inc(xg_in, 16)
                store(e, e + 1)
            store(NE - 1, NE)
            n_over = pool.value_load(RI[0:1, 11:12], min_val=0, max_val=MAX_OVER)
            with pool.If(n_over > 0):
                with pool.Fori(0, n_over) as x:
                    pool.dma_start(XG[:], rows(xg_d, x + NE)).then_inc(xg_in, 16)
                    store(x + NE, x + (NE + 1))
            pool.sem_inc(y_done, 1)
            for i in range(4):
                if i >= 2:
                    pool.wait_ge(yg_free, i - 1)
                for c in range(2):
                    pool.indirect_dma_start(YG[i % 2][c][:, :], None, yg_d[:, :],
                                            bass.IndirectOffsetOnAxis(ap=DI[:, c, i:i + 1], axis=0)
                                            ).then_inc(yg_in[i % 2], 16)
            pool.wait_ge(lnr_in, 16)
            for i in range(3):
                pool.wait_ge(n_ready, i + 1)
                pool.tensor_tensor(ZF[i][:], ZF[i][:], LNR[:, 0, :], ALU.mult).then_inc(zg_ready, 1)
                pool.wait_ge(zg_ready, i + 1)
                pool.tensor_tensor(ZF[i][:], ZF[i][:], LNR[:, 1, :], ALU.add).then_inc(out_ready, 1)

        @block.scalar
        def _(act):
            t = Turns()
            def full_split(r, h):
                act.wait_ge(raw_loaded[r], t.n(("raw", r)) * 16)
                act.wait_ge(unit_done[h], t.n(("hs", h)))
                act.activation(HI[h][:], RAW[r][:], ACT.Copy).then_inc(hi_ready[h], 1)

            def done(h):
                act.wait_ge(unit_done[h], t.n(("ud", h)) + 1)

            for s in raw_used:
                act.sem_inc(s, 1)
            for s in unit_done:
                act.sem_inc(s, 1)
            for s in pair_free:
                act.sem_inc(s, 1)
            act.sem_inc(mod_free, 1)
            act.sem_inc(ys_free, 1)
            act.sem_inc(ys_a, 1)
            act.wait_ge(small_in, 16)
            act.activation(SILC[:].rearrange("p k v -> p (k v)"), sm("cc"), ACT.Silu).then_inc(silc_ready, 1)
            act.activation(IDR[:], ident, ACT.Copy).then_inc(idr_ready, 1)
            act.wait_ge(mask_in, 16)
            act.activation(MASK[:], MASKF[:], ACT.Copy).then_inc(idr_ready, 1)

            for half in range(2):
                act.wait_ge(raw_used[3], half + 2)
                act.activation(MROW[0:2, half * 1024:(half + 1) * 1024].rearrange("p (b n) -> p b n", b=2),
                               PS[0:2, 2 * half:2 * half + 2, :], ACT.Copy).then_inc(mrow_ready, 1)

            cnt = {"tmp": 0}

            def to_hi(k):
                cnt["tmp"] += 1
                act.wait_ge(tmp_ready, cnt["tmp"])
                act.activation(AH[:, k, :], TMP[k % 2][:], ACT.Copy).then_inc(ah_ready, 1)

            def scale_x(stage, k):
                act.activation(XZ[:, k, :], XZ[:, k, :], ACT.Identity, bias=COEF[:, stage, 3, k:k + 1],
                               scale=COEF[:, stage, 2, k:k + 1]).then_inc(xz_ready, 1)

            act.wait_ge(idr_ready, 2)
            for k in range(KD):
                act.wait_ge(ctx_tmp, k + 1)
                act.activation(CXH[:, k, :], TMP[k % 2][:, 0:CTX], ACT.Copy).then_inc(cxh_ready, 1)
            for k in range(KD):
                to_hi(k)

            def layer_norm(stage):
                act.wait_ge(stats_full, stage)
                act.activation(M2[:], PS[:, 6, :], ACT.Square).then_inc(m2_ready, 1)
                act.wait_ge(var_ready, stage)
                act.activation(RSTD[:], VAR[:], ACT.Sqrt).then_inc(sd_ready, 1)

            zc = [0]

            def square(k):
                zc[0] += 1
                act.wait_ge(z_ready, zc[0])
                act.activation(SQ[k % 2][:], XZ[:, k, :], ACT.Square).then_inc(sq_ready, 1)

            fl = {"n": 0}
            for r in range(4):
                t.skip(("raw", r), 2)
            full_split(0, 0)
            for name, count, units in SEGMENTS:
                svs = SLOT[units]
                ns = units
                if name[:2] == "up":
                    f0 = fl["n"]
                    act.preload_act_table(ACT.Silu)
                    with t.loop(act, count, ring_per(units)) as i:
                        for j, h in enumerate(svs):
                            nx = svs[(j + 1) % ns]
                            full_split(nx, nx)
                            done(h)
                            b = j % 2
                            act.activation(SG[b][:], PS[:, 2 * b, :], ACT.Silu).then_inc(sg_ready, 1)
                            act.wait_ge(f_ready, i * ns + (f0 + j + 1))
                            act.activation(FH[:, bass.ds(i * ns + j, 1), :].rearrange("p o n -> p (o n)"),
                                           TMP[b][:], ACT.Copy).then_inc(fh_ready, 1)
                    fl["n"] += count * ns
                    continue
                if name == "conv":
                    with t.loop(act, count, ring_per(units)) as i:
                        for j, h in enumerate(svs):
                            nx = svs[(j + 1) % ns]
                            full_split(nx, nx)
                            done(h)
                            if j == 0:
                                act.activation(CS[:], PS[:, 0:2, :], ACT.Copy).then_inc(cs_ready, 1)
                            elif j == 2:
                                act.wait_ge(yc_ready, i + 1)
                                act.activation(FH[:, bass.ds(i * 2, 2), :], TM2[:], ACT.Copy).then_inc(fh_ready, 1)
                    continue
                if name == "q":
                    with t.loop(act, count, ring_per(units)) as i:
                        for j, h in enumerate(svs):
                            nx = svs[(j + 1) % ns]
                            full_split(nx, nx)
                            done(h)
                    attention_act(act)
                    continue
                for j, h in enumerate(svs):
                    if name != "co" or j + 1 < ns:
                        nx = svs[(j + 1) % ns]
                        full_split(nx, nx)
                    done(h)
                    if name == "kv" and j == 0:
                        act.activation(KCH[:].rearrange("p a n -> p (a n)"), PS[:, 2, :], ACT.Copy).then_inc(kvh_ready, 1)
                    if name == "kv" and j == 1:
                        act.activation(VCH[:].rearrange("p a n -> p (a n)"), PS[:, 3, :], ACT.Copy).then_inc(kvh_ready, 1)
                        act.activation(VH[:, 1:5, :].rearrange("p (b a) n -> p b (a n)", b=2), PS[:, 4:6, :],
                                       ACT.Copy).then_inc(kvh_ready, 1)
                    if name in ("o", "dn2", "co"):
                        square(2 * j)
                        square(2 * j + 1)
                if name in ("o", "dn2"):
                    layer_norm({"o": 1, "dn2": 2}[name])
                    for k in range(KD):
                        to_hi(k)
                        scale_x({"o": 1, "dn2": 2}[name], k)
                if name == "co":
                    layer_norm(3)
                    for k in range(KD):
                        act.wait_ge(tmp_ready, cnt["tmp"] + k + 1)
                        act.activation(HF[:, k, :], XZ[:, k, :], ACT.Identity, bias=COEF[:, 3, 1, k:k + 1],
                                       scale=COEF[:, 3, 0, k:k + 1]).then_inc(hf_ready, 1)
                        act.wait_ge(hf_ready, k + 1)
                        scale_x(3, k)

            for r, h in MOE_BODY[:2]:
                full_split(r, h)
            act.wait_ge(gate_in, 1)
            act.activation(DD[:, 1, :], DD[:, 0, :], ACT.Exp).then_inc(gate_exp, 1)
            for i in range(8):
                act.wait_ge(tr_full, i + 1)
                dst = HT[:, i, :] if i < 4 else XR[:, i - 4, :]
                act.activation(dst.rearrange("p (b n) -> p b n", b=2), PS[:, 2 + 2 * (i % 2):4 + 2 * (i % 2), :],
                               ACT.Copy).then_inc(tr_free, 1)
            act.wait_ge(tr_free, 8)
            act.sem_inc(pair_free[1], 1)
            act.sem_inc(pair_free[2], 1)

            per_g = dict(times(PER_EXP_RING, 1))
            per_g.update({"ht": 2})
            act.wait_ge(routed, 1)

            def expert_round(r):
                act.preload_act_table(ACT.Silu)
                for q in range(4):
                    act.wait_ge(xt_full, r * 4 - (3 - q))
                    act.activation(XTH[:, 2 * q:2 * q + 2, :].rearrange("p k n -> p (k n)"), PS[:, q, :],
                                   ACT.Copy).then_inc(xth_ready, 1)
                with t.loop(act, GROUPS, per_g):
                    for j, (_, h) in enumerate(MOE_BODY):
                        full_split(*MOE_BODY[(j + 2) % 6])
                        if j != 4:
                            done(h)
                        if j in (0, 2):
                            act.activation(SE[:, j // 2, :], PS[:, j, :], ACT.Silu).then_inc(se_ready, 1)
                        if j in (2, 4):
                            q = j // 2 - 1
                            act.wait_ge(ht_full, t.n("ht"))
                            act.activation(HH[:, q].rearrange("p a n -> p (a n)"), PS[:, 2 * q, :],
                                           ACT.Copy).then_inc(hh_ready, 1)
                        if j == 4:
                            done(h)
                act.wait_ge(ys_free, r)
                act.activation(YS[:, 0, :].rearrange("p (b n) -> p b n", b=2), PS[:, 4:6, :], ACT.Copy).then_inc(ys_a, 1)

            def ahead():
                for r, h in MOE_BODY[:2]:
                    full_split(r, h)

            def unused():
                for _, h in MOE_BODY[:2]:
                    t.skip(("ud", h), 1)

            per_e = times(per_g, GROUPS)
            with t.loop(act, NE, per_e) as e:
                expert_round(e + 1)
            unused()
            n_over = act.value_load(RI[0:1, 11:12], min_val=0, max_val=MAX_OVER)
            with act.If(n_over > 0):
                per_x = plus_ahead(per_e)
                with t.loop(act, n_over, per_x) as x:
                    ahead()
                    expert_round(x + (NE + 1))
                    unused()

            act.wait_ge(g2_full, 1)
            act.activation(G2R[:].rearrange("p (b n) -> p b n", b=2), PS[:, 0:2, :], ACT.Copy).then_inc(g2_ready, 1)
            for i in range(4):
                act.wait_ge(yg_in[i % 2], 32 * (i // 2 + 1))
                act.activation(ZF[i][:], YG[i % 2][0][:], ACT.Copy, scale=GA[:, 0, i:i + 1]).then_inc(z_part, 1)
                act.wait_ge(v_ready, i + 1)
                act.activation(BAG[:, 3:4], BAG[:, 2:3], ACT.Sqrt).then_inc(sdf_ready, 1)

        @block.vector
        def _(dve):
            t = Turns()

            def step(ins):
                ins.then_inc(dve_step, 1)
                dve.wait_ge(dve_step, t.n("step"))

            def split(r, h):
                dve.wait_ge(hi_ready[h], t.n(("hs", h)))
                dve.tensor_tensor(LO[h][:], RAW[r][:], HI[h][:].bitcast(F32), ALU.subtract).then_inc(raw_used[r], 1)

            def done(h):
                dve.wait_ge(unit_done[h], t.n(("ud", h)) + 1)

            mf = [1]

            def mod_batch(n):
                cols_ = slice(2 * (MOD_A + n * MOD_B), 2 * (MOD_A + (n + 1) * MOD_B))
                dve.wait_ge(mod_full, t.n("mod"))
                dve.scalar_tensor_tensor(out=MOD[:, 0, cols_], in0=PS[:, 7, 0:2 * MOD_B], scalar=float(D),
                                         in1=bmod[:, 0, cols_], op0=ALU.mult, op1=ALU.add).then_inc(mod_free, 1)
                mf[0] += 1

            dve.memset(K[:, :, 0:BLK], 0.0)
            dve.memset(K[:, :, BLK + T:], 0.0)
            step(dve.memset(ROT[:], 0.0))
            dve.tensor_copy(VH[:, 0, :], ROT[:, 0:256])
            dve.tensor_copy(VH[:, 5, :], ROT[:, 0:256])
            dve.tensor_copy(VL[:, 0, :], ROT[:, 0:256])
            dve.tensor_copy(VL[:, 5, :], ROT[:, 0:256]).then_inc(pads_ready, 1)
            dve.wait_ge(small_in, 16)
            step(dve.tensor_scalar(NSINK[:], sm("sink"), -1.0, None, ALU.mult))
            for half in range(2):
                cols_ = slice(half * KD, (half + 1) * KD)
                dve.wait_ge(mod_full, t.n("mod"))
                dve.tensor_tensor(MOD[:, :, cols_], PS[:, 7, 0:2 * KD].rearrange("p (t v) -> p v t", v=2),
                                  bmod[:, :, cols_], ALU.add).then_inc(mod_free, 1)
            mf[0] += 2
            dve.wait_ge(mod_free, mf[0])
            dve.tensor_scalar(COEF[:, 0, 0, :], modcol(0, 1), 1.0, None, ALU.add)
            step(dve.tensor_scalar(CG[:], MOD[:, 1, 8:16], 1.0, None, ALU.add))
            dve.wait_ge(cxin, 16)
            for k in range(KD):
                if k >= 2:
                    dve.wait_ge(cxl_ready, k - 1)
                dve.tensor_scalar(TMP[k % 2][:, 0:CTX], CX[:, k, :], CG[:, k:k + 1], MOD[:, 1, k:k + 1],
                                  ALU.mult, ALU.add).then_inc(ctx_tmp, 1)
                dve.wait_ge(ctx_tmp, k + 1)
                dve.wait_ge(cxh_ready, k + 1)
                dve.tensor_tensor(CXL[:, k, :], TMP[k % 2][:, 0:CTX], CXH[:, k, :].bitcast(F32),
                                  ALU.subtract).then_inc(cxl_ready, 1)

            nt = [0]

            def modulate(stage, shift, n_of):
                for k in range(KD):
                    n_of(k)
                    nt[0] += 1
                    if nl[0]:
                        dve.wait_ge(al_ready, nl[0])
                    dve.tensor_scalar(TMP[k % 2][:], XZ[:, k, :], COEF[:, stage, 0, k:k + 1], shift[:, k:k + 1],
                                      ALU.mult, ALU.add).then_inc(tmp_ready, 1)
                    if k >= 1:
                        low(k - 1)
                    if stage == 0:
                        dve.wait_ge(tmp_ready, nt[0])
                        dve.tensor_scalar(XZ[:, k, :], XZ[:, k, :], ALPHA, None, ALU.mult)
                low(KD - 1)

            nl = [0]

            def low(k):
                nl[0] += 1
                dve.wait_ge(tmp_ready, nl[0])
                dve.wait_ge(ah_ready, nl[0])
                dve.tensor_tensor(AL[:, k, :], TMP[k % 2][:], AH[:, k, :].bitcast(F32),
                                  ALU.subtract).then_inc(al_ready, 1)

            dve.wait_ge(xin, 16)
            dve.wait_ge(cxl_ready, KD)
            modulate(0, MOD[:, 0, 0:8], lambda k: None)
            dve.wait_ge(al_ready, KD)

            def coefs(stage, ln, layer, ch_shift, ch_scale):
                c = COEF[:, stage]
                dve.wait_ge(mod_free, mf[0])
                g, b = lng[:, ln, :], lnb[:, ln, :]
                step(dve.tensor_scalar(c[:, 2, :], modcol(layer, ch_scale), 1.0, None, ALU.add))
                dve.tensor_tensor(c[:, 0, :], c[:, 2, :], g, ALU.mult)
                step(dve.tensor_tensor(c[:, 3, :], c[:, 2, :], b, ALU.mult))
                step(dve.tensor_tensor(c[:, 1, :], c[:, 3, :], modcol(layer, ch_shift), ALU.add))
                dve.tensor_scalar(c[:, 2, :], g, ALPHA, None, ALU.mult)
                step(dve.tensor_scalar(c[:, 3, :], b, ALPHA, None, ALU.mult))

            def norm_start(stage):
                dve.wait_ge(m2_ready, stage)
                dve.scalar_tensor_tensor(out=VAR[:], in0=PS[:, 7, :], scalar=EPS, in1=M2[:], op0=ALU.add,
                                         op1=ALU.subtract).then_inc(var_ready, 1)
                for k in range(4):
                    dve.tensor_tensor(XZ[:, k, :], XZ[:, k, :], PS[:, 6, :], ALU.subtract)
                dve.wait_ge(sd_ready, stage)
                step(dve.reciprocal(RSTD[:], RSTD[:]))
                for k in range(4, KD):
                    ins = dve.tensor_tensor(XZ[:, k, :], XZ[:, k, :], PS[:, 6, :], ALU.subtract)
                step(ins)

            def norm_k(k):
                step(dve.tensor_tensor(XZ[:, k, :], XZ[:, k, :], RSTD[:], ALU.mult))

            nz = [0]
            ns_ = [0]

            def residual(k, src, gate):
                return dve.scalar_tensor_tensor(out=XZ[:, k, :], in0=src, scalar=gate[:, k:k + 1], in1=XZ[:, k, :],
                                                op0=ALU.mult, op1=ALU.add)

            def sums(k):
                ns_[0] += 1
                if k == 0:
                    dve.wait_ge(z_ready, ns_[0])
                    dve.tensor_copy(ZS[:], XZ[:, 0, :])
                    dve.wait_ge(sq_ready, ns_[0])
                    step(dve.tensor_copy(QS[:], SQ[0][:]))
                else:
                    dve.tensor_tensor(ZS[:], ZS[:], XZ[:, k, :], ALU.add)
                    dve.wait_ge(sq_ready, ns_[0])
                    ins = dve.tensor_tensor(QS[:], QS[:], SQ[k % 2][:], ALU.add)
                    if k == KD - 1:
                        ins.then_inc(stats_in, 1)
                    else:
                        step(ins)

            split(0, 0)
            rot_mask = [(i + 16) % 32 for i in range(32)]

            def rope_tile(bank, dst, last_read_sem):
                n = t.n("rope")
                if not isinstance(n, int) or n > 1:
                    dve.wait_ge(rope_done, n - 1)
                dve.tensor_tensor(dst, PS[:, bank, :], COS[:], ALU.mult)
                ins = dve.stream_shuffle(ROT[:], PS[:, bank, :], rot_mask)
                if last_read_sem is not None:
                    ins.then_inc(last_read_sem, 1)
                    dve.wait_ge(last_read_sem, t.n(("rel", id(last_read_sem))) + 1)
                else:
                    step(ins)
                step(dve.tensor_tensor(ROT[:], ROT[:], SIN[:], ALU.mult))
                dve.tensor_tensor(dst, dst, ROT[:], ALU.add).then_inc(rope_done, 1)

            fl = [0]
            for name, count, units in SEGMENTS:
                svs = SLOT[units]
                ns = units
                ringp = {k: v for k, v in ring_per(units).items() if k[0] != "raw"}

                if name == "kv":
                    dve.wait_ge(rope_in, 32)
                    split(1, 1)
                    done(0)
                    dve.wait_ge(kvh_ready, 1)
                    dve.tensor_tensor(KCL[:].rearrange("p a n -> p (a n)"), PS[:, 2, :],
                                      KCH[:].rearrange("p a n -> p (a n)").bitcast(F32), ALU.subtract)
                    rope_tile(0, K[:, 0, BLK:BLK + T], None)
                    rope_tile(1, K[:, 1, BLK:BLK + T], pair_free[0])
                    split(0, 0)
                    done(1)
                    dve.wait_ge(kvh_ready, 2)
                    dve.tensor_tensor(VCL[:].rearrange("p a n -> p (a n)"), PS[:, 3, :],
                                      VCH[:].rearrange("p a n -> p (a n)").bitcast(F32),
                                      ALU.subtract).then_inc(pair_free[1], 1)
                    dve.wait_ge(kvh_ready, 3)
                    dve.tensor_tensor(VL[:, 1:5, :].rearrange("p (b a) n -> p b (a n)", b=2), PS[:, 4:6, :],
                                      VH[:, 1:5, :].rearrange("p (b a) n -> p b (a n)", b=2).bitcast(F32),
                                      ALU.subtract).then_inc(pair_free[2], 1)
                    t.n(("rel", id(pair_free[1])))
                elif name == "q":
                    per = dict(ringp)
                    per.update({"step": 6, "rope": 4, ("rel", id(pair_free[0])): 1, ("rel", id(pair_free[1])): 1})
                    with t.loop(dve, count, per) as i:
                        for j, h in enumerate(svs):
                            nx = svs[(j + 1) % ns]
                            split(nx, nx)
                            done(h)
                            pf = pair_free[j]
                            for c in range(2):
                                dst = Q[:, bass.ds(i * 4 + (2 * j + c), 1), :].rearrange("p o n -> p (o n)")
                                rope_tile(2 * j + c, dst, pf if c else None)
                    mod_batch(0)
                    attention_dve(dve, t)
                    dve.memset(ZT[:], 0.0).then_inc(zero_ready, 1)
                    mod_batch(1)
                    coefs(1, 0, 0, 3, 4)
                elif name[:2] == "up":
                    f0 = fl[0]
                    with t.loop(dve, count, ringp) as i:
                        for j, h in enumerate(svs):
                            nx = svs[(j + 1) % ns]
                            split(nx, nx)
                            done(h)
                            b = j % 2
                            n = i * ns + (f0 + j + 1)
                            dve.wait_ge(sg_ready, n)
                            dve.tensor_tensor(TMP[b][:], SG[b][:], PS[:, 2 * b + 1, :], ALU.mult).then_inc(f_ready, 1)
                            dve.wait_ge(f_ready, n)
                            dve.sem_inc(pair_free[b], 1)
                            dve.wait_ge(fh_ready, n)
                            fs = bass.ds(i * ns + j, 1)
                            dve.tensor_tensor(FL[:, fs, :].rearrange("p o n -> p (o n)"), TMP[b][:],
                                              FH[:, fs, :].rearrange("p o n -> p (o n)").bitcast(F32),
                                              ALU.subtract).then_inc(fl_ready, 1)
                            dve.wait_ge(fl_ready, n)
                    fl[0] += count * ns
                elif name == "conv":
                    dve.memset(UP[:, :, 0:1], 0.0)
                    step(dve.memset(UP[:, :, T + 1:T + 2], 0.0))
                    per = dict(ringp)
                    per.update({"step": 6})
                    with t.loop(dve, count, per) as i:
                        split(1, 1)
                        done(0)
                        step(dve.tensor_copy(CWG[:], cw[:, :, bass.ds(i * 2, 2)]))
                        split(2, 2)
                        done(1)
                        dve.wait_ge(cs_ready, i + 1)
                        step(dve.tensor_tensor(UP[:, :, 1:T + 1], PS[:, 2:4, :], CS[:], ALU.mult))
                        dve.sem_inc(pair_free[0], 1)
                        dve.sem_inc(pair_free[1], 1)
                        for c in range(2):
                            ins = dve.tensor_scalar(YC[:, c, :], UP[:, c, 0:T], CWG[:, 0, c:c + 1], None, ALU.mult)
                        step(ins)
                        for w_ in (1, 2):
                            for c in range(2):
                                ins = dve.scalar_tensor_tensor(out=YC[:, c, :], in0=UP[:, c, w_:w_ + T],
                                                               scalar=CWG[:, w_, c:c + 1], in1=YC[:, c, :],
                                                               op0=ALU.mult, op1=ALU.add)
                            step(ins)
                        split(0, 0)
                        done(2)
                        dve.tensor_tensor(TM2[:], PS[:, 4:6, :], YC[:], ALU.mult).then_inc(yc_ready, 1)
                        dve.wait_ge(yc_ready, i + 1)
                        dve.sem_inc(pair_free[2], 1)
                        dve.wait_ge(fh_ready, i + (fl[0] + 1))
                        step(dve.tensor_tensor(FL[:, bass.ds(i * 2, 2), :], TM2[:],
                                               FH[:, bass.ds(i * 2, 2), :].bitcast(F32), ALU.subtract))
                    dve.sem_inc(fl_ready, 1)
                else:
                    layer = 1 if name == "co" else 0
                    if name == "dn0":
                        mod_batch(2)
                        coefs(2, 1, 1, 0, 1)
                    if name == "dn2":
                        mod_batch(3)
                    if name == "co":
                        mod_batch(4)
                        coefs(3, 2, 1, 3, 4)
                    gate = modcol(layer, 2 if name in ("o", "co") else 5)
                    lastpart = name in ("o", "dn2", "co")
                    tiles = DOWN6 if name == "dn1" else [[2 * j, 2 * j + 1] for j in range(4)]
                    dve.wait_ge(mod_free, mf[0])
                    if name in ("dn0", "co"):
                        dve.wait_ge(xz_ready, KD if name == "dn0" else 2 * KD)
                    for j, h in enumerate(svs):
                        if name != "co" or j + 1 < ns:
                            nx = svs[(j + 1) % ns]
                            split(nx, nx)
                        done(h)
                        for k in tiles[j]:
                            bank = k % 4
                            ins = residual(k, PS[:, bank, :], gate)
                            if lastpart:
                                nz[0] += 1
                                ins.then_inc(z_ready, 1)
                                dve.wait_ge(z_ready, nz[0])
                                if k % 2:
                                    dve.sem_inc(pair_free[bank // 2], 1)
                                sums(k)
                            else:
                                step(ins)
                                if k % 2:
                                    dve.sem_inc(pair_free[bank // 2], 1)
                    if lastpart:
                        stage = {"o": 1, "dn2": 2, "co": 3}[name]
                        norm_start(stage)
                        dve.sem_inc(mod_free, 1)
                        mf[0] += 1
                        if stage < 3:
                            modulate(stage, COEF[:, stage, 1, :], norm_k)
                            dve.wait_ge(al_ready, nl[0])
                        else:
                            for k in range(KD):
                                dve.tensor_tensor(XZ[:, k, :], XZ[:, k, :], RSTD[:], ALU.mult).then_inc(tmp_ready, 1)

            for r, h in MOE_BODY[:2]:
                split(r, h)
            dve.wait_ge(lg_full, 1)
            dve.tensor_copy(LG[:, 0:2, :], PS[:, 0:2, 0:NE])
            step(dve.tensor_copy(LG[:, 2:4, :], PS[:, 6:8, 0:NE]))
            dve.sem_inc(pair_free[0], 1)
            for i in range(4):
                step(dve.max(MX[:, i, :], LG[:, i, :]))
                step(dve.max_index(IX[:, i, :], MX[:, i, :], LG[:, i, :]))
            step(dve.tensor_copy(IXF[:], IX[:, :, 0:2]))
            dve.wait_ge(rc_in, 16)
            for c in range(2):
                for i in range(4):
                    ins = dve.tensor_scalar(OH[:, c, i, :], RT[:, 256:264], IXF[:, i, c:c + 1], None, ALU.is_equal)
            step(ins)
            dve.tensor_tensor(MM[:], OH[:, 0], OH[:, 1], ALU.add).then_inc(mask_ready, 1)
            dve.tensor_tensor(DD[:, 0, :], MX[:, :, 1], MX[:, :, 0], ALU.subtract).then_inc(gate_in, 1)
            dve.wait_ge(gate_exp, 1)
            step(dve.tensor_scalar(DD[:, 2, :], DD[:, 1, :], 1.0, None, ALU.add))
            step(dve.reciprocal(GA[:, 0, :], DD[:, 2, :]))
            step(dve.tensor_tensor(GA[:, 1, :], DD[:, 1, :], GA[:, 0, :], ALU.mult))
            dve.wait_ge(pos_full, 1)
            step(dve.tensor_copy(RF[:, 0:8], PS[:, 0, 32:40]))
            step(dve.tensor_scalar(OV[:, 0, :], RF[:, 0:8], float(CAP), None, ALU.is_gt))
            step(dve.tensor_tensor_scan(OV[:, 1, :], RT[:, 0:8], OV[:, 0, :], 0.0, ALU.mult, ALU.add))
            step(dve.tensor_scalar(ADJ[:], OV[:, 1, :], float(CAP), float((NE - 2) * CAP), ALU.mult, ALU.add))
            dve.tensor_scalar(PT1[:].rearrange("p t e -> p (t e)"), PS[:, 0, 0:32], float(CAP), None, ALU.is_ge)
            step(dve.tensor_tensor(ADJ[:], ADJ[:], RT[:, 264:272], ALU.subtract))
            for i in range(4):
                dve.tensor_tensor(PB[:, i, :], PS[:, 0, 8 * i:8 * i + 8], RT[:, 264:272], ALU.add)
                ins = dve.tensor_tensor(PT1[:, i, :], PT1[:, i, :], ADJ[:], ALU.mult)
            step(ins)
            dve.sem_inc(pair_free[0], 1)
            step(dve.tensor_tensor(PB[:], PB[:], PT1[:], ALU.add))
            for c in range(2):
                step(dve.tensor_tensor(PT1[:], OH[:, c], PB[:], ALU.mult))
                step(dve.tensor_reduce(DF[:, c, :], PT1[:], AX.X, ALU.add))
            dve.tensor_copy(DI[:], DF[:]).then_inc(dest_ready, 1)
            step(dve.tensor_copy(RF[:, 11:12], OV[:, 1, 7:8]))
            for x in range(MAX_OVER):
                step(dve.tensor_scalar(OV[:, 2, :], OV[:, 1, :], float(x), None, ALU.is_le))
                step(dve.tensor_reduce(RF[:, 8 + x:9 + x], OV[:, 2, :], AX.X, ALU.add))
            step(dve.tensor_copy(RI[:, 0:12], RF[:, 0:12]))
            dve.wait_ge(tr_free, 8)
            dve.sem_inc(routed, 1)

            per_g = {k: v for k, v in PER_EXP_RING.items() if k[0] != "raw"}
            per_g.update({"se": 2, "hh": 2})

            def expert_round(r):
                for q in range(4):
                    dve.wait_ge(xth_ready, t.n("xth"))
                    dve.tensor_tensor(XTL[:, 2 * q:2 * q + 2, :].rearrange("p k n -> p (k n)"), PS[:, q, :],
                                      XTH[:, 2 * q:2 * q + 2, :].rearrange("p k n -> p (k n)").bitcast(F32),
                                      ALU.subtract).then_inc(xtl_ready, 1)
                dve.wait_ge(ys_a, r)
                dve.wait_ge(ys_b, r)
                dve.memset(PS[:, 4:8, :], 0.0).then_inc(y_zero, 1)
                with t.loop(dve, GROUPS, per_g):
                    for j, (_, h) in enumerate(MOE_BODY):
                        if j in (0, 2, 5):
                            split(*MOE_BODY[(j + 2) % 6])
                        if j != 4:
                            done(h)
                        if j in (1, 3):
                            q = j // 2
                            dve.wait_ge(se_ready, t.n("se"))
                            dve.tensor_tensor(HE[:, q, :], SE[:, q, :], PS[:, j, :], ALU.mult).then_inc(he_ready, 1)
                            split(*MOE_BODY[(j + 2) % 6])
                        if j in (2, 4):
                            q = j // 2 - 1
                            dve.wait_ge(hh_ready, t.n("hh"))
                            dve.tensor_tensor(HL[:, q].rearrange("p a n -> p (a n)"), PS[:, 2 * q, :],
                                              HH[:, q].rearrange("p a n -> p (a n)").bitcast(F32),
                                              ALU.subtract).then_inc(hl_ready, 1)
                        if j == 4:
                            split(*MOE_BODY[0])
                            done(h)
                dve.wait_ge(ys_free, r)
                dve.tensor_copy(YS[:, 1, :].rearrange("p (b n) -> p b n", b=2), PS[:, 6:8, :]).then_inc(ys_b, 1)

            def unused():
                for _, h in MOE_BODY[:2]:
                    t.skip(("ud", h), 1)

            per_e = times(per_g, GROUPS)
            per_e["xth"] = 4
            dve.sem_inc(ys_b, 1)
            with t.loop(dve, NE, per_e) as e:
                expert_round(e + 1)
            unused()
            n_over = dve.value_load(RI[0:1, 11:12], min_val=0, max_val=MAX_OVER)
            with dve.If(n_over > 0):
                with t.loop(dve, n_over, plus_ahead(per_e)) as x:
                    for r, h in MOE_BODY[:2]:
                        split(r, h)
                    expert_round(x + (NE + 1))
                    unused()

            dve.wait_ge(y_done, 1)
            for k in range(KD):
                ins = dve.tensor_scalar(DG[:, k, :], ident, MOD[:, 0, 88 + k:89 + k], float(D), ALU.mult, ALU.mult)
            ins.then_inc(dg_ready, 1)
            dve.wait_ge(lnr_in, 16)
            fs = sem("final_step")
            fn = [0]

            def fstep(ins):
                fn[0] += 1
                ins.then_inc(fs, 1)
                dve.wait_ge(fs, fn[0])

            for i in range(4):
                z = ZF[i]
                y1 = YG[i % 2][1]
                dve.wait_ge(z_part, i + 1)
                dve.scalar_tensor_tensor(out=z[:], in0=y1[:], scalar=GA[:, 1, i:i + 1], in1=z[:], op0=ALU.mult,
                                         op1=ALU.add).then_inc(yg_free, 1)
                dve.wait_ge(yg_free, i + 1)
                if i == 0:
                    dve.wait_ge(g2_ready, 1)
                fstep(dve.tensor_tensor(z[:], z[:], G2R[:], ALU.mult))
                fstep(dve.tensor_tensor(z[:], z[:], XR[:, i, :], ALU.add))
                for c in range(2):
                    ins = dve.bn_stats(BST[:, c, :], z[:, 512 * c:512 * c + 512])
                fstep(ins)
                fstep(dve.bn_aggr(BAG[:, 0:2], BST[:]))
                dve.tensor_scalar(BAG[:, 2:3], BAG[:, 1:2], EPS, None, ALU.add).then_inc(v_ready, 1)
                dve.wait_ge(sdf_ready, i + 1)
                fstep(dve.reciprocal(BAG[:, 3:4], BAG[:, 3:4]))
                dve.tensor_scalar(z[:], z[:], BAG[:, 0:1], BAG[:, 3:4], ALU.subtract, ALU.mult).then_inc(n_ready, 1)
                if i == 3:
                    dve.wait_ge(n_ready, 4)
                    fstep(dve.tensor_tensor(z[:], z[:], LNR[:, 0, :], ALU.mult))
                    dve.tensor_tensor(z[:], z[:], LNR[:, 1, :], ALU.add).then_inc(out_last, 1)
                else:
                    dve.wait_ge(n_ready, i + 1)

        @block.tensor
        def _(pe):
            t = Turns()

            def three(outp, wh, wl, ah, al, first, last):
                pe.matmul(outp, wh, ah, start=first, stop=False, skip_group_check=True)
                pe.matmul(outp, wh, al, start=False, stop=False, skip_group_check=True)
                return pe.matmul(outp, wl, ah, start=False, stop=last, skip_group_check=True)

            def ready(r, h):
                pe.wait_ge(hi_ready[h], t.n(("hs", h)))
                pe.wait_ge(raw_used[r], t.n(("raw", r)) + 1)

            def pair(p):
                pe.wait_ge(pair_free[p], t.n(("pair", p)))

            def unit_k(h, outs, ah=AH, al=AL, arrived=None):
                hi = HI[h][:].rearrange("p (k n) -> p k n", k=KD)
                lo = LO[h][:].rearrange("p (k n) -> p k n", k=KD)
                for c, k in walk(arrived):
                    if c == 0:
                        here(arrived, k)
                    ins = three(outs[c], hi[:, k, c * P:(c + 1) * P], lo[:, k, c * P:(c + 1) * P],
                                ah[:, k, :], al[:, k, :], k == 0, k == KD - 1)
                ins.then_inc(unit_done[h], 1)

            def walk(arrived):
                if arrived is None:
                    return [(c, k) for c in range(2) for k in range(KD)]
                return [(c, k) for k in range(KD) for c in range(2)]

            def here(arrived, k):
                if arrived is not None:
                    pe.wait_ge(al_ready, arrived + k + 1)

            pe.wait_ge(silc_ready, 1)
            for u in range(MOD_A):
                r = u % 4
                pe.wait_ge(raw_loaded[r], t.n(("raw", r)) * 16)
                for k in range(KD):
                    ins = pe.matmul(PS[0:2, u // 2, (u % 2) * 256:(u % 2 + 1) * 256], SILC[:, k, :], raw8(r)[:, k, :],
                                    start=(k == 0), stop=(k == KD - 1), skip_group_check=True)
                ins.then_inc(raw_used[r], 1)
            for half in range(2):
                pe.wait_ge(mrow_ready, half + 1)
                pe.wait_ge(mod_free, t.n("mod"))
                for c in range(KD):
                    ins = pe.transpose(PS[:, 7, 2 * c:2 * c + 2],
                                       MROW[0:2, half * 1024 + c * P:half * 1024 + (c + 1) * P], ident[0:2, 0:2])
                ins.then_inc(mod_full, 1)
            pe.wait_ge(cxl_ready, KD)

            def stats(stage):
                pe.wait_ge(stats_in, stage)
                pe.wait_ge(mod_free, t.n("mod"))
                pe.matmul(PS[:, 6, :], mean_w, ZS[:], start=True, stop=True)
                pe.matmul(PS[:, 7, :], mean_w, QS[:], start=True, stop=True).then_inc(stats_full, 1)

            fl_n = 0
            t.skip(("raw", 3), 1)

            def mod_batch(n):
                pe.wait_ge(mod_sums, (n + 1) * MOD_B)
                pe.wait_ge(mod_free, t.n("mod"))
                ms = MSA if n < 2 else MSB
                for c in range(2 * MOD_B):
                    ins = pe.matmul(PS[:, 7, c:c + 1], ms[:, c // 2, (c % 2) * P:(c % 2 + 1) * P], mean_w[:, 0:1],
                                    start=True, stop=True, skip_group_check=True)
                ins.then_inc(mod_full, 1)

            for name, count, units in SEGMENTS:
                ns = units
                pos = [(r, r, j) for j, r in enumerate(SLOT[units])]
                rper = {k: v for k, v in ring_per(units).items() if k[0] != "ud"}
                if name == "kv":
                    for r, h, j in pos:
                        ready(r, h)
                        hi = HI[h][:].rearrange("p (k n) -> p k n", k=KD)
                        lo = LO[h][:].rearrange("p (k n) -> p k n", k=KD)
                        if j == 0:
                            pair(0)
                            pair(1)
                            for c in range(2):
                                for k in range(KD):
                                    three(PS[:, 2, c * CTX:(c + 1) * CTX], hi[:, k, c * P:(c + 1) * P],
                                          lo[:, k, c * P:(c + 1) * P], CXH[:, k, :], CXL[:, k, :], k == 0, k == KD - 1)
                            unit_k(h, [PS[:, 0, :], PS[:, 1, :]], arrived=0)
                        else:
                            pair(2)
                            for m in range(6):
                                bank, col = 3 + m // 2, (m % 2) * 256
                                ah, al = (CXH, CXL) if m < 2 else (AH, AL)
                                o_ = (m % 2) * P if m < 2 else (m - 2) * P
                                for k in range(KD):
                                    ins = three(PS[:, bank, col:col + 256], ah[:, k, o_:o_ + P], al[:, k, o_:o_ + P],
                                                hi[:, k, :], lo[:, k, :], k == 0, k == KD - 1)
                            ins.then_inc(unit_done[h], 1)
                elif name == "q":
                    rper.update({("pair", 0): 1, ("pair", 1): 1})
                    with t.loop(pe, count, rper) as i:
                        for r, h, j in pos:
                            ready(r, h)
                            pair(j)
                            unit_k(h, [PS[:, 2 * j, :], PS[:, 2 * j + 1, :]])
                    mod_batch(0)
                    attention_pe(pe, three)
                elif name[:2] == "up":
                    rper.update({("pair", 0): ns // 2, ("pair", 1): ns // 2})
                    with t.loop(pe, count, rper) as i:
                        for r, h, j in pos:
                            ready(r, h)
                            pair(j % 2)
                            hi = HI[h][:].rearrange("p (g k n) -> p g k n", g=2, k=KD)
                            lo = LO[h][:].rearrange("p (g k n) -> p g k n", g=2, k=KD)
                            arrived = KD if (name, j) == ("up0", 0) else None
                            for c, k in walk(arrived):
                                if c == 0:
                                    here(arrived, k)
                                ins = three(PS[:, 2 * (j % 2) + c, :], hi[:, c, k, :], lo[:, c, k, :],
                                            AH[:, k, :], AL[:, k, :], k == 0, k == KD - 1)
                            ins.then_inc(unit_done[h], 1)
                    fl_n += count * ns
                elif name == "dn1":
                    pe.wait_ge(fl_ready, fl_n)
                    nk = FF_PARTS[1]
                    for r, h, j in pos:
                        ready(r, h)
                        hi = HI[h][:].rearrange("p (a n) -> p a n", n=P)
                        lo = LO[h][:].rearrange("p (a n) -> p a n", n=P)
                        for a in range(16):
                            d, k = divmod(16 * j + a, nk)
                            if k == 0 and d % 2 == 0:
                                pair((d // 2) % 2)
                            ins = three(PS[:, d % 4, :], hi[:, a, :], lo[:, a, :], FH[:, k, :], FL[:, k, :],
                                        k == 0, k == nk - 1)
                        ins.then_inc(unit_done[h], 1)
                elif name == "conv":
                    rper.update({("pair", 0): 1, ("pair", 1): 1, ("pair", 2): 1})
                    with t.loop(pe, count, rper) as i:
                        for r, h, j in pos:
                            ready(r, h)
                            pair(j)
                            unit_k(h, [PS[:, 2 * j, :], PS[:, 2 * j + 1, :]], arrived=2 * KD if j == 0 else None)
                    fl_n += 1
                else:
                    a_, l_ = (AH, AL) if name == "o" else (FH, FL)
                    if name == "o":
                        pe.wait_ge(ol_ready, 4 * NBLK)
                        mod_batch(1)
                    else:
                        mod_batch({"dn0": 2, "dn2": 3, "co": 4}[name])
                        pe.wait_ge(fl_ready, fl_n)
                    for r, h, j in pos:
                        ready(r, h)
                        pair(j % 2)
                        unit_k(h, [PS[:, 2 * (j % 2), :], PS[:, 2 * (j % 2) + 1, :]], a_, l_)
                if name in ("o", "dn2", "co"):
                    stats({"o": 1, "dn2": 2, "co": 3}[name])

            pair(0)
            for k in range(KD):
                pe.wait_ge(hf_ready, k + 1)
                for i, bank in enumerate((0, 1, 6, 7)):
                    ins = pe.matmul(PS[:, bank, 0:NE], HF[:, k, i * P:(i + 1) * P], wr[:, k, :],
                                    start=(k == 0), stop=(k == KD - 1), skip_group_check=True)
            ins.then_inc(lg_full, 1)

            def rows(i):
                if i >= 2:
                    pe.wait_ge(tr_free, i - 1)
                else:
                    pair(1 + i)
                src = HF if i < 4 else XZ
                for k in range(KD):
                    ins = pe.transpose(PS[:, 2 + 2 * (i % 2) + k // 4, (k % 4) * P:(k % 4 + 1) * P],
                                       src[:, k, (i % 4) * P:(i % 4 + 1) * P], ident)
                ins.then_inc(tr_full, 1)

            for i in range(4):
                rows(i)
            pe.wait_ge(rc_in, 16)
            pe.wait_ge(mask_ready, 1)
            pair(0)
            for i in range(4):
                for j in range(i + 1):
                    pe.matmul(PS[:, 0, 8 * i:8 * i + 8], ones if j < i else upper, MM[:, j, :], start=(j == 0),
                              stop=(j == i), skip_group_check=True)
            for j in range(4):
                ins = pe.matmul(PS[:, 0, 32:40], ones, MM[:, j, :], start=(j == 0), stop=(j == 3),
                                skip_group_check=True)
            ins.then_inc(pos_full, 1)
            pe.wait_ge(xz_ready, 3 * KD)
            for i in range(4, 8):
                rows(i)
            pe.wait_ge(routed, 1)

            per_g = {k: v for k, v in PER_EXP_RING.items() if k[0] != "ud"}
            per_g.update({"he": 2, "hl": 2})

            def turn_hidden(q, tiles):
                pe.wait_ge(he_ready, t.n("he"))
                for k in range(2):
                    for s in range(tiles):
                        ins = pe.transpose(PS[:, 2 * q, k * CAP + s * P:k * CAP + (s + 1) * P],
                                           HE[:, q, s * 256 + k * P:s * 256 + (k + 1) * P], ident)
                ins.then_inc(ht_full, 1)

            def expert_groups(tiles, r):
                with t.loop(pe, GROUPS, per_g):
                    for j, (rs_, h) in enumerate(MOE_BODY):
                        ready(rs_, h)
                        if j < 4:
                            hi = HI[h][:].rearrange("p (k n) -> p k n", k=KD)
                            lo = LO[h][:].rearrange("p (k n) -> p k n", k=KD)
                            for s in range(tiles):
                                cols_ = slice(s * P, (s + 1) * P)
                                for k in range(KD):
                                    if j == 0 and s == 0 and k % 2 == 0:
                                        pe.wait_ge(xtl_ready, r * 4 - (3 - k // 2))
                                    ins = three(PS[:, j, s * 256:(s + 1) * 256], XTH[:, k, cols_], XTL[:, k, cols_],
                                                hi[:, k, :], lo[:, k, :], k == 0, k == KD - 1)
                        else:
                            q = j - 4
                            pe.wait_ge(hl_ready, t.n("hl"))
                            if j == 4:
                                pe.wait_ge(y_zero, r)
                            hi = HI[h][:].rearrange("p (k n) -> p k n", k=2)
                            lo = LO[h][:].rearrange("p (k n) -> p k n", k=2)
                            for k in range(2):
                                if (j, k) == (4, 1):
                                    turn_hidden(1, tiles)
                                for s in range(tiles):
                                    cols_ = slice(s * P, (s + 1) * P)
                                    for b in range(2):
                                        ins = three(PS[:, 4 + 2 * s + b, :], HH[:, q, k, cols_], HL[:, q, k, cols_],
                                                    hi[:, k, b * 512:(b + 1) * 512], lo[:, k, b * 512:(b + 1) * 512],
                                                    False, True)
                        ins.then_inc(unit_done[h], 1)
                        if j == 2:
                            turn_hidden(0, tiles)

            def expert_round(r, count):
                pe.wait_ge(xg_in, r * 16)
                for k in range(KD):
                    for s in range(2):
                        ins = pe.transpose(PS[:, k // 2, (k % 2) * CAP + s * P:(k % 2) * CAP + (s + 1) * P],
                                           XG[:, s, k * P:(k + 1) * P], ident)
                    if k % 2:
                        ins.then_inc(xt_full, 1)
                if count is None:
                    expert_groups(2, r)
                else:
                    saved = dict(t.at)
                    with pe.If(count < P + 1):
                        expert_groups(1, r)
                    t.at = saved
                    with pe.If(count > P):
                        expert_groups(2, r)

            def unused():
                for r, h in MOE_BODY[:2]:
                    ready(r, h)
                    pe.sem_inc(unit_done[h], 1)

            per_e = times(per_g, GROUPS)
            with t.loop(pe, NE, per_e) as e:
                cnt = pe.value_load(RI[0:1, bass.ds(e, 1)], min_val=0, max_val=T)
                expert_round(e + 1, cnt)
            unused()
            n_over = pe.value_load(RI[0:1, 11:12], min_val=0, max_val=MAX_OVER)
            with pe.If(n_over > 0):
                with t.loop(pe, n_over, plus_ahead(per_e)) as x:
                    expert_round(x + (NE + 1), None)
                    unused()

            pe.wait_ge(dg_ready, 1)
            for k in range(KD):
                ins = pe.matmul(PS[:, k // 4, (k % 4) * P:(k % 4 + 1) * P], mean_w, DG[:, k, :], start=True, stop=True,
                                skip_group_check=True)
            ins.then_inc(g2_full, 1)



def kernel(**inputs):
    import numpy as np
    import concourse.bacc as _bacc
    from concourse.bass_utils import run_bass_kernel_spmd as _run

    f = np.float32
    a = {k: np.asarray(v) for k, v in inputs.items()}

    def cols(w):
        return w.reshape(KD, P, -1, 256).transpose(2, 1, 0, 3).reshape(-1, P, UNIT)

    order = [8 * kp + 4 * h + g for kp in range(2) for g in range(4) for h in range(2)]
    feat = np.concatenate([np.arange(h * HD, (h + 1) * HD) for h in order])
    mods = np.concatenate([cols(a["w_mod"][0]), cols(a["w_mod"][1])])
    wqkv = a["attn_w_qkv"][0]
    split = {
        "kv": cols(wqkv[:, D:]), "q": cols(wqkv[:, :D][:, feat]), "o": cols(a["attn_w_o"][0][feat]),
        "co": cols(a["conv_w_out"][0]),
        "conv": cols(a["conv_w_in"][0]).reshape(3, 4, P, UNIT)[[1, 2, 0]].transpose(1, 0, 2, 3).reshape(12, P, UNIT),
    }
    w1 = a["ffn_w1"][0].reshape(KD, P, FF // P, P).transpose(2, 1, 0, 3)
    w3 = a["ffn_w3"][0].reshape(KD, P, FF // P, P).transpose(2, 1, 0, 3)
    up = np.stack([w1, w3], axis=2).reshape(FF // P, P, UNIT)
    t0 = 0
    for i, n in enumerate(FF_PARTS):
        split[f"up{i}"] = up[t0:t0 + n]
        w2 = a["ffn_w2"][0][t0 * P:(t0 + n) * P]
        if n == KD:
            split[f"dn{i}"] = cols(w2)
        else:
            split[f"dn{i}"] = w2.reshape(n, P, KD, P).transpose(1, 2, 0, 3).reshape(P, -1, UNIT).transpose(1, 0, 2)
        t0 += n
    w_pre = np.empty((N_PRE, P, UNIT), f)
    u = 0
    for name, count, units in SEGMENTS:
        w_pre[u:u + count * units] = split[name]
        u += count * units
    w_all = np.zeros((NE * GROUPS * 6 + 2, P, UNIT), f)
    w_moe = w_all[:-2].reshape(NE, GROUPS, 6, P, UNIT)
    e1 = a["moe_w1"][0].reshape(NE, KD, P, GROUPS, 2, 256)
    e3 = a["moe_w3"][0].reshape(NE, KD, P, GROUPS, 2, 256)
    e2 = a["moe_w2"][0].reshape(NE, GROUPS, 2, 2, P, D)
    for q in range(2):
        w_moe[:, :, 2 * q] = e1[:, :, :, :, q].transpose(0, 3, 2, 1, 4).reshape(NE, GROUPS, P, UNIT)
        w_moe[:, :, 2 * q + 1] = e3[:, :, :, :, q].transpose(0, 3, 2, 1, 4).reshape(NE, GROUPS, P, UNIT)
        w_moe[:, :, 4 + q] = e2[:, :, q].transpose(0, 1, 3, 2, 4).reshape(NE, GROUPS, P, UNIT)

    small = np.zeros((P, N_SM), f)

    def put(name, v):
        lo, hi = SM[name]
        small[:, lo:hi] = v.reshape(P, hi - lo)

    put("cc", np.stack([a["c"][0].reshape(KD, P).T, a["c_ctx"].reshape(KD, P).T], axis=2))
    bm = a["b_mod"].reshape(96, P).T
    put("bmod", np.stack([bm, bm], axis=1))
    put("lng", a["ln_g"].reshape(4 * KD, P).T)
    put("lnb", a["ln_b"].reshape(4 * KD, P).T)
    put("ident", np.eye(P, dtype=f))
    put("mean", np.full((P, P), 1.0 / D, f))
    put("sink", np.broadcast_to(a["attn_sink"][0][order], (P, NH)))
    put("cw", a["conv_w"][0].reshape(3 * KD, P).T)
    put("wr", a["moe_router"][0].reshape(KD, P, NE).transpose(1, 0, 2))

    inv = (10000.0 ** (-np.arange(0, HD // 2, 2, dtype=f) / f(HD // 2))).astype(f)
    pos = np.arange(T)
    ar, ac = (pos // 64).astype(f)[:, None] * inv, (pos % 64).astype(f)[:, None] * inv
    ang = np.concatenate([ar, ar, ac, ac], axis=-1).T
    sign = np.where(np.arange(HD) % 32 < 16, -1.0, 1.0).astype(f)[:, None]
    rope = np.concatenate([np.tile(np.cos(ang), (2, 1)), np.tile(np.sin(ang) * sign, (2, 1))], axis=1).astype(f)
    qi, kj = np.arange(P)[:, None], np.arange(P)[None, :]
    mask = np.zeros((P, NBLK, 2, P), f)
    mask[:, :, 0][np.broadcast_to((kj < qi)[:, None], (P, NBLK, P))] = MASKED
    mask[:, :, 1][np.broadcast_to((kj > qi)[:, None], (P, NBLK, P))] = MASKED
    mask[:, 0, 0] = MASKED
    mask[:, NBLK - 1, 1] = MASKED
    rconst = np.zeros((P, N_RC), f)
    rconst[:, 0:P] = 1.0
    rconst[:, P:2 * P] = (qi < kj)
    rconst[:, 256:264] = np.arange(NE)
    rconst[:, 264:272] = np.arange(NE) * CAP
    lnrow = np.broadcast_to(np.concatenate([a["ln_g"][1, 1], a["ln_b"][1, 1]]), (P, 2 * D))

    arrays = {
        "small": small, "x_t": a["x"][0].T.reshape(KD, P, T).transpose(1, 0, 2),
        "ctx_t": a["ctx"][0].T.reshape(KD, P, CTX).transpose(1, 0, 2), "rope": rope,
        "mask": mask.reshape(P, NBLK, 2 * P), "rconst": rconst, "lnrow": lnrow, "w_mod": mods, "w_pre": w_pre, "w_moe": w_all,
    }
    arrays = {k: np.ascontiguousarray(v) for k, v in arrays.items()}
    nc = _bacc.Bacc("TRN2", target_bir_lowering=False, num_devices=1)
    args = [nc.dram_tensor(k, v.shape, F32, kind="ExternalInput").ap() for k, v in arrays.items()]
    args.append(nc.dram_tensor("out", (1, T, D), F32, kind="ExternalOutput").ap())
    program(nc, *args)
    r = _run(nc, [arrays], core_ids=[0])
    return r.results[0]["out"]
```
